# Optimizing a Trainium2 kernel written in Bass

```python
import math
import jax, jax.numpy as jnp
from jax import lax
import numpy as np

D_MODEL = 1024
BATCH = 1
SEQ = 512
DEPTH = 1

CHUNK = 64
MEM_LEN = 256
EPS = 1e-6
S5_WIDTH = D_MODEL // 2
S5_GROUP_DIM = 16
S5_GROUPS = S5_WIDTH // S5_GROUP_DIM
S5_STATE = 64
SGU_WIDTH = D_MODEL // 2
SGU_GROUPS = 4
SGU_GROUP_DIM = SGU_WIDTH // SGU_GROUPS
SGU_BLOCK = 2 * CHUNK
XA_HEADS = 4
XA_HEAD_DIM = 128
XA_WIDTH = XA_HEADS * XA_HEAD_DIM
N_BRANCHES = 3
D_FF = -(-8 * D_MODEL // (3 * 256)) * 256
SPLITS = (S5_WIDTH, S5_WIDTH + SGU_WIDTH, S5_WIDTH + 2 * SGU_WIDTH,
          S5_WIDTH + 2 * SGU_WIDTH + XA_WIDTH)
IN_WIDTH = S5_WIDTH + 2 * SGU_WIDTH + XA_WIDTH + N_BRANCHES * D_MODEL

kernel_name = "hybrid_s5_gmlp_memxattn_block"

def _rms(x, g):
    xf = x.astype(jnp.float32)
    y = xf * lax.rsqrt(jnp.mean(xf * xf, axis=-1, keepdims=True) + EPS)
    return (y * g.astype(jnp.float32)).astype(x.dtype)

def _layernorm(x, g, b):
    xf = x.astype(jnp.float32)
    mu = jnp.mean(xf, axis=-1, keepdims=True)
    var = jnp.mean(jnp.square(xf - mu), axis=-1, keepdims=True)
    y = (xf - mu) * lax.rsqrt(var + EPS)
    return (y * g.astype(jnp.float32) + b.astype(jnp.float32)).astype(x.dtype)

def _s5_combine(e1, e2):
    a1r, a1i, b1r, b1i = e1
    a2r, a2i, b2r, b2i = e2
    ar = a1r * a2r - a1i * a2i
    ai = a1r * a2i + a1i * a2r
    br = a2r * b1r - a2i * b1i + b2r
    bi = a2r * b1i + a2i * b1r + b2i
    return ar, ai, br, bi

def _s5(u, a_re, a_im, log_dt, bm_re, bm_im, cm_re, cm_im, d_skip):
    bsz, seq, _ = u.shape
    uf = u.astype(jnp.float32)
    ug = uf.reshape(bsz, seq, S5_GROUPS, S5_GROUP_DIM)
    ar = a_re.astype(jnp.float32)
    ai = a_im.astype(jnp.float32)
    dt = jnp.exp(log_dt.astype(jnp.float32))[:, None]
    mag = jnp.exp(ar * dt)
    ab_re = mag * jnp.cos(ai * dt)
    ab_im = mag * jnp.sin(ai * dt)
    nr = ab_re - 1.0
    den = ar * ar + ai * ai
    f_re = (nr * ar + ab_im * ai) / den
    f_im = (ab_im * ar - nr * ai) / den
    br = bm_re.astype(jnp.float32)
    bi = bm_im.astype(jnp.float32)
    bb_re = f_re[..., None] * br - f_im[..., None] * bi
    bb_im = f_re[..., None] * bi + f_im[..., None] * br
    bu_re = jnp.einsum('blgh,gph->blgp', ug, bb_re)
    bu_im = jnp.einsum('blgh,gph->blgp', ug, bb_im)
    a_re_seq = jnp.broadcast_to(ab_re, (1, seq, S5_GROUPS, S5_STATE))
    a_im_seq = jnp.broadcast_to(ab_im, (1, seq, S5_GROUPS, S5_STATE))
    _, _, s_re, s_im = lax.associative_scan(
        _s5_combine, (a_re_seq, a_im_seq, bu_re, bu_im), axis=1)
    y = (jnp.einsum('blgp,ghp->blgh', s_re, cm_re.astype(jnp.float32))
         - jnp.einsum('blgp,ghp->blgh', s_im, cm_im.astype(jnp.float32)))
    y = y.reshape(bsz, seq, S5_WIDTH) + d_skip.astype(jnp.float32) * uf
    return y.astype(u.dtype)

def _sgu(zu, zv, g_sgu, beta_sgu, w_s, b_s):
    bsz, seq, _ = zu.shape
    u = jax.nn.gelu(zu)
    v = _layernorm(jax.nn.gelu(zv), g_sgu, beta_sgu)
    v = v.reshape(bsz, seq // SGU_BLOCK, SGU_BLOCK, SGU_GROUPS, SGU_GROUP_DIM)
    mask = jnp.tril(jnp.ones((SGU_BLOCK, SGU_BLOCK), dtype=w_s.dtype))
    w = w_s * mask[None]
    sv = jnp.einsum('gts,bcsgd->bctgd', w, v) + b_s.T[None, None, :, :, None]
    return u * sv.reshape(bsz, seq, SGU_WIDTH)

def _mem_xattn(zq, mem, g_mem, w_kv):
    bsz, seq, _ = zq.shape
    q = zq.reshape(bsz, seq, XA_HEADS, XA_HEAD_DIM)
    kv = _rms(mem, g_mem) @ w_kv
    k, v = jnp.split(kv, 2, axis=-1)
    k = k.reshape(bsz, MEM_LEN, XA_HEADS, XA_HEAD_DIM)
    v = v.reshape(bsz, MEM_LEN, XA_HEADS, XA_HEAD_DIM)
    s = jnp.einsum('blhd,bmhd->bhlm', q, k).astype(jnp.float32) * (XA_HEAD_DIM ** -0.5)
    p = jax.nn.softmax(s, axis=-1).astype(v.dtype)
    o = jnp.einsum('bhlm,bmhd->blhd', p, v)
    return o.reshape(bsz, seq, XA_WIDTH)

def setup_inputs(seed: int = 0) -> dict:
    key = jax.random.key(seed)
    ks = jax.random.split(key, 32)

    def nrm(k, shape, scale):
        return jax.random.normal(k, shape, jnp.float32) * scale

    def gain(k, shape):
        return 1.0 + 0.05 * jax.random.normal(k, shape, jnp.float32)

    L = DEPTH
    G, P, H = S5_GROUPS, S5_STATE, S5_GROUP_DIM
    a_re = -0.5 * jnp.exp(0.1 * jax.random.normal(ks[5], (L, G, P), jnp.float32))
    a_im = (math.pi * jnp.arange(P, dtype=jnp.float32))[None, None, :] + \
        0.1 * jax.random.normal(ks[6], (L, G, P), jnp.float32)
    log_dt = jax.random.uniform(ks[7], (L, G), jnp.float32,
                                minval=math.log(1e-3), maxval=math.log(1e-1))
    return {
        "x": jax.random.normal(ks[0], (BATCH, SEQ, D_MODEL), jnp.float32),
        "mem": jax.random.normal(ks[1], (BATCH, MEM_LEN, D_MODEL), jnp.float32),
        "g_mix": gain(ks[2], (L, D_MODEL)),
        "w_in": nrm(ks[3], (L, D_MODEL, IN_WIDTH), D_MODEL ** -0.5),
        "b_gate": nrm(ks[4], (L, N_BRANCHES * D_MODEL), 0.02),
        "a_re": a_re,
        "a_im": a_im,
        "log_dt": log_dt,
        "bm_re": nrm(ks[8], (L, G, P, H), (2 * H) ** -0.5),
        "bm_im": nrm(ks[9], (L, G, P, H), (2 * H) ** -0.5),
        "cm_re": nrm(ks[10], (L, G, H, P), (2 * P) ** -0.5),
        "cm_im": nrm(ks[11], (L, G, H, P), (2 * P) ** -0.5),
        "d_skip": nrm(ks[12], (L, S5_WIDTH), 1.0),
        "w_glu": nrm(ks[13], (L, S5_WIDTH, S5_WIDTH), S5_WIDTH ** -0.5),
        "b_glu": nrm(ks[14], (L, S5_WIDTH), 0.02),
        "g_sgu": gain(ks[15], (L, SGU_WIDTH)),
        "beta_sgu": nrm(ks[16], (L, SGU_WIDTH), 0.02),
        "w_s": nrm(ks[17], (L, SGU_GROUPS, SGU_BLOCK, SGU_BLOCK), SGU_BLOCK ** -0.5),
        "b_s": gain(ks[18], (L, SGU_GROUPS, SGU_BLOCK)),
        "g_mem": gain(ks[19], (L, D_MODEL)),
        "w_kv": nrm(ks[20], (L, D_MODEL, 2 * XA_WIDTH), D_MODEL ** -0.5),
        "w_a_out": nrm(ks[21], (L, S5_WIDTH, D_MODEL), S5_WIDTH ** -0.5),
        "w_b_out": nrm(ks[22], (L, SGU_WIDTH, D_MODEL), SGU_WIDTH ** -0.5),
        "w_c_out": nrm(ks[23], (L, XA_WIDTH, D_MODEL), XA_WIDTH ** -0.5),
        "w_out": nrm(ks[24], (L, D_MODEL, D_MODEL), D_MODEL ** -0.5),
        "g_ffn": gain(ks[25], (L, D_MODEL)),
        "w_gate": nrm(ks[26], (L, D_MODEL, D_FF), D_MODEL ** -0.5),
        "w_up": nrm(ks[27], (L, D_MODEL, D_FF), D_MODEL ** -0.5),
        "w_down": nrm(ks[28], (L, D_FF, D_MODEL), D_FF ** -0.5),
        "g_final": gain(ks[29], (D_MODEL,)),
    }

def reference(x, mem, g_mix, w_in, b_gate, a_re, a_im, log_dt, bm_re, bm_im, cm_re, cm_im,
              d_skip, w_glu, b_glu, g_sgu, beta_sgu, w_s, b_s, g_mem, w_kv,
              w_a_out, w_b_out, w_c_out, w_out, g_ffn, w_gate, w_up, w_down, g_final):
    bsz, seq, _ = x.shape
    for l in range(DEPTH):
        h = _rms(x, g_mix[l])
        z = h @ w_in[l]
        za, zu, zv, zq, zg = jnp.split(z, SPLITS, axis=-1)
        ya = jax.nn.gelu(_s5(za, a_re[l], a_im[l], log_dt[l], bm_re[l], bm_im[l],
                             cm_re[l], cm_im[l], d_skip[l]))
        ya = (ya * jax.nn.sigmoid(ya @ w_glu[l] + b_glu[l])) @ w_a_out[l]
        yb = _sgu(zu, zv, g_sgu[l], beta_sgu[l], w_s[l], b_s[l]) @ w_b_out[l]
        yc = _mem_xattn(zq, mem, g_mem[l], w_kv[l]) @ w_c_out[l]
        gates = jax.nn.sigmoid(zg + b_gate[l]).reshape(bsz, seq, N_BRANCHES, D_MODEL)
        merged = gates[:, :, 0] * ya + gates[:, :, 1] * yb + gates[:, :, 2] * yc
        x = x + merged @ w_out[l]
        hf = _rms(x, g_ffn[l])
        x = x + (jax.nn.silu(hf @ w_gate[l]) * (hf @ w_up[l])) @ w_down[l]
    return _rms(x, g_final)


_drawn_inputs = setup_inputs


def setup_inputs(seed=0):
    import zlib

    import numpy as np

    out = dict(_drawn_inputs(seed))
    spreads = {}
    factors = {'b_gate': 8.0,
     'a_re': 64.0,
     'a_im': 40.016,
     'log_dt': 41.208,
     'bm_re': 55.928,
     'bm_im': 57.84,
     'cm_re': 56.816,
     'cm_im': 56.848,
     'b_glu': 64.0,
     'g_sgu': 17.824,
     'beta_sgu': 43.817,
     'b_s': 13.293,
     'g_mem': 8.0,
     'w_glu': 4.121,
     'g_ffn': 5.179}
    for name, (base, spread) in spreads.items():
        noise = np.random.default_rng([zlib.crc32(name.encode()), seed]).standard_normal(out[name].shape)
        drawn = base * np.exp(spread * noise) if base else spread * noise
        out[name] = __import__('jax').numpy.asarray(drawn.astype(out[name].dtype))
    for name, factor in factors.items():
        out[name] = (out[name] * factor).astype(out[name].dtype)
    return out
```

```python
from contextlib import ExitStack

import concourse.bass as bass
import numpy as np
from concourse import mybir

P = 128
D = 1024
T = 512
M = 256
KD = D // P
WB = 512
KB = WB // P
FF = 2816
KF = FF // P
HEADS = 4
EPS = 1e-6
SCALE = 128.0 ** -0.5
TILE = 1024

BLOCKS = 16
ROUND = 4
ROUNDS = BLOCKS // ROUND
L = 4
NC = T // L
CH = 32

T_ZA, T_ZU, T_ZV, T_ZQ, T_K, T_V = 0, 4, 8, 12, 16, 20
T_J1 = 24
T_GLU = T_J1 + 6 * 4
T_J2 = T_GLU + 2
T_WO = T_J2 + 3 * 4
T_FF = T_WO + KD
T_DN = T_FF + 4 * (KF // 2)
TILES = T_DN + KF
RAW = 2
NS = 2

C_ARE, C_AIM, C_LDT = 0, 16, 32
C_BRE, C_BIM = 48, 48 + 256
C_CRE, C_CIM = C_BIM + 256, C_BIM + 512
C_D = C_CIM + 256
C_GMIX = C_D + 16
C_GMEM, C_GFFN, C_GFIN = C_GMIX + 8, C_GMIX + 16, C_GMIX + 24
C_BGATE = C_GFIN + 8
C_BGLU = C_BGATE + 24
C_ID = C_BGLU + 4
N_SMALL = C_ID + P

TWO_PI = 2 * np.pi
ROUNDER = 12582912.0
PI_HI = 6.28125
PI_MID = float(np.float32(round((TWO_PI - PI_HI) * 2 ** 20) / 2 ** 20))
PI_LO = float(np.float32(TWO_PI - PI_HI - PI_MID))
HALF_PI = float(np.float32(np.pi / 2))
SIN_MAX = 3.1415925


def build(nc, xt_d, mem_d, small_d, sgu_d, w_d, out_d):
    F = mybir.dt.float32
    R = mybir.dt.float32r
    ACT = mybir.ActivationFunctionType
    ALU = mybir.AluOpType
    AX = mybir.AxisListType.X
    ds = bass.ds

    with ExitStack() as ctx:
        def sem(name):
            return ctx.enter_context(nc.semaphore(name))

        base = (nc.sbuf_base + 63) // 64 * 64

        def at(name, off, shape, dt=F):
            return nc.alloc_sbuf_tensor_at(name, shape, dt, offset=off)

        o_raw = base
        o_hi = o_raw + RAW * 4096
        o_lo = o_hi + NS * 4096
        o_x = o_lo + NS * 4096
        o_h = o_x + 16384
        o_a = o_h + 32768
        o_b = o_a + 16384
        o_c = o_b + 32768
        o_u = o_c + 32768
        o_e = o_u + 8192
        o_f = o_e + 16384
        o_g = o_f + 8192
        o_s = o_g + 6144
        o_d = o_s + (N_SMALL * 4 + 63) // 64 * 64

        raw = at("raw", o_raw, [P, RAW, TILE])
        w_hi = at("w_hi", o_hi, [P, NS, TILE], R)
        w_lo = at("w_lo", o_lo, [P, NS, TILE], R)
        xT = at("xT", o_x, [P, KD, T])
        h_hi = at("h_hi", o_h, [P, KD, T], R)
        h_lo = at("h_lo", o_h + 16384, [P, KD, T], R)
        memf = at("memf", o_a, [P, KD, M])
        qT = at("qT", o_a, [P, HEADS, T])
        kT = at("kT", o_a + 8192, [P, HEADS, M])
        vM = at("vM", o_a + 12288, [P, 2, WB])
        mgf = at("mgf", o_a, [P, KD, T])
        vtok = at("vtok", o_b, [P, 4, WB])
        ug = at("ug", o_b + 8192, [P, KB, T])
        sgu = at("sgu", o_b + 16384, [P, 4, WB])
        prob = at("prob", o_b + 24576, [P, 8, M])
        bb_tmp = at("bb_tmp", o_b + 24576, [P, 4, BLOCKS, 16])
        ba = [at(f"ba{i}", o_b + 2048 * i, [P, ROUND, L, CH]) for i in range(2)]
        gt = [at(f"gt{i}", o_b + 4096 + 2048 * i, [P, ROUND, P]) for i in range(2)]
        ca = [at(f"ca{i}", o_b + 8192 + 4096 * i, [P, ROUND, L + 1, CH]) for i in range(2)]
        toep = at("toep", o_b + 16384, [P, ROUND, P])
        uc = at("uc", o_b + 18432, [P, ROUND, NC])
        rot = [at(f"rot{i}", o_b + 20480 + 2048 * i, [P, ROUND, NC]) for i in range(4)]
        st = [at(f"st{i}", o_b + 28672 + 2048 * i, [P, ROUND, NC]) for i in range(2)]
        ya_hi = at("ya_hi", o_b, [P, KB, T], R)
        ya_lo = at("ya_lo", o_b + 8192, [P, KB, T], R)
        y2f = at("y2f", o_b + 16384, [P, 2, T])
        mg_hi = at("mg_hi", o_b, [P, KD, T], R)
        mg_lo = at("mg_lo", o_b + 16384, [P, KD, T], R)
        m_hi = at("m_hi", o_c, [P, KD, M], R)
        m_lo = at("m_lo", o_c + 8192, [P, KD, M], R)
        yb_hi = at("yb_hi", o_c, [P, KB, T], R)
        yb_lo = at("yb_lo", o_c + 8192, [P, KB, T], R)
        y2_hi = at("y2_hi", o_c, [P, KB, T], R)
        y2_lo = at("y2_lo", o_c + 8192, [P, KB, T], R)
        tab_tmp = at("tab_tmp", o_c + 16384, [P, 4, BLOCKS, NC // 2])
        o_hiT = at("o_hiT", o_c + 16384, [P, HEADS, T], R)
        o_loT = at("o_loT", o_c + 24576, [P, HEADS, T], R)
        uT = at("uT", o_u, [P, KB, T])
        act_hi = at("act_hi", o_a, [P, KF, T], R)
        act_lo = at("act_lo", o_a + KF * T * 4, [P, KF, T], R)
        assert o_a + 2 * KF * T * 4 == o_e
        cosT = at("cosT", o_e, [P, BLOCKS, NC])
        sinT = at("sinT", o_e + 8192, [P, BLOCKS, NC])
        silu = at("silu", o_e, [P, 2, T])
        actf = at("actf", o_e + 4096, [P, 2, T])
        rstd = at("rstd", o_e + 8192, [P, T])
        std = at("std", o_e + 10240, [P, T])
        hn = at("hn", o_f, [P, 2, T])
        outf = at("outf", o_f + 4096, [P, 2, T])
        pT = at("pT", o_f, [P, 2, 2, T])
        yaf = at("yaf", o_f, [P, KB, T])
        mf = at("mf", o_f, [P, 2, T])
        sq = at("sq", o_g, [P, 2, T])
        sqsum = at("sqsum", o_g + 4096, [P, T])
        th = at("th", o_g, [P, 2, T])
        prod = at("prod", o_g + 4096, [P, T])
        small = at("small", o_s, [P, N_SMALL])
        s5p = at("s5p", o_d, [P, 20, BLOCKS])
        ones = at("ones", o_d + 1280, [P, P])
        eps = at("eps", o_d + 1792, [P, 1])
        hbias = at("hbias", o_d + 1824, [P, 28])
        stats = at("stats", o_d + 1952, [P, 4, 6])
        mv = at("mv", o_d + 2048, [P, 4, 2])
        vrs = at("vrs", o_d + 2080, [P, 4])
        smx = at("smx", o_d + 2112, [P, 16])
        ssum = at("ssum", o_d + 2176, [P, 16])
        srec = at("srec", o_d + 2240, [P, 16])
        vstd = at("vstd", o_d + 2304, [P, 4])
        snm = at("snm", o_d + 2336, [P, 16])
        assert o_d + 2400 <= nc.sbuf_usable_end, o_d + 2400 - nc.sbuf_usable_end

        bank = [ctx.enter_context(nc.psum_tensor(f"bank{i}", [P, T], F)) for i in range(8)]
        ident = small[:, C_ID:C_ID + P]

        def fv(t):
            return t.bitcast(F)

        def flat(ap):
            return ap.rearrange("p a b -> p (a b)")

        raw_loaded = [sem(f"raw_loaded{i}") for i in range(RAW)]
        w_rounded = sem("w_rounded")
        w_ready = sem("w_ready")
        w_used = sem("w_used")
        x_loaded = [sem(f"x_loaded{i}") for i in range(4)]
        mem_loaded, small_loaded, sgu_loaded = sem("mem_loaded"), sem("small_loaded"), sem("sgu_loaded")
        consts = sem("consts")
        wst_masked = sem("wst_masked")
        dve_step = sem("dve_step")
        norms = {}
        for n in ("x", "m", "f", "o"):
            norms[n] = {k: sem(f"{n}_{k}") for k in ("sq", "sum", "ssq", "std", "hn", "hi", "lo")}
        za_taken, zu_taken, zv_taken = sem("za_taken"), sem("zu_taken"), sem("zv_taken")
        zq_taken, k_taken, v_taken = sem("zq_taken"), sem("k_taken"), sem("v_taken")
        var_ready, vstd_ready, vln_ready = sem("var_ready"), sem("vstd_ready"), sem("vln_ready")
        sgu_done, sgu_taken, yb_f, yb_hi_s, yb_lo_s = (sem("sgu_done"), sem("sgu_taken"), sem("yb_f"),
                                                       sem("yb_hi_s"), sem("yb_lo_s"))
        sc_done, mx_ready, exp_done, p_ready = (sem("sc_done"), sem("mx_ready"), sem("exp_done"),
                                                sem("p_ready"))
        pt_done, pt_act, pt_dve = sem("pt_done"), sem("pt_act"), sem("pt_dve")
        pv_done, o_hi_s, o_lo_s = sem("pv_done"), sem("o_hi_s"), sem("o_lo_s")
        dt_ready, ang_ready, trig_ready, s5_const = (sem("dt_ready"), sem("ang_ready"),
                                                     sem("trig_ready"), sem("s5_const"))
        j1_th, j1_merge = sem("j1_th"), sem("j1_merge")
        uc_ready, bc_ready, gt_done, gt_ready = (sem("uc_ready"), sem("bc_ready"), sem("gt_done"),
                                                 sem("gt_ready"))
        vin_done, st_ready, y_done, y_taken = (sem("vin_done"), sem("st_ready"), sem("y_done"),
                                               sem("y_taken"))
        glu_th, y2_f, y2_hi_s, y2_lo_s = sem("glu_th"), sem("y2_f"), sem("y2_hi_s"), sem("y2_lo_s")
        ya_hi_s, ya_lo_s = sem("ya_hi_s"), sem("ya_lo_s")
        j2_th, j2_prod, j2_m, j2_hi, j2_lo = (sem("j2_th"), sem("j2_prod"), sem("j2_m"), sem("j2_hi"),
                                              sem("j2_lo"))
        x1_ready = sem("x1_ready")
        ff_silu, ff_act, ff_hi, ff_lo = sem("ff_silu"), sem("ff_act"), sem("ff_hi"), sem("ff_lo")
        dn_done, x2_ready = sem("dn_done"), sem("x2_ready")
        out_ready, out_stored = sem("out_ready"), sem("out_stored")

        def before(eng, *sems):
            for x in sems:
                eng.drain().then_inc(x, 1)

        class Steps:

            def __init__(self, eng, s):
                self.eng, self.s, self.base, self.n = eng, s, 0, 0

            def go(self, ins):
                ins.then_inc(self.s, 1)
                self.n += 1

            def wait(self):
                self.eng.wait_ge(self.s, self.base + self.n)

            def link(self, ins):
                self.go(ins)
                self.wait()

            def enter(self, i, per):
                self.outer, self.per = self.base + self.n, per
                self.base, self.n = self.base + self.n + i * per, 0

            def leave(self, count):
                assert self.n == self.per, self.n
                self.base, self.n = self.outer + count * self.per, 0

        block = ctx.enter_context(nc.Block())

        @block.sync
        def _(sp):
            for i in range(4):
                sp.dma_start(xT[:, 2 * i:2 * i + 2, :], xt_d[:, 2 * i:2 * i + 2, :]).then_inc(x_loaded[i], 16)
            for s in range(RAW):
                sp.dma_start(raw[:, s, :], w_d[s, :, :]).then_inc(raw_loaded[s], 16)
            with nc.sync.Fori(1, TILES // RAW) as i:
                for s in range(RAW):
                    sp.wait_ge(w_ready, i * RAW + (s + 1 - RAW))
                    sp.dma_start(raw[:, s, :], w_d[ds(i * RAW + s, 1), :, :].rearrange("a p n -> p (a n)")
                                 ).then_inc(raw_loaded[s], 16)
            for n in range(KD):
                sp.wait_ge(out_ready, n + 1)
                sp.dma_start(out_d[n, :, :], xT[:, n, :]).then_inc(out_stored, 16)
            sp.wait_ge(out_stored, 16 * KD)

        @block.gpsimd
        def _(pool):
            nc.gpsimd.memset(ones[:, :], 1.0)
            nc.gpsimd.memset(eps[:, :], EPS).then_inc(consts, 1)

            pool.wait_ge(sgu_loaded, 16)
            wst = sgu[:, 3, :].rearrange("p (g t) -> p g t", g=4)
            nc.gpsimd.affine_select(out=wst, in_=wst, pattern=[[0, 4], [1, P]], compare_op=ALU.is_ge,
                                    fill=0.0, base=0, channel_multiplier=-1).then_inc(wst_masked, 1)
            with nc.gpsimd.Fori(0, TILES // NS) as i:
                for s in range(NS):
                    pool.wait_ge(w_rounded, i * NS + (s + 1))
                    nc.gpsimd.tensor_tensor(w_lo[:, s, :], raw[:, s, :], fv(w_hi[:, s, :]),
                                            ALU.subtract).then_inc(w_ready, 1)

        @block.scalar
        def _(act):
            act.dma_start(small[:, :], small_d).then_inc(small_loaded, 16)
            act.dma_start(memf[:, :, :], mem_d).then_inc(mem_loaded, 16)
            act.dma_start(sgu[:, :, :], sgu_d).then_inc(sgu_loaded, 16)

            def round_weights(t, m=0, per=0):
                slot = t % NS
                act.wait_ge(raw_loaded[slot], 16 * (per // 2) * m + 16 * (t // 2 + 1))
                if t >= NS:
                    act.wait_ge(w_used, per * m + (t + 1 - NS))
                nc.scalar.activation(w_hi[:, slot, :], raw[:, slot, :], ACT.Copy).then_inc(w_rounded, 1)

            def square(s, src, k, width):
                if k >= 2:
                    act.wait_ge(s["sum"], k - 1)
                nc.scalar.activation(sq[:, k % 2, 0:width], src, ACT.Square).then_inc(s["sq"], 1)

            def root(s, b, width):
                act.wait_ge(s["ssq"], 1)
                nc.scalar.activation(std[:, 0:width], bank[b][:, 0:width], ACT.Sqrt, bias=eps[:, 0:1],
                                     scale=1.0 / D).then_inc(s["std"], 1)

            def round_tile(s, dst, k, width):
                act.wait_ge(s["hn"], k + 1)
                nc.scalar.activation(dst, hn[:, k % 2, 0:width], ACT.Copy).then_inc(s["hi"], 1)

            act.wait_ge(consts, 1)
            for k in range(KD):
                if k % 2 == 0:
                    act.wait_ge(x_loaded[k // 2], 16)
                square(norms["x"], xT[:, k, :], k, T)
            round_weights(0)
            round_weights(1)
            root(norms["x"], 7, T)
            for k in range(KD):
                round_tile(norms["x"], h_hi[:, k, :], k, T)
            act.wait_ge(mem_loaded, 16)
            act.wait_ge(norms["x"]["sum"], KD)
            for k in range(KD):
                square(norms["m"], memf[:, k, :], k, M)
            for c in range(KB):
                act.wait_ge(w_used, T_ZA + c + 1)
                nc.scalar.activation(uT[:, c, :], bank[c][:, :], ACT.Copy).then_inc(za_taken, 1)
                round_weights(T_ZA + c + 2)
            act.wait_ge(norms["x"]["lo"], KD)
            root(norms["m"], 6, M)
            act.wait_ge(small_loaded, 16)
            nc.scalar.activation(s5p[:, 0, :], small[:, C_LDT:C_LDT + 16], ACT.Exp).then_inc(dt_ready, 1)
            for c in range(KB):
                act.wait_ge(w_used, T_ZU + c + 1)
                nc.scalar.activation(ug[:, c, :], bank[4 + c][:, :], ACT.Gelu_apprx_tanh).then_inc(zu_taken, 1)
                round_weights(T_ZU + c + 2)
                if c == 0:
                    for k in range(KD):
                        round_tile(norms["m"], m_hi[:, k, :], k, M)
                if c == 2:
                    act.wait_ge(ang_ready, 1)
                    nc.scalar.activation(s5p[:, 1, :], s5p[:, 4, :], ACT.Exp)
                    nc.scalar.activation(s5p[:, 2, :], s5p[:, 6, :], ACT.Sin)
                    nc.scalar.activation(s5p[:, 3, :], s5p[:, 5, :], ACT.Sin).then_inc(trig_ready, 1)
            for t in range(T_ZV + 2, T_ZQ + 2):
                round_weights(t)
            for c in range(4):
                act.wait_ge(w_used, T_ZV + 4)
                nc.scalar.activation(vtok[:, c, :], bank[c][:, :], ACT.Gelu_apprx_tanh).then_inc(zv_taken, 1)
            round_weights(T_ZQ + 2)
            act.wait_ge(var_ready, 4)
            nc.scalar.activation(vstd[:, :], mv[:, :, 1], ACT.Sqrt, bias=eps[:, 0:1]).then_inc(vstd_ready, 1)
            for t in range(T_ZQ + 3, T_V + 2):
                round_weights(t)

            def softmax_exp(h):
                for tt in range(4):
                    act.wait_ge(mx_ready, 2 * h + tt // 2 + 1)
                    if h >= 2:
                        act.wait_ge(pt_done, h - 1)
                    i = 4 * h + tt
                    nc.scalar.activation(prob[:, i % 8, :], score(h, tt), ACT.Exp, bias=snm[:, i:i + 1],
                                         scale=SCALE, accum_out=ssum[:, i:i + 1]).then_inc(exp_done, 1)

            def score(h, tt):
                b = (4, 6, 6, 2)[h] + tt // 2
                return bank[b][:, (tt % 2) * M:(tt % 2 + 1) * M]

            def take_pt(h):
                act.wait_ge(pt_done, h + 1)
                if h >= 2:
                    act.wait_ge(pv_done, h - 1)
                nc.scalar.activation(pT[:, h % 2, 0, :], bank[(4, 4, 4, 6)[h]][:, :], ACT.Copy).then_inc(pt_act, 1)

            def round_o(h):
                act.wait_ge(pv_done, h + 1)
                return nc.scalar.activation(o_hiT[:, h, :], bank[h % 2][:, :], ACT.Copy)

            softmax_exp(0)
            round_weights(T_V + 2)
            softmax_exp(1)
            for t in range(T_V + 3, T_J1 + 2):
                round_weights(t)
            for g in range(4):
                act.wait_ge(yb_f, g + 1)
                nc.scalar.activation(yb_hi[:, g, :], ug[:, g, :], ACT.Copy).then_inc(yb_hi_s, 1)
            take_pt(0)
            softmax_exp(2)
            take_pt(1)
            softmax_exp(3)
            round_o(0).then_inc(o_hi_s, 1)
            round_o(1).then_inc(o_hi_s, 1)
            take_pt(2)
            take_pt(3)
            round_o(2).then_inc(o_hi_s, 1)
            round_o(3).then_inc(o_hi_s, 1)
            act.wait_ge(s5_const, 1)
            nc.scalar.mul(hbias[:, :], small[:, C_BGATE:C_BGATE + 28], 0.5)
            def gate_tanh(buf, b, bias):
                return nc.scalar.activation(th[:, buf, :], bank[b][:, :], ACT.Tanh, bias=bias, scale=0.5)

            act.wait_ge(za_taken, KB)
            act.wait_ge(o_lo_s, HEADS)
            before(act, j1_th, y_taken)
            act.wait_ge(j1_th, 1)
            with nc.scalar.Fori(0, ROUNDS) as m:
                for n in range(2):
                    act.wait_ge(w_used, 6 * m + (T_J1 + n + 1))
                    act.wait_ge(j1_merge, 4 * m + 1)
                    gate_tanh(n, n, hbias[:, ds(2 * m + (8 + n), 1)]).then_inc(j1_th, 1)
                    round_weights(T_J1 + 2 + n, m, 6)
                act.wait_ge(y_taken, m + 1)
                for q in range(ROUND):
                    for j in range(L):
                        src = uT[32 * q:32 * q + 32, ds(m, 1), :].rearrange("p a (c j) -> p (a c) j", j=L)
                        ins = nc.scalar.activation(uc[32 * j:32 * j + 32, q, :], src[:, :, j], ACT.Copy)
                ins.then_inc(uc_ready, 1)
                round_weights(T_J1 + 4, m, 6)
                for n in range(2):
                    act.wait_ge(w_used, 6 * m + (T_J1 + n + 4))
                    act.wait_ge(j1_merge, 4 * m + (n + 2))
                    gate_tanh(n, n, hbias[:, ds(2 * m + (16 + n), 1)]).then_inc(j1_th, 1)
                    round_weights(T_J1 + 5 + n, m, 6)
                round_weights(T_J1 + 7, m, 6)
                act.wait_ge(y_done, m + 1)
                for q in range(ROUND):
                    for i in range(L):
                        dst = yaf[32 * q:32 * q + 32, ds(m, 1), :].rearrange("p a (c j) -> p (a c) j", j=L)
                        ins = nc.scalar.activation(dst[:, :, i], bank[7][32 * i:32 * i + 32, q * NC:(q + 1) * NC],
                                                   ACT.Gelu_apprx_tanh)
                ins.then_inc(y_taken, 1)
            act.wait_ge(y_taken, ROUNDS + 1)
            for c in range(KB):
                nc.scalar.activation(ya_hi[:, c, :], yaf[:, c, :], ACT.Copy).then_inc(ya_hi_s, 1)
            for c in range(KB):
                act.wait_ge(w_used, T_GLU + c // 2 + 1)
                act.wait_ge(j1_merge, 17)
                if c >= 2:
                    act.wait_ge(y2_f, c - 1)
                gate_tanh(c % 2, c, hbias[:, 24 + c:25 + c]).then_inc(glu_th, 1)
                if c % 2:
                    round_weights(T_GLU + 2 + c // 2)
                act.wait_ge(y2_f, c + 1)
                nc.scalar.activation(y2_hi[:, c, :], y2f[:, c % 2, :], ACT.Copy).then_inc(y2_hi_s, 1)
            act.wait_ge(y2_lo_s, KB)
            before(act, j2_th)
            with nc.scalar.Fori(0, 2) as i:
                for p in range(2):
                    for n in range(2):
                        g = 2 * p + n
                        act.wait_ge(w_used, 6 * i + (T_J2 + 3 * p + n + 1))
                        act.wait_ge(j2_prod, 4 * i + (g if g >= 2 else 1))
                        gate_tanh(n, 4 * p + n, hbias[:, ds(4 * i + g, 1)]).then_inc(j2_th, 1)
                        round_weights(T_J2 + 3 * p + 2 + n, i, 6)
                    round_weights(T_J2 + 3 * p + 4, i, 6)
                    for n in range(2):
                        g = 2 * p + n
                        act.wait_ge(j2_m, 4 * i + (g + 1))
                        nc.scalar.activation(mg_hi[:, ds(4 * i + g, 1), :], mf[:, n:n + 1, :], ACT.Copy
                                             ).then_inc(j2_hi, 1)
            s = norms["f"]
            with nc.scalar.Fori(0, 2) as i:
                for c in range(4):
                    round_weights(T_WO + c + 2, i, 4)
                    act.wait_ge(x1_ready, 4 * i + (c + 2))
                    act.wait_ge(s["sum"], 4 * i + (c if c >= 2 else 1))
                    nc.scalar.activation(sq[:, c % 2:c % 2 + 1, :], xT[:, ds(4 * i + c, 1), :], ACT.Square
                                         ).then_inc(s["sq"], 1)
            root(s, 4, T)
            for k in range(KD):
                round_tile(s, h_hi[:, k, :], k, T)
            before(act, ff_silu)
            with nc.scalar.Fori(0, KF // 2) as i:
                for n in range(2):
                    act.wait_ge(w_used, 4 * i + (T_FF + n + 1))
                    act.wait_ge(ff_act, 2 * i + 1)
                    nc.scalar.activation(silu[:, n, :], bank[n][:, :], ACT.Silu).then_inc(ff_silu, 1)
                    round_weights(T_FF + 2 + n, i, 4)
                for n in range(2):
                    round_weights(T_FF + 4 + n, i, 4)
                    act.wait_ge(ff_act, 2 * i + (n + 2))
                    nc.scalar.activation(act_hi[:, ds(2 * i + n, 1), :], actf[:, n:n + 1, :], ACT.Copy
                                         ).then_inc(ff_hi, 1)
            with nc.scalar.Fori(0, KF // 2 - 1) as i:
                for j in range(2):
                    round_weights(T_DN + 2 + j, i, 2)
            s = norms["o"]
            for k in range(KD):
                act.wait_ge(x2_ready, k + 1)
                square(s, xT[:, k, :], k, T)
            root(s, 0, T)

        @block.vector
        def _(dve):
            V = nc.vector
            steps = Steps(dve, dve_step)
            go, link = steps.go, steps.link

            def tt(out, a, b, op):
                return V.tensor_tensor(out, a, b, op)

            def add_square(s, k, width, value):
                dve.wait_ge(s["sq"], value)
                if k == 0:
                    V.tensor_copy(sqsum[:, 0:width], sq[:, 0, 0:width]).then_inc(s["sum"], 1)
                else:
                    dve.wait_ge(s["sum"], k)
                    tt(sqsum[:, 0:width], sqsum[:, 0:width], sq[:, k % 2, 0:width], ALU.add).then_inc(s["sum"], 1)

            def normalise(s, src, gain, hi, lo, width):
                dve.wait_ge(s["std"], 1)
                link(V.reciprocal(rstd[:, 0:width], std[:, 0:width]))

                def low(k):
                    dve.wait_ge(s["hi"], k + 1)
                    tt(lo[:, k, :], hn[:, k % 2, 0:width], fv(hi[:, k, :]), ALU.subtract).then_inc(s["lo"], 1)

                for k in range(KD):
                    if k >= 2:
                        dve.wait_ge(s["lo"], k - 1)
                    V.scalar_tensor_tensor(hn[:, k % 2, 0:width], src[:, k, :], small[:, gain + k:gain + k + 1],
                                           rstd[:, 0:width], ALU.mult, ALU.mult).then_inc(s["hn"], 1)
                    if k >= 1:
                        low(k - 1)
                low(KD - 1)
                dve.wait_ge(s["lo"], KD)

            for k in range(KD):
                add_square(norms["x"], k, T, k + 1)
            dve.wait_ge(small_loaded, 16)
            normalise(norms["x"], xT, C_GMIX, h_hi, h_lo, T)
            dve.wait_ge(norms["x"]["ssq"], 1)
            for k in range(KD):
                add_square(norms["m"], k, M, k + 1)
            normalise(norms["m"], memf, C_GMEM, m_hi, m_lo, M)

            (DT, MAG, SN, CS, XR, RC, RR, TH, ARE, AIM, T0, T1, T2, FRE, FIM, M4, ER, EI, T3, T4) = (
                s5p[:, i, :] for i in range(20))
            are, aim = small[:, C_ARE:C_ARE + 16], small[:, C_AIM:C_AIM + 16]
            dve.wait_ge(dt_ready, 1)
            go(tt(XR, are, DT, ALU.mult))
            link(tt(TH, aim, DT, ALU.mult))
            link(V.tensor_scalar(T0, TH, 1.0 / TWO_PI, ROUNDER, ALU.mult, ALU.add))
            link(V.tensor_scalar(T1, T0, ROUNDER, None, ALU.subtract))
            link(V.scalar_tensor_tensor(T0, T1, -PI_HI, TH, ALU.mult, ALU.add))
            link(V.scalar_tensor_tensor(T2, T1, -PI_MID, T0, ALU.mult, ALU.add))
            link(V.scalar_tensor_tensor(T0, T1, -PI_LO, T2, ALU.mult, ALU.add))
            link(V.tensor_scalar(RR, T0, SIN_MAX, -SIN_MAX, ALU.min, ALU.max))
            link(V.tensor_scalar(T1, RR, -1.0, None, ALU.mult))
            link(tt(T2, T1, RR, ALU.max))
            V.tensor_scalar(RC, T2, -1.0, HALF_PI, ALU.mult, ALU.add).then_inc(ang_ready, 1)
            dve.wait_ge(trig_ready, 1)
            go(tt(ARE, MAG, CS, ALU.mult))
            go(tt(AIM, MAG, SN, ALU.mult))
            go(tt(T0, are, are, ALU.mult))
            go(tt(T1, aim, aim, ALU.mult))
            steps.wait()
            go(V.tensor_scalar(T2, ARE, -1.0, None, ALU.add))
            link(tt(T3, T0, T1, ALU.add))
            link(V.reciprocal(T4, T3))
            go(tt(T0, T2, are, ALU.mult))
            go(tt(T1, AIM, aim, ALU.mult))
            steps.wait()
            link(tt(T3, T0, T1, ALU.add))
            link(tt(FRE, T3, T4, ALU.mult))
            go(tt(T0, AIM, are, ALU.mult))
            go(tt(T1, T2, aim, ALU.mult))
            steps.wait()
            link(tt(T3, T0, T1, ALU.subtract))
            link(tt(FIM, T3, T4, ALU.mult))
            def wide(v, n):
                return v.unsqueeze(2).to_broadcast([P, BLOCKS, n])

            bre = small[:, C_BRE:C_BRE + 256].rearrange("p (b h) -> p b h", h=16)
            bim = small[:, C_BIM:C_BIM + 256].rearrange("p (b h) -> p b h", h=16)
            go(tt(bb_tmp[:, 0, :, :], bre, wide(FRE, 16), ALU.mult))
            go(tt(bb_tmp[:, 1, :, :], bim, wide(FIM, 16), ALU.mult))
            go(tt(bb_tmp[:, 2, :, :], bim, wide(FRE, 16), ALU.mult))
            go(tt(bb_tmp[:, 3, :, :], bre, wide(FIM, 16), ALU.mult))
            steps.wait()
            go(tt(bre, bb_tmp[:, 0, :, :], bb_tmp[:, 1, :, :], ALU.subtract))
            go(tt(bim, bb_tmp[:, 2, :, :], bb_tmp[:, 3, :, :], ALU.add))
            cim = small[:, C_CIM:C_CIM + 256]
            link(V.tensor_scalar(cim, cim, -1.0, None, ALU.mult))
            link(tt(T0, MAG, MAG, ALU.mult))
            link(tt(M4, T0, T0, ALU.mult))

            def turn_squared(re, im, rs, is_):
                go(tt(T0, rs, rs, ALU.mult))
                go(tt(T1, is_, is_, ALU.mult))
                go(V.scalar_tensor_tensor(T2, rs, 2.0, is_, ALU.mult, ALU.mult))
                steps.wait()
                go(tt(re, T0, T1, ALU.subtract))
                link(V.tensor_copy(im, T2))

            turn_squared(ER, EI, CS, SN)
            turn_squared(ER, EI, ER, EI)
            go(V.memset(cosT[:, :, 0:1], 1.0))
            link(V.memset(sinT[:, :, 0:1], 0.0))
            n = 1
            while n < NC:
                q = [tab_tmp[:, j, :, 0:n] for j in range(4)]
                go(tt(q[0], cosT[:, :, 0:n], wide(ER, n), ALU.mult))
                go(tt(q[1], sinT[:, :, 0:n], wide(EI, n), ALU.mult))
                go(tt(q[2], sinT[:, :, 0:n], wide(ER, n), ALU.mult))
                go(tt(q[3], cosT[:, :, 0:n], wide(EI, n), ALU.mult))
                steps.wait()
                go(tt(cosT[:, :, n:2 * n], q[0], q[1], ALU.subtract))
                link(tt(sinT[:, :, n:2 * n], q[2], q[3], ALU.add))
                n *= 2
                if n < NC:
                    turn_squared(ER, EI, ER, EI)

            for c in range(4):
                dve.wait_ge(zv_taken, c + 1)
                link(V.bn_stats(stats[:, c, :], vtok[:, c, :]))
                V.bn_aggr(mv[:, c, :], stats[:, c, :]).then_inc(var_ready, 1)
            for c in range(KB):
                dve.wait_ge(w_used, T_ZQ + c + 1)
                V.tensor_copy(qT[:, c, :], bank[4 + c][:, :]).then_inc(zq_taken, 1)
            dve.wait_ge(vstd_ready, 1)
            link(V.reciprocal(vrs[:, :], vstd[:, :]))
            dve.wait_ge(sgu_loaded, 16)
            for c in range(4):
                link(V.tensor_scalar(vtok[:, c, :], vtok[:, c, :], mv[:, c, 0:1], vrs[:, c:c + 1],
                                     ALU.subtract, ALU.mult))
                link(tt(vtok[:, c, :], vtok[:, c, :], sgu[:, 0, :], ALU.mult))
                tt(vtok[:, c, :], vtok[:, c, :], sgu[:, 1, :], ALU.add).then_inc(vln_ready, 1)
            for c in range(HEADS):
                dve.wait_ge(w_used, T_K + c + 1)
                V.tensor_copy(kT[:, c, :], bank[c][:, 0:M]).then_inc(k_taken, 1)

            def head_max(h):
                for half in range(2):
                    i = 4 * h + 2 * half
                    dve.wait_ge(sc_done, 2 * h + half + 1)
                    b = (4, 6, 6, 2)[h] + half
                    link(V.tensor_reduce(smx[:, i:i + 2], bank[b][:, :].rearrange("p (a m) -> p a m", m=M),
                                         AX, ALU.max))
                    V.tensor_scalar(snm[:, i:i + 2], smx[:, i:i + 2], -SCALE, None, ALU.mult
                                    ).then_inc(mx_ready, 1)

            def head_scale(h):
                dve.wait_ge(exp_done, 4 * h + 4)
                link(V.reciprocal(srec[:, 4 * h:4 * h + 4], ssum[:, 4 * h:4 * h + 4]))
                for t4 in range(4):
                    i = 4 * h + t4
                    V.tensor_scalar(prob[:, i % 8, :], prob[:, i % 8, :], srec[:, i:i + 1], None, ALU.mult
                                    ).then_inc(p_ready, 1)

            def take_pt(h):
                dve.wait_ge(pt_done, h + 1)
                if h >= 2:
                    dve.wait_ge(pv_done, h - 1)
                V.tensor_copy(pT[:, h % 2, 1, :], bank[(5, 5, 5, 7)[h]][:, :]).then_inc(pt_dve, 1)

            def low_o(h):
                dve.wait_ge(o_hi_s, h + 1)
                return tt(o_loT[:, h, :], bank[h % 2][:, :], fv(o_hiT[:, h, :]), ALU.subtract)

            head_max(0)
            head_max(1)
            for c in range(2):
                dve.wait_ge(w_used, T_V + 4)
                V.tensor_copy(vM[:, c, :], bank[c][:, :]).then_inc(v_taken, 1)
            head_scale(0)
            for g in range(4):
                dve.wait_ge(sgu_done, g + 1)
                b = (2, 3, 0, 1)[g]
                bias = sgu[:, 2, g * P:(g + 1) * P].unsqueeze(1).to_broadcast([P, 4, P])
                tt(prod[:, :].rearrange("p (b t) -> p b t", b=4), bank[b][:, :].rearrange("p (b t) -> p b t", b=4),
                   bias, ALU.add).then_inc(sgu_taken, 1)
                dve.wait_ge(sgu_taken, g + 1)
                tt(ug[:, g, :], prod[:, :], ug[:, g, :], ALU.mult).then_inc(yb_f, 1)
                dve.wait_ge(yb_f, g + 1)
            head_scale(1)
            take_pt(0)
            head_max(2)
            for g in range(4):
                dve.wait_ge(yb_hi_s, g + 1)
                tt(yb_lo[:, g, :], ug[:, g, :], fv(yb_hi[:, g, :]), ALU.subtract).then_inc(yb_lo_s, 1)
            take_pt(1)
            head_scale(2)
            head_max(3)
            low_o(0).then_inc(o_lo_s, 1)
            low_o(1).then_inc(o_lo_s, 1)
            head_scale(3)
            take_pt(2)
            take_pt(3)
            low_o(2).then_inc(o_lo_s, 1)
            low_o(3).then_inc(o_lo_s, 1)
            dve.wait_ge(yb_lo_s, 4)
            dve.wait_ge(pv_done, 4)
            for i in range(2):
                go(V.memset(ba[i][:, :, L - 1, :], 0.0))
                go(V.memset(ca[i][:, :, 0, :], 0.0))
                go(V.memset(st[i][:, :, 0:1], 0.0))
            go(V.memset(toep[:, :, :], 0.0))
            steps.wait()
            before(dve, j1_merge, s5_const)

            def blk(v, m):
                return v[:, ds(4 * m, 4)]

            with nc.vector.Fori(0, ROUNDS) as m:
                steps.enter(m, 75)
                dve.wait_ge(y_taken, m + 1)
                for i, (cb, cc) in enumerate(((C_BRE, C_CRE), (C_BIM, C_CIM))):
                    for g in range(2):
                        pr = slice(64 * g, 64 * g + 64)
                        for dst, col in ((ba[i][pr, :, L - 1, 16 * g:16 * g + 16], cb),
                                         (ca[i][pr, :, 0, 16 * g:16 * g + 16], cc)):
                            src = small[pr, col:col + 256].rearrange("p (b h) -> p b h", h=16)[:, ds(4 * m, 4), :]
                            go(V.tensor_copy(dst, src))
                steps.wait()
                dre = s5p[:, 8, :][:, ds(4 * m, 4)].unsqueeze(2).to_broadcast([P, ROUND, CH])
                dim = s5p[:, 9, :][:, ds(4 * m, 4)].unsqueeze(2).to_broadcast([P, ROUND, CH])
                q = [rot[j][:, :, 0:CH] for j in range(4)]
                for j in range(L - 2, -1, -1):
                    go(tt(q[0], ba[0][:, :, j + 1, :], dre, ALU.mult))
                    go(tt(q[1], ba[1][:, :, j + 1, :], dim, ALU.mult))
                    go(tt(q[2], ba[1][:, :, j + 1, :], dre, ALU.mult))
                    go(tt(q[3], ba[0][:, :, j + 1, :], dim, ALU.mult))
                    steps.wait()
                    go(tt(ba[0][:, :, j, :], q[0], q[1], ALU.subtract))
                    link(tt(ba[1][:, :, j, :], q[2], q[3], ALU.add))
                for j in range(1, L + 1):
                    go(tt(q[0], ca[0][:, :, j - 1, :], dre, ALU.mult))
                    go(tt(q[1], ca[1][:, :, j - 1, :], dim, ALU.mult))
                    go(tt(q[2], ca[1][:, :, j - 1, :], dre, ALU.mult))
                    go(tt(q[3], ca[0][:, :, j - 1, :], dim, ALU.mult))
                    steps.wait()
                    go(tt(ca[0][:, :, j, :], q[0], q[1], ALU.add))
                    ins = tt(ca[1][:, :, j, :], q[2], q[3], ALU.subtract)
                    if j < L:
                        link(ins)
                    else:
                        ins.then_inc(bc_ready, 1)
                dve.wait_ge(gt_done, m + 1)
                go(V.tensor_copy(flat(gt[0][:, :, :]), bank[4][:, :]))
                go(V.tensor_copy(flat(gt[1][:, :, :]), bank[5][:, :]))
                resp = bank[6][0:CH, :].rearrange("p (b c) -> p b c", b=ROUND)
                go(V.tensor_copy(toep[0:CH, :, CH:P], resp[:, :, CH:P]))
                skip = small[0:CH, C_D:C_D + 16][:, ds(4 * m, 4)].unsqueeze(2).to_broadcast([CH, ROUND, CH])
                diag = rot[0][0:CH, :, 0:CH]
                link(tt(diag, ident[0:CH, 0:CH].unsqueeze(1).to_broadcast([CH, ROUND, CH]), skip, ALU.mult))
                link(tt(toep[0:CH, :, 0:CH], resp[:, :, 0:CH], diag, ALU.add))
                for j in range(1, L):
                    ins = V.tensor_copy(toep[CH * j:CH * j + CH, :, CH * j:P], toep[0:CH, :, 0:P - CH * j])
                ins.then_inc(gt_ready, 1)

                def merge(first, n):
                    val = 4 * m + ((0 if first else 2) + n + 1)
                    dve.wait_ge(w_used, 6 * m + (T_J1 + (3 if first else 6)))
                    dve.wait_ge(j1_th, val + 1)
                    dst = mgf[:, ds(2 * m + n, 1), :].rearrange("p a t -> p (a t)")
                    if first:
                        V.scalar_tensor_tensor(dst, th[:, n, :], 1.0, bank[2 + n][:, :], ALU.add, ALU.mult
                                               ).then_inc(j1_merge, 1)
                    else:
                        V.scalar_tensor_tensor(prod[:, :], th[:, n, :], 1.0, bank[2 + n][:, :], ALU.add,
                                               ALU.mult).then_inc(j1_merge, 1)
                        dve.wait_ge(j1_merge, val + 1)
                        link(tt(dst, dst, prod[:, :], ALU.add))

                merge(True, 0)
                merge(True, 1)
                dve.wait_ge(vin_done, m + 1)
                vre = bank[4][:, :].rearrange("p (b c) -> p b c", b=ROUND)
                vim = bank[5][:, :].rearrange("p (b c) -> p b c", b=ROUND)
                cos, sin = cosT[:, ds(4 * m, 4), :], sinT[:, ds(4 * m, 4), :]
                go(tt(rot[0][:, :, :], vre, cos, ALU.mult))
                go(tt(rot[1][:, :, :], vim, sin, ALU.mult))
                go(tt(rot[2][:, :, :], vim, cos, ALU.mult))
                go(tt(rot[3][:, :, :], vre, sin, ALU.mult))
                steps.wait()
                go(tt(rot[0][:, :, :], rot[0][:, :, :], rot[1][:, :, :], ALU.add))
                link(tt(rot[2][:, :, :], rot[2][:, :, :], rot[3][:, :, :], ALU.subtract))
                for b in range(ROUND):
                    decay = s5p[:, 15, :][:, ds(4 * m + b, 1)].to_broadcast([P, NC])
                    go(V.tensor_tensor_scan(rot[1][:, b, :], decay, rot[0][:, b, :], 0.0, ALU.mult, ALU.add))
                    go(V.tensor_tensor_scan(rot[3][:, b, :], decay, rot[2][:, b, :], 0.0, ALU.mult, ALU.add))
                steps.wait()
                rre, rim = rot[1][:, :, 0:NC - 1], rot[3][:, :, 0:NC - 1]
                cos, sin = cosT[:, ds(4 * m, 4), 0:NC - 1], sinT[:, ds(4 * m, 4), 0:NC - 1]
                q0, q2 = rot[0][:, :, 0:NC - 1], rot[2][:, :, 0:NC - 1]
                go(tt(q0, rre, cos, ALU.mult))
                go(tt(q2, rim, sin, ALU.mult))
                steps.wait()
                link(tt(st[0][:, :, 1:NC], q0, q2, ALU.subtract))
                go(tt(q0, rre, sin, ALU.mult))
                go(tt(q2, rim, cos, ALU.mult))
                steps.wait()
                tt(st[1][:, :, 1:NC], q0, q2, ALU.add).then_inc(st_ready, 1)
                merge(False, 0)
                merge(False, 1)
                dve.wait_ge(st_ready, m + 1)
                dve.wait_ge(gt_ready, m + 1)
                dve.wait_ge(bc_ready, m + 1)
            steps.leave(ROUNDS)
            for c in range(KB):
                dve.wait_ge(ya_hi_s, c + 1)
                tt(ya_lo[:, c, :], yaf[:, c, :], fv(ya_hi[:, c, :]), ALU.subtract).then_inc(ya_lo_s, 1)
            dve.wait_ge(ya_lo_s, KB)
            for c in range(KB):
                dve.wait_ge(glu_th, c + 1)
                if c >= 2:
                    dve.wait_ge(y2_lo_s, c - 1)
                V.scalar_tensor_tensor(y2f[:, c % 2, :], th[:, c % 2, :], 1.0, yaf[:, c, :], ALU.add, ALU.mult
                                       ).then_inc(y2_f, 1)
                dve.wait_ge(y2_hi_s, c + 1)
                tt(y2_lo[:, c, :], y2f[:, c % 2, :], fv(y2_hi[:, c, :]), ALU.subtract).then_inc(y2_lo_s, 1)
            dve.wait_ge(y2_lo_s, KB)
            before(dve, j2_prod, j2_lo)
            with nc.vector.Fori(0, 2) as i:
                for p in range(2):
                    for n in range(2):
                        g = 2 * p + n
                        dve.wait_ge(w_used, 6 * i + (T_J2 + 3 * p + 3))
                        dve.wait_ge(j2_th, 4 * i + (g + 2))
                        if g:
                            dve.wait_ge(j2_m, 4 * i + g)
                        V.scalar_tensor_tensor(prod[:, :], th[:, n, :], 1.0, bank[4 * p + 2 + n][:, :],
                                               ALU.add, ALU.mult).then_inc(j2_prod, 1)
                        dve.wait_ge(j2_prod, 4 * i + (g + 2))
                        dve.wait_ge(j2_lo, 4 * i + (g if g >= 2 else 1))
                        V.scalar_tensor_tensor(mf[:, n, :], prod[:, :], 0.5,
                                               mgf[:, ds(4 * i + g, 1), :].rearrange("p a t -> p (a t)"),
                                               ALU.mult, ALU.add).then_inc(j2_m, 1)
                    for n in range(2):
                        g = 2 * p + n
                        dve.wait_ge(j2_hi, 4 * i + (g + 1))
                        tt(mg_lo[:, ds(4 * i + g, 1), :], mf[:, n:n + 1, :], fv(mg_hi[:, ds(4 * i + g, 1), :]),
                           ALU.subtract).then_inc(j2_lo, 1)
            s = norms["f"]
            V.memset(sqsum[:, :], 0.0).then_inc(s["sum"], 1)
            before(dve, x1_ready)
            with nc.vector.Fori(0, 2) as i:
                for c in range(4):
                    dve.wait_ge(w_used, 4 * i + (T_WO + c + 1))
                    xi = xT[:, ds(4 * i + c, 1), :].rearrange("p a t -> p (a t)")
                    V.scalar_tensor_tensor(xi, bank[c][:, :], 0.5, xi, ALU.mult, ALU.add).then_inc(x1_ready, 1)
                    dve.wait_ge(s["sq"], 4 * i + (c + 1))
                    dve.wait_ge(s["sum"], 4 * i + (c + 1))
                    tt(sqsum[:, :], sqsum[:, :], sq[:, c % 2, :], ALU.add).then_inc(s["sum"], 1)
            normalise(s, xT, C_GFFN, h_hi, h_lo, T)
            before(dve, ff_act, ff_lo)
            with nc.vector.Fori(0, KF // 2) as i:
                for n in range(2):
                    dve.wait_ge(w_used, 4 * i + (T_FF + n + 3))
                    dve.wait_ge(ff_silu, 2 * i + (n + 2))
                    dve.wait_ge(ff_lo, 2 * i + 1)
                    tt(actf[:, n, :], bank[2 + n][:, :], silu[:, n, :], ALU.mult).then_inc(ff_act, 1)
                for n in range(2):
                    dve.wait_ge(ff_hi, 2 * i + (n + 1))
                    tt(act_lo[:, ds(2 * i + n, 1), :], actf[:, n:n + 1, :], fv(act_hi[:, ds(2 * i + n, 1), :]),
                       ALU.subtract).then_inc(ff_lo, 1)
            s = norms["o"]
            for k in range(KD):
                dve.wait_ge(dn_done, k + 1)
                tt(xT[:, k, :], bank[k][:, :], xT[:, k, :], ALU.add).then_inc(x2_ready, 1)
                if k:
                    add_square(s, k - 1, T, k)
            add_square(s, KD - 1, T, KD)
            dve.wait_ge(s["std"], 1)
            link(V.reciprocal(rstd[:, :], std[:, :]))
            for k in range(KD):
                V.scalar_tensor_tensor(xT[:, k, :], xT[:, k, :], small[:, C_GFIN + k:C_GFIN + k + 1],
                                       rstd[:, :], ALU.mult, ALU.mult).then_inc(out_ready, 1)

        @block.tensor
        def _(pe):
            mm = nc.tensor.matmul

            def product(out, a, b, first, last):
                mm(out, a[0], b[0], start=first, stop=False)
                mm(out, a[0], b[1], start=False, stop=False)
                return mm(out, a[1], b[0], start=False, stop=last)

            def weight(slot, k, c0, n, width):
                lo = k * width + c0
                return w_hi[:, slot % NS, lo:lo + n], w_lo[:, slot % NS, lo:lo + n]

            def pair(hi, lo, k):
                return hi[:, k, :], lo[:, k, :]

            def column_tile(out, slot, x, kn, c0=0, width=P):
                for k in range(kn):
                    ins = product(out, weight(slot, k, c0, P, width), x(k), k == 0, k == kn - 1)
                return ins

            def tile_ready(t):
                pe.wait_ge(w_ready, t + 1)

            def h(k):
                return pair(h_hi, h_lo, k)

            def square_sum(s, b, width, count):
                pe.wait_ge(s["sum"], count)
                mm(bank[b][:, 0:width], ones[:, :], sqsum[:, 0:width], start=True, stop=True).then_inc(s["ssq"], 1)

            pe.wait_ge(consts, 1)
            square_sum(norms["x"], 7, T, KD)
            for c in range(KB):
                tile_ready(T_ZA + c)
                for k in range(KD):
                    if c == 0:
                        pe.wait_ge(norms["x"]["lo"], k + 1)
                    ins = product(bank[c][:, :], weight(c, k, 0, P, P), h(k), k == 0, k == KD - 1)
                ins.then_inc(w_used, 1)
            square_sum(norms["m"], 6, M, KD)
            for c in range(KB):
                tile_ready(T_ZU + c)
                if c == 2:
                    pe.wait_ge(norms["m"]["std"], 1)
                column_tile(bank[4 + c][:, :], c, h, KD).then_inc(w_used, 1)
            pe.wait_ge(za_taken, KB)
            for t in range(4):
                tile_ready(T_ZV + t)
                for c in range(4):
                    for j in range(2):
                        k = 2 * t + j
                        ins = product(bank[c][:, :], [x[:, c * P:(c + 1) * P] for x in h(k)],
                                      weight(t, j, 0, WB, WB), k == 0, k == KD - 1)
                ins.then_inc(w_used, 1)
            for c in range(KB):
                tile_ready(T_ZQ + c)
                pe.wait_ge(zu_taken, c + 1)
                column_tile(bank[4 + c][:, :], c, h, KD).then_inc(w_used, 1)
            pe.wait_ge(norms["m"]["lo"], KD)
            for c in range(KB):
                tile_ready(T_K + c)
                pe.wait_ge(zv_taken, c + 1)
                column_tile(bank[c][:, 0:M], c, lambda k: pair(m_hi, m_lo, k), KD).then_inc(w_used, 1)

            def scores(head):
                for half in range(2):
                    b = (4, 6, 6, 2)[head] + half
                    for j in range(2):
                        t0 = (2 * half + j) * P
                        ins = mm(bank[b][:, j * M:(j + 1) * M], qT[:, head, t0:t0 + P], kT[:, head, :],
                                 start=True, stop=True)
                    ins.then_inc(sc_done, 1)

            def transposes(head):
                pe.wait_ge(p_ready, 4 * head + 4)
                for half in range(2):
                    b = (4, 4, 4, 6)[head] + half
                    for t in range(4):
                        ins = nc.tensor.transpose(bank[b][:, t * P:(t + 1) * P],
                                                  prob[:, (4 * head + t) % 8, half * P:(half + 1) * P], ident)
                ins.then_inc(pt_done, 1)

            def values(head):
                pe.wait_ge(pt_act, head + 1)
                pe.wait_ge(pt_dve, head + 1)
                for half in range(2):
                    ins = mm(bank[head % 2][:, :], vM[:, half, head * P:(head + 1) * P], pT[:, head % 2, half, :],
                             start=half == 0, stop=half == 1)
                ins.then_inc(pv_done, 1)

            pe.wait_ge(k_taken, HEADS)
            pe.wait_ge(zq_taken, KB)
            scores(0)
            scores(1)
            for t in range(4):
                tile_ready(T_V + t)
                for c in range(2):
                    for j in range(2):
                        k = 2 * t + j
                        ins = product(bank[c][:, :], [x[:, c * P:(c + 1) * P] for x in pair(m_hi, m_lo, k)],
                                      weight(t, j, 0, WB, WB), k == 0, k == KD - 1)
                ins.then_inc(w_used, 1)
            pe.wait_ge(vln_ready, 4)
            pe.wait_ge(wst_masked, 1)
            for g in range(4):
                if g >= 2:
                    pe.wait_ge(v_taken, g - 1)
                for b in range(4):
                    ins = mm(bank[(2, 3, 0, 1)[g]][:, b * P:(b + 1) * P], vtok[:, b, g * P:(g + 1) * P],
                             sgu[:, 3, g * P:(g + 1) * P], start=True, stop=True)
                ins.then_inc(sgu_done, 1)
            transposes(0)
            pe.wait_ge(exp_done, 8)
            scores(2)
            pe.wait_ge(pt_act, 1)
            pe.wait_ge(pt_dve, 1)
            transposes(1)
            pe.wait_ge(sgu_taken, 2)
            scores(3)
            pe.wait_ge(sgu_taken, 3)
            values(0)
            pe.wait_ge(sgu_taken, 4)
            values(1)
            transposes(2)
            transposes(3)
            pe.wait_ge(o_lo_s, 1)
            values(2)
            pe.wait_ge(o_lo_s, 2)
            values(3)

            pe.wait_ge(yb_lo_s, 4)
            pe.wait_ge(o_lo_s, 4)
            with nc.tensor.Fori(0, ROUNDS) as m:
                def gates(j0, b0, free):
                    for n in range(2):
                        pe.wait_ge(w_ready, 6 * m + (T_J1 + j0 + n + 1))
                        pe.wait_ge(j1_th, 4 * m + free[n])
                        column_tile(bank[b0 + n][:, :], j0 + n, h, KD).then_inc(w_used, 1)

                def outs(j0, hi, lo, free):
                    pe.wait_ge(w_ready, 6 * m + (T_J1 + j0 + 1))
                    for n in range(2):
                        pe.wait_ge(j1_merge, 4 * m + free[n])
                        ins = column_tile(bank[2 + n][:, :], j0, lambda k: pair(hi, lo, k), KB, n * P, 2 * P)
                    ins.then_inc(w_used, 1)

                gates(0, 0, (1, 1))
                pe.wait_ge(bc_ready, m + 1)
                for i in range(2):
                    for q in range(ROUND):
                        nc.tensor.transpose(bank[4 + i][:, q * P:(q + 1) * P],
                                            ba[i][:, q, :, :].rearrange("p a b -> p (a b)"), ident)
                for q in range(ROUND):
                    for i in range(2):
                        ins = mm(bank[6][0:CH, q * P:(q + 1) * P], ba[i][:, q, L - 1, :],
                                 ca[i][:, q, 0:L, :].rearrange("p a b -> p (a b)"), start=i == 0, stop=i == 1)
                ins.then_inc(gt_done, 1)
                outs(2, yb_hi, yb_lo, (1, 1))
                pe.wait_ge(gt_ready, m + 1)
                pe.wait_ge(uc_ready, m + 1)
                for i in range(2):
                    for q in range(ROUND):
                        ins = mm(bank[4 + i][:, q * P:(q + 1) * P], gt[i][:, q, :], uc[:, q, :], start=True, stop=True)
                ins.then_inc(vin_done, 1)
                gates(3, 0, (2, 3))
                outs(5, o_hiT, o_loT, (2, 3))
                pe.wait_ge(st_ready, m + 1)
                pe.wait_ge(y_taken, m + 1)
                for q in range(ROUND):
                    o = bank[7][:, q * P:(q + 1) * P]
                    mm(o, toep[:, q, :], uc[:, q, :], start=True, stop=False)
                    mm(o, ca[0][:, q, 1:L + 1, :].rearrange("p a b -> p (a b)"), st[0][:, q, :], start=False, stop=False)
                    ins = mm(o, ca[1][:, q, 1:L + 1, :].rearrange("p a b -> p (a b)"), st[1][:, q, :],
                             start=False, stop=True)
                ins.then_inc(y_done, 1)
            pe.wait_ge(ya_lo_s, KB)
            pe.wait_ge(j1_th, 17)
            pe.wait_ge(j1_merge, 17)
            for t in range(2):
                tile_ready(T_GLU + t)
                for n in range(2):
                    ins = column_tile(bank[2 * t + n][:, :], t, lambda k: pair(ya_hi, ya_lo, k), KB, n * P, 2 * P)
                ins.then_inc(w_used, 1)
            with nc.tensor.Fori(0, 2) as i:
                for p in range(2):
                    pe.wait_ge(j2_th, 4 * i + 1)
                    for n in range(2):
                        pe.wait_ge(w_ready, 6 * i + (T_J2 + 3 * p + n + 1))
                        column_tile(bank[4 * p + n][:, :], 3 * p + n, h, KD).then_inc(w_used, 1)
                    pe.wait_ge(w_ready, 6 * i + (T_J2 + 3 * p + 3))
                    pe.wait_ge(j2_prod, 4 * i + 1)
                    for n in range(2):
                        ins = column_tile(bank[4 * p + 2 + n][:, :], 3 * p + 2, lambda k: pair(y2_hi, y2_lo, k), KB,
                                          n * P, 2 * P)
                    ins.then_inc(w_used, 1)
            pe.wait_ge(j2_lo, 9)
            pe.wait_ge(j2_th, 9)
            with nc.tensor.Fori(0, 2) as i:
                pe.wait_ge(x1_ready, 4 * i + 1)
                for c in range(4):
                    pe.wait_ge(w_ready, 4 * i + (T_WO + c + 1))
                    column_tile(bank[c][:, :], c, lambda k: pair(mg_hi, mg_lo, k), KD).then_inc(w_used, 1)
            square_sum(norms["f"], 4, T, KD + 1)
            pe.wait_ge(norms["f"]["lo"], KD)
            with nc.tensor.Fori(0, KF // 2) as i:
                for g, free in enumerate((ff_silu, ff_act)):
                    pe.wait_ge(free, 2 * i + 1)
                    for n in range(2):
                        pe.wait_ge(w_ready, 4 * i + (T_FF + 2 * g + n + 1))
                        column_tile(bank[2 * g + n][:, :], n, h, KD).then_inc(w_used, 1)
            pe.wait_ge(ff_silu, KF + 1)
            pe.wait_ge(ff_act, KF + 1)
            pe.wait_ge(ff_lo, KF - 1)

            def down(slot, x, first, last):
                for n in range(KD):
                    ins = product(bank[n][:, :], weight(slot, 0, n * P, P, 0), x, first, last)
                    if last:
                        ins.then_inc(dn_done, 1)
                if not last:
                    ins.then_inc(w_used, 1)

            for k in range(2):
                tile_ready(T_DN + k)
                down(k, pair(act_hi, act_lo, k), k == 0, False)
            with nc.tensor.Fori(1, KF // 2 - 1) as i:
                for j in range(2):
                    pe.wait_ge(w_ready, 2 * i + (T_DN + j + 1))
                    x = [a[:, ds(2 * i + j, 1), :].rearrange("p a t -> p (a t)") for a in (act_hi, act_lo)]
                    down(j, x, False, False)
            pe.wait_ge(ff_lo, KF + 1)
            for k in range(KF - 2, KF):
                tile_ready(T_DN + k)
                down(k, pair(act_hi, act_lo, k), False, k == KF - 1)
            square_sum(norms["o"], 0, T, KD)


def _stream(w_in, w_kv, w_glu, w_a, w_b, w_c, w_out, w_gate, w_up, w_down):
    tiles = []

    def columns(w, c, n=1):
        part = w[:, c * P:(c + n) * P].reshape(-1, P, n * P)
        tiles.append(part.transpose(1, 0, 2).reshape(P, TILE))

    def rows(w, k, n=1):
        tiles.append(w[k * P:(k + n) * P].reshape(n, P, -1).transpose(1, 0, 2).reshape(P, TILE))

    za, zu, zv, zq, gates = np.split(w_in, [WB, 2 * WB, 3 * WB, 4 * WB], axis=1)
    for w in (za, zu):
        for c in range(KB):
            columns(w, c)
    for k in range(0, KD, 2):
        rows(zv, k, 2)
    for w in (zq, w_kv[:, :WB]):
        for c in range(KB):
            columns(w, c)
    for k in range(0, KD, 2):
        rows(w_kv[:, WB:], k, 2)
    for m in range(4):
        for g, w in ((1, w_b), (2, w_c)):
            for n in range(2):
                columns(gates, g * KD + 2 * m + n)
            columns(w, 2 * m, 2)
    for c in range(0, KB, 2):
        columns(w_glu, c, 2)
    for m in range(4):
        for n in range(2):
            columns(gates, 2 * m + n)
        columns(w_a, 2 * m, 2)
    for c in range(KD):
        columns(w_out, c)
    for f in range(0, KF, 2):
        for w in (w_gate, w_up):
            for n in range(2):
                columns(w, f + n)
    for k in range(KF):
        rows(w_down, k)
    assert len(tiles) == TILES
    return np.stack(tiles)


def kernel(**inputs):
    import concourse.bacc as bacc
    from concourse.bass_utils import run_bass_kernel_spmd

    a = {k: np.asarray(v) for k, v in inputs.items()}

    def feature_major(x, n):
        return np.ascontiguousarray(x.reshape(n, KD, P).transpose(2, 1, 0))

    def states(v):
        return v.reshape(BLOCKS, P).T

    def vector(v):
        return v.reshape(-1, P).T

    def b_rows(v):
        return v.reshape(BLOCKS, P, 16).transpose(1, 0, 2).reshape(P, 256)

    def c_rows(v):
        return b_rows(v.transpose(0, 2, 1))

    skip = np.tile(a["d_skip"][0].reshape(BLOCKS, CH).T, (L, 1))
    small = np.concatenate([
        states(a["a_re"][0]), states(a["a_im"][0]),
        states(np.broadcast_to(a["log_dt"][0][:, None], (32, 64))),
        b_rows(a["bm_re"][0]), b_rows(a["bm_im"][0]), c_rows(a["cm_re"][0]), c_rows(a["cm_im"][0]),
        skip, vector(a["g_mix"][0]), vector(a["g_mem"][0]), vector(a["g_ffn"][0]), vector(a["g_final"]),
        vector(a["b_gate"][0]), vector(a["b_glu"][0]), np.eye(P, dtype=np.float32)], axis=1)
    wide = [np.broadcast_to(v.reshape(1, WB), (P, WB)) for v in (a["g_sgu"][0], a["beta_sgu"][0], a["b_s"][0])]
    mix = a["w_s"][0].transpose(2, 0, 1).reshape(P, WB)
    arrays = {
        "xt_dram": feature_major(a["x"], T),
        "mem_dram": feature_major(a["mem"], M),
        "small_dram": np.ascontiguousarray(small),
        "sgu_dram": np.ascontiguousarray(np.stack([*wide, mix], axis=1)),
        "w_dram": _stream(*(a[k][0] for k in ("w_in", "w_kv", "w_glu", "w_a_out", "w_b_out", "w_c_out", "w_out",
                                              "w_gate", "w_up", "w_down"))),
    }
    nc = bacc.Bacc("TRN2", target_bir_lowering=False, num_devices=1)
    args = [nc.dram_tensor(n, x.shape, mybir.dt.from_np(x.dtype), kind="ExternalInput").ap()
            for n, x in arrays.items()]
    out = nc.dram_tensor("out_dram", (KD, P, T), mybir.dt.float32, kind="ExternalOutput").ap()
    build(nc, *args, out)
    r = run_bass_kernel_spmd(nc, [arrays], core_ids=[0])
    return r.results[0]["out_dram"].reshape(D, T).T.reshape(1, T, D)
```

```python
from contextlib import ExitStack

import concourse.bass as bass
import numpy as np
from concourse import mybir

P = 128
D = 1024
T = 512
M = 256
KD = D // P
WB = 512
KB = WB // P
FF = 2816
KF = FF // P
HEADS = 4
EPS = 1e-6
SCALE = 128.0 ** -0.5
TILE = 1024

BLOCKS = 16
ROUND = 4
ROUNDS = BLOCKS // ROUND
L = 4
NC = T // L
CH = 32

T_ZA, T_ZV = 0, 4
T_QK = 8
T_VU = 16
T_J1 = 24
T_J2 = T_J1 + 6 * 4
T_GLU = T_J2 + 2
T_WO = T_J2 + 14
T_FF = T_WO + KD
T_DN = T_FF + 4 * (KF // 2)
TILES = T_DN + KF
RAW = 2
NS = 2

C_GMIX, C_GMEM, C_GFFN, C_GFIN = 0, 8, 16, 24
C_BGATE = 32
C_BGLU = C_BGATE + 24
C_ID = C_BGLU + 4
C_ARE = C_ID + P
C_AIM, C_LDT = C_ARE + 16, C_ARE + 32
PADDED = BLOCKS + ROUND
C_BRE = C_ARE + 48
C_BIM = C_BRE + 16 * PADDED
C_CRE = C_BIM + 16 * PADDED
C_CIM = C_CRE + 256
C_D = C_CIM + 256
N_SMALL = C_D + 16

TWO_PI = 2 * np.pi
ROUNDER = 12582912.0
PI_HI = 6.28125
PI_MID = float(np.float32(round((TWO_PI - PI_HI) * 2 ** 20) / 2 ** 20))
PI_LO = float(np.float32(TWO_PI - PI_HI - PI_MID))
HALF_PI = float(np.float32(np.pi / 2))
SIN_MAX = 3.1415925


def build(nc, xt_d, mem_d, small_d, sgu_d, w_d, out_d):
    F = mybir.dt.float32
    R = mybir.dt.float32r
    ACT = mybir.ActivationFunctionType
    ALU = mybir.AluOpType
    AX = mybir.AxisListType.X
    ds = bass.ds

    with ExitStack() as ctx:
        def sem(name):
            return ctx.enter_context(nc.semaphore(name))

        base = (nc.sbuf_base + 63) // 64 * 64

        def at(name, off, shape, dt=F):
            return nc.alloc_sbuf_tensor_at(name, shape, dt, offset=off)

        o_raw = base
        o_hi = o_raw + RAW * 4096
        o_lo = o_hi + NS * 4096
        o_x = o_lo + NS * 4096
        o_h = o_x + 16384
        o_a = o_h + 32768
        o_b = o_a + 16384
        o_c = o_b + 32768
        o_u = o_c + 32768
        o_e = o_u + 8192
        o_f = o_e + 16384
        o_g = o_f + 8192
        o_s = o_g + 6144
        o_d = o_s + (N_SMALL * 4 + 63) // 64 * 64

        raw = at("raw", o_raw, [P, RAW, TILE])
        w_hi = at("w_hi", o_hi, [P, NS, TILE], R)
        w_lo = at("w_lo", o_lo, [P, NS, TILE], R)
        xT = at("xT", o_x, [P, KD, T])
        h_hi = at("h_hi", o_h, [P, KD, T], R)
        h_lo = at("h_lo", o_h + 16384, [P, KD, T], R)
        memf = at("memf", o_a, [P, KD, M])
        qT = at("qT", o_a, [P, HEADS, T])
        kT = at("kT", o_a + 8192, [P, HEADS, M])
        vM = at("vM", o_a + 12288, [P, 2, WB])
        mgf = at("mgf", o_a, [P, KD, T])
        vtok = at("vtok", o_b, [P, 4, WB])
        ug = at("ug", o_b + 8192, [P, KB, T])
        sgu = at("sgu", o_b + 16384, [P, 4, WB])
        prob = at("prob", o_b + 24576, [P, 8, M])
        bb_tmp = at("bb_tmp", o_b + 24576, [P, 4, BLOCKS, 16])
        ba = [at(f"ba{i}", o_b + 2048 * i, [P, ROUND, L, CH]) for i in range(2)]
        gt = [at(f"gt{i}", o_b + 4096 + 2048 * i, [P, ROUND, P]) for i in range(2)]
        ca = [at(f"ca{i}", o_b + 8192 + 4096 * i, [P, ROUND, L + 1, CH]) for i in range(2)]
        toep = at("toep", o_b + 16384, [P, ROUND, P])
        uc = at("uc", o_b + 18432, [P, ROUND, NC])
        rot = [at(f"rot{i}", o_b + 20480 + 2048 * i, [P, ROUND, NC]) for i in range(4)]
        st = [at(f"st{i}", o_b + 28672 + 2048 * i, [P, ROUND, NC]) for i in range(2)]
        ya_hi = at("ya_hi", o_b, [P, KB, T], R)
        ya_lo = at("ya_lo", o_b + 8192, [P, KB, T], R)
        y2f = at("y2f", o_b + 16384, [P, 2, T])
        mg_hi = at("mg_hi", o_b, [P, KD, T], R)
        mg_lo = at("mg_lo", o_b + 16384, [P, KD, T], R)
        m_hi = at("m_hi", o_c, [P, KD, M], R)
        m_lo = at("m_lo", o_c + 8192, [P, KD, M], R)
        yb_hi = at("yb_hi", o_c, [P, KB, T], R)
        yb_lo = at("yb_lo", o_c + 8192, [P, KB, T], R)
        y2_hi = at("y2_hi", o_c, [P, KB, T], R)
        y2_lo = at("y2_lo", o_c + 8192, [P, KB, T], R)
        tab_tmp = at("tab_tmp", o_c + 16384, [P, 4, BLOCKS, NC // 2])
        o_hiT = at("o_hiT", o_c + 16384, [P, HEADS, T], R)
        o_loT = at("o_loT", o_c + 24576, [P, HEADS, T], R)
        uT = at("uT", o_u, [P, KB, T])
        act_hi = at("act_hi", o_a, [P, KF, T], R)
        act_lo = at("act_lo", o_a + KF * T * 4, [P, KF, T], R)
        assert o_a + 2 * KF * T * 4 == o_e
        cosT = at("cosT", o_e, [P, BLOCKS, NC])
        sinT = at("sinT", o_e + 8192, [P, BLOCKS, NC])
        silu = at("silu", o_e, [P, 2, T])
        actf = at("actf", o_e + 4096, [P, 2, T])
        zg = at("zg", o_e, [P, 4, T])
        std = at("std", o_e + 10240, [P, T])
        hn = at("hn", o_f, [P, 2, T])
        pT = at("pT", o_f, [P, 2, 2, T])
        yaf = at("yaf", o_f, [P, KB, T])
        mf = at("mf", o_f, [P, 2, T])
        sq = at("sq", o_g, [P, 2, T])
        sqsum = at("sqsum", o_g + 4096, [P, T])
        th = at("th", o_g, [P, 2, T])
        prod = at("prod", o_g + 4096, [P, T])
        small = at("small", o_s, [P, N_SMALL])
        s5p = at("s5p", o_d, [P, 20, PADDED])
        o_d2 = o_d + 1600
        ones = at("ones", o_d2, [P, P])
        rstd = at("rstd", o_d2 + 512, [P, T])
        o_d3 = o_d2 + 2560
        (eps, hbias, stats, mv, vrs, vstd, smx, snm, ssum, srec, tstd, trstd) = (
            at(n, o_d3 + 128 * i, shape) for i, (n, shape) in enumerate((
                ("eps", [P, 1]), ("hbias", [P, 28]), ("stats", [P, 4, 6]), ("mv", [P, 4, 2]), ("vrs", [P, 4]),
                ("vstd", [P, 4]), ("smx", [P, 16]), ("snm", [P, 16]), ("ssum", [P, 16]), ("srec", [P, 16]),
                ("tstd", [P, 4]), ("trstd", [P, 4]))))
        assert o_d3 + 128 * 12 <= nc.sbuf_usable_end, o_d3 + 128 * 12 - nc.sbuf_usable_end

        bank = [ctx.enter_context(nc.psum_tensor(f"bank{i}", [P, T], F)) for i in range(8)]
        ident = small[:, C_ID:C_ID + P]

        def fv(t):
            return t.bitcast(F)

        def flat(ap):
            return ap.rearrange("p a b -> p (a b)")

        def sems(names):
            return [sem(n) for n in names.split()]

        raw_loaded = [sem(f"raw_loaded{i}") for i in range(RAW)]
        w_rounded, w_ready = sems("w_rounded w_ready")
        w_used = sem("w_used")
        x_loaded = [sem(f"x_loaded{i}") for i in range(4)]
        vec_loaded, small_loaded, mem_loaded, sgu_loaded = sems("vec_loaded small_loaded mem_loaded sgu_loaded")
        consts, wst_masked = sems("consts wst_masked")
        dve_step = sem("dve_step")
        norms = {n: dict(zip(("sq", "sum", "ssq", "std", "hn", "hi", "lo"),
                             sems(" ".join(f"{n}_{k}" for k in ("sq", "sum", "ssq", "std", "hn", "hi", "lo")))))
                 for n in ("x", "m", "f", "o")}
        tok_ssq, tok_std, rstd_ready = sems("tok_ssq tok_std rstd_ready")
        za_taken, zv_taken, zq_taken, k_taken, v_taken, zu_scaled, zu_ready = sems(
            "za_taken zv_taken zq_taken k_taken v_taken zu_scaled zu_ready")
        var_ready, vstd_ready, vln_ready = sems("var_ready vstd_ready vln_ready")
        sgu_done, sgu_taken, yb_f, yb_hi_s, yb_lo_s = sems("sgu_done sgu_taken yb_f yb_hi_s yb_lo_s")
        sc_done, mx_ready, exp_done, p_ready = sems("sc_done mx_ready exp_done p_ready")
        pt_done, pt_act, pt_dve, pv_done, o_hi_s, o_lo_s = sems("pt_done pt_act pt_dve pv_done o_hi_s o_lo_s")
        dt_ready, ang_ready, trig_ready, s5_const = sems("dt_ready ang_ready trig_ready s5_const")
        j1_g, j1_th, j1_merge = sems("j1_g j1_th j1_merge")
        uc_ready, bc_ready, gt_done, gt_ready, vin_done, st_ready, y_done, y_taken = sems(
            "uc_ready bc_ready gt_done gt_ready vin_done st_ready y_done y_taken")
        ya_hi_s, ya_lo_s, glu_th, y2_f, y2_hi_s, y2_lo_s = sems("ya_hi_s ya_lo_s glu_th y2_f y2_hi_s y2_lo_s")
        j2_g, j2_th, j2_prod, j2_m, j2_hi, j2_lo = sems("j2_g j2_th j2_prod j2_m j2_hi j2_lo")
        x1_ready = sem("x1_ready")
        ff_g, ff_u, ff_silu, ff_act, ff_hi, ff_lo = sems("ff_g ff_u ff_silu ff_act ff_hi ff_lo")
        dn_done, x2_ready, xg_ready, out_dve, out_pool, out_stored = sems(
            "dn_done x2_ready xg_ready out_dve out_pool out_stored")
        POOL_OUT = 3

        def before(eng, *sems):
            for x in sems:
                eng.drain().then_inc(x, 1)

        SCORE_BANK, PT_BANK = (0, 2, 0, 0), (2, 2, 0, 2)
        SGU_BANK = (6, 7, 0, 1)
        J2_TILE = [T_J2 + t for t in (0, 1, 4, 5, 8, 9, 10, 11)]
        J2_OUT = [T_J2 + t for t in (6, 7, 12, 13)]
        Y_BANK, G_BANK = (2, 3, 6, 7), (0, 1, 4, 5)

        class Steps:

            def __init__(self, eng, s):
                self.eng, self.s, self.base, self.n = eng, s, 0, 0

            def go(self, ins):
                ins.then_inc(self.s, 1)
                self.n += 1

            def wait(self):
                self.eng.wait_ge(self.s, self.base + self.n)

            def link(self, ins):
                self.go(ins)
                self.wait()

            def enter(self, i, per):
                self.outer, self.per = self.base + self.n, per
                self.base, self.n = self.base + self.n + i * per, 0

            def leave(self, count):
                assert self.n == self.per, self.n
                self.base, self.n = self.outer + count * self.per, 0

        block = ctx.enter_context(nc.Block())

        @block.sync
        def _(sp):
            def load_weights(s, t, tile):
                sp.dma_start(raw[:, s, :], tile).then_inc(raw_loaded[s], 16)

            def load_x(i):
                sp.dma_start(xT[:, 2 * i:2 * i + 2, :], xt_d[:, 2 * i:2 * i + 2, :]).then_inc(x_loaded[i], 16)

            sp.dma_start(small[:, 0:C_ARE], small_d[:, 0:C_ARE]).then_inc(vec_loaded, 16)
            load_x(0)
            load_weights(0, 0, w_d[0, :, :])
            for i in range(1, 4):
                load_x(i)
            load_weights(1, 1, w_d[1, :, :])
            sp.dma_start(memf[:, :, :], mem_d).then_inc(mem_loaded, 16)
            sp.dma_start(small[:, C_ARE:N_SMALL], small_d[:, C_ARE:N_SMALL]).then_inc(small_loaded, 16)
            sp.dma_start(sgu[:, :, :], sgu_d).then_inc(sgu_loaded, 16)
            with nc.sync.Fori(1, TILES // RAW) as i:
                for s in range(RAW):
                    sp.wait_ge(w_ready, i * RAW + (s + 1 - RAW))
                    load_weights(s, i * RAW + s, w_d[ds(i * RAW + s, 1), :, :].rearrange("a p n -> p (a n)"))
            by_pool = 0
            for n in range(KD - POOL_OUT):
                sp.wait_ge(out_dve, n + 1)
                sp.dma_start(out_d[n, :, :], xT[:, n, :]).then_inc(out_stored, 16)
                if n % 2 == 1 or n == KD - POOL_OUT - 1:
                    sp.wait_ge(out_pool, by_pool + 1)
                    k = KD - POOL_OUT + by_pool
                    sp.dma_start(out_d[k, :, :], xT[:, k, :]).then_inc(out_stored, 16)
                    by_pool += 1
            assert by_pool == POOL_OUT
            sp.wait_ge(out_stored, 16 * KD)

        @block.gpsimd
        def _(pool):
            nc.gpsimd.memset(ones[:, :], 1.0)
            nc.gpsimd.memset(eps[:, :], EPS).then_inc(consts, 1)

            def low_weights(s, t):
                pool.wait_ge(w_rounded, t + 1)
                nc.gpsimd.tensor_tensor(w_lo[:, s, :], raw[:, s, :], fv(w_hi[:, s, :]),
                                        ALU.subtract).then_inc(w_ready, 1)

            for t in range(NS):
                low_weights(t, t)
            pool.wait_ge(sgu_loaded, 16)
            wst = sgu[:, 3, :].rearrange("p (g t) -> p g t", g=4)
            nc.gpsimd.affine_select(out=wst, in_=wst, pattern=[[0, 4], [1, P]], compare_op=ALU.is_ge,
                                    fill=0.0, base=0, channel_multiplier=-1).then_inc(wst_masked, 1)
            with nc.gpsimd.Fori(1, TILES // NS) as i:
                for s in range(NS):
                    low_weights(s, i * NS + s)
            for k in range(KD - POOL_OUT, KD):
                pool.wait_ge(xg_ready, k + 1)
                pool.wait_ge(rstd_ready, 3)
                nc.gpsimd.tensor_tensor(xT[:, k, :], xT[:, k, :], rstd[:, :], ALU.mult).then_inc(out_pool, 1)

        @block.scalar
        def _(act):
            def round_weights(t, m=0, per=0):
                slot = t % NS
                act.wait_ge(raw_loaded[slot], 16 * (per // 2) * m + 16 * (t // 2 + 1))
                if t >= NS:
                    act.wait_ge(w_used, per * m + (t + 1 - NS))
                nc.scalar.activation(w_hi[:, slot, :], raw[:, slot, :], ACT.Copy).then_inc(w_rounded, 1)

            def square(s, src, k, width):
                if k >= 2:
                    act.wait_ge(s["sum"], k - 1)
                nc.scalar.activation(sq[:, k % 2, 0:width], src, ACT.Square).then_inc(s["sq"], 1)

            def root(s, b, width):
                act.wait_ge(s["ssq"], 1)
                nc.scalar.activation(std[:, 0:width], bank[b][:, 0:width], ACT.Sqrt, bias=eps[:, 0:1],
                                     scale=1.0 / D).then_inc(s["std"], 1)

            def round_tile(s, dst, k, width):
                act.wait_ge(s["hn"], k + 1)
                nc.scalar.activation(dst, hn[:, k % 2, 0:width], ACT.Copy).then_inc(s["hi"], 1)

            for k in range(KD):
                round_tile(norms["x"], h_hi[:, k, :], k, T)
                if k == 0:
                    round_weights(0)
            round_weights(1)
            for k in range(KD):
                square(norms["x"], xT[:, k, :], k, T)
            round_weights(T_ZA + 2)
            act.wait_ge(consts, 1)
            root(norms["x"], 7, T)
            act.wait_ge(tok_ssq, 1)
            nc.scalar.activation(tstd[:, :], bank[6][:, 0:4], ACT.Sqrt, bias=eps[:, 0:1], scale=1.0 / D
                                 ).then_inc(tok_std, 1)
            round_weights(T_ZA + 3)
            act.wait_ge(mem_loaded, 16)
            act.wait_ge(norms["x"]["sum"], KD)
            for k in range(KD):
                square(norms["m"], memf[:, k, :], k, M)
            round_weights(T_ZV)
            round_weights(T_ZV + 1)
            act.wait_ge(rstd_ready, 1)
            root(norms["m"], 6, M)
            act.wait_ge(small_loaded, 16)
            nc.scalar.activation(s5p[:, 0, 0:16], small[:, C_LDT:C_LDT + 16], ACT.Exp).then_inc(dt_ready, 1)
            for k in range(KD):
                round_tile(norms["m"], m_hi[:, k, :], k, M)
            round_weights(T_ZV + 2)
            act.wait_ge(ang_ready, 1)
            nc.scalar.activation(s5p[:, 1, 0:16], s5p[:, 4, 0:16], ACT.Exp)
            nc.scalar.activation(s5p[:, 2, 0:16], s5p[:, 6, 0:16], ACT.Sin)
            nc.scalar.activation(s5p[:, 3, 0:16], s5p[:, 5, 0:16], ACT.Sin).then_inc(trig_ready, 1)
            round_weights(T_ZV + 3)
            round_weights(T_QK)
            round_weights(T_QK + 1)
            act.wait_ge(w_used, T_ZV + 4)
            act.wait_ge(rstd_ready, 1)
            for c in range(4):
                nc.scalar.activation(vtok[:, c, :], bank[4 + c][:, :], ACT.Gelu_apprx_tanh,
                                     scale=trstd[:, c:c + 1]).then_inc(zv_taken, 1)
            for t in range(2, 6):
                round_weights(T_QK + t)
            act.wait_ge(var_ready, 4)
            nc.scalar.activation(vstd[:, :], mv[:, :, 1], ACT.Sqrt, bias=eps[:, 0:1]).then_inc(vstd_ready, 1)
            for t in range(6, 10):
                round_weights(T_QK + t)

            def softmax_exp(h):
                for tt in range(4):
                    act.wait_ge(mx_ready, 2 * h + tt // 2 + 1)
                    if h >= 2:
                        act.wait_ge(pt_done, h - 1)
                    i = 4 * h + tt
                    b = SCORE_BANK[h] + tt // 2
                    nc.scalar.activation(prob[:, i % 8, :], bank[b][:, (tt % 2) * M:(tt % 2 + 1) * M], ACT.Exp,
                                         bias=snm[:, i:i + 1], scale=SCALE, accum_out=ssum[:, i:i + 1]
                                         ).then_inc(exp_done, 1)

            def gelu_u(c):
                act.wait_ge(zu_scaled, c + 1)
                nc.scalar.activation(ug[:, c, :], ug[:, c, :], ACT.Gelu_apprx_tanh).then_inc(zu_ready, 1)

            def take_pt(h):
                act.wait_ge(pt_done, h + 1)
                if h >= 2:
                    act.wait_ge(pv_done, h - 1)
                nc.scalar.activation(pT[:, h % 2, 0, :], bank[PT_BANK[h]][:, :], ACT.Copy).then_inc(pt_act, 1)

            def round_o(h):
                act.wait_ge(pv_done, h + 1)
                nc.scalar.activation(o_hiT[:, h, :], bank[4 + h % 2][:, :], ACT.Copy).then_inc(o_hi_s, 1)

            def round_yb(g):
                act.wait_ge(yb_f, g + 1)
                nc.scalar.activation(yb_hi[:, g, :], ug[:, g, :], ACT.Copy).then_inc(yb_hi_s, 1)

            softmax_exp(0)
            softmax_exp(1)
            round_weights(T_VU + 2)
            round_weights(T_VU + 3)
            gelu_u(0)
            round_weights(T_VU + 4)
            take_pt(0)
            softmax_exp(2)
            round_weights(T_VU + 5)
            gelu_u(1)
            round_weights(T_VU + 6)
            round_weights(T_VU + 7)
            gelu_u(2)
            round_weights(T_J1)
            take_pt(1)
            softmax_exp(3)
            round_weights(T_J1 + 1)
            gelu_u(3)
            take_pt(2)
            round_o(0)
            take_pt(3)
            round_o(1)
            for g in range(4):
                round_yb(g)
            round_o(2)
            round_o(3)
            act.wait_ge(vec_loaded, 16)
            nc.scalar.mul(hbias[:, :], small[:, C_BGATE:C_BGATE + 28], 0.5)
            act.wait_ge(s5_const, 1)
            before(act, y_taken)
            act.wait_ge(y_taken, 1)

            def half_tanh(buf, src, bias):
                return nc.scalar.activation(buf, src, ACT.Tanh, bias=bias, scale=0.5)

            def gate(n, m, done, col):
                act.wait_ge(j1_g, 4 * m + (done + 1))
                half_tanh(th[:, n, :], th[:, n, :], hbias[:, ds(2 * m + (col + n), 1)]).then_inc(j1_th, 1)

            with nc.scalar.Fori(0, ROUNDS) as m:
                for n in range(2):
                    round_weights(T_J1 + 2 + n, m, 6)
                    gate(n, m, n + 1, 8)
                act.wait_ge(y_done, m + 1)
                for q in range(ROUND):
                    for j in range(L):
                        src = uT[32 * q:32 * q + 32, ds(m, 1), :].rearrange("p a (c j) -> p (a c) j", j=L)
                        ins = nc.scalar.activation(uc[32 * j:32 * j + 32, q, :], src[:, :, j], ACT.Copy)
                ins.then_inc(uc_ready, 1)
                for j in range(4, 7):
                    round_weights(T_J1 + j, m, 6)
                for n in range(2):
                    gate(n, m, n + 3, 16)
                round_weights(T_J1 + 7, m, 6)
                act.wait_ge(y_done, m + 2)
                for q in range(ROUND):
                    for i in range(L):
                        dst = yaf[32 * q:32 * q + 32, ds(m, 1), :].rearrange("p a (c j) -> p (a c) j", j=L)
                        ins = nc.scalar.activation(dst[:, :, i], bank[7][32 * i:32 * i + 32, q * NC:(q + 1) * NC],
                                                   ACT.Gelu_apprx_tanh)
                ins.then_inc(y_taken, 1)
            act.wait_ge(y_taken, ROUNDS + 1)
            act.wait_ge(j1_merge, 17)
            for c in range(KB):
                nc.scalar.activation(ya_hi[:, c, :], yaf[:, c, :], ACT.Copy).then_inc(ya_hi_s, 1)

            def gate0(g):
                act.wait_ge(j2_g, g + 1)
                half_tanh(zg[:, g % 4, :], zg[:, g % 4, :], hbias[:, g:g + 1]).then_inc(j2_th, 1)

            def round_merged(g):
                act.wait_ge(j2_m, g + 1)
                nc.scalar.activation(mg_hi[:, g, :], mf[:, g % 2, :], ACT.Copy).then_inc(j2_hi, 1)

            for n in range(2):
                round_weights(T_J2 + 2 + n)
                gate0(n)
            for t in range(2):
                round_weights(T_J2 + 4 + t)
                act.wait_ge(w_used, T_GLU + t + 1)
                for c in (2 * t, 2 * t + 1):
                    if c >= 2:
                        act.wait_ge(y2_f, c - 1)
                    half_tanh(th[:, c % 2, :], bank[Y_BANK[c]][:, :], hbias[:, 24 + c:25 + c]).then_inc(glu_th, 1)
                for c in (2 * t, 2 * t + 1):
                    act.wait_ge(y2_f, c + 1)
                    nc.scalar.activation(y2_hi[:, c, :], y2f[:, c % 2, :], ACT.Copy).then_inc(y2_hi_s, 1)
            for n in range(2):
                round_weights(T_J2 + 6 + n)
                gate0(2 + n)
            for g in (0, 2):
                round_weights(T_J2 + 8 + g // 2)
                round_merged(g)
                round_merged(g + 1)
            for n in range(4):
                round_weights(T_J2 + 10 + n)
                gate0(4 + n)
            for g in (4, 6):
                round_weights(T_WO + g // 2 - 2)
                round_merged(g)
                round_merged(g + 1)
            s = norms["f"]
            with nc.scalar.Fori(0, 2) as i:
                for c in range(4):
                    round_weights(T_WO + c + 2, i, 4)
                    act.wait_ge(s["hn"], 4 * i + (c + 1))
                    nc.scalar.activation(h_hi[:, ds(4 * i + c, 1), :], hn[:, 0:1, :], ACT.Copy).then_inc(s["hi"], 1)
                    act.wait_ge(s["sum"], 4 * i + (c if c >= 2 else 1))
                    nc.scalar.activation(sq[:, c % 2:c % 2 + 1, :], xT[:, ds(4 * i + c, 1), :], ACT.Square
                                         ).then_inc(s["sq"], 1)
            root(s, 4, T)
            with nc.scalar.Fori(0, KF // 2) as i:
                for n in range(2):
                    round_weights(T_FF + 2 + n, i, 4)
                    act.wait_ge(ff_g, 2 * i + (n + 2))
                    nc.scalar.activation(silu[:, n, :], silu[:, n, :], ACT.Silu).then_inc(ff_silu, 1)
                for n in range(2):
                    round_weights(T_FF + 4 + n, i, 4)
                    act.wait_ge(ff_act, 2 * i + (n + 1))
                    nc.scalar.activation(act_hi[:, ds(2 * i + n, 1), :], actf[:, n:n + 1, :], ACT.Copy
                                         ).then_inc(ff_hi, 1)
            with nc.scalar.Fori(0, KF // 2 - 1) as i:
                for j in range(2):
                    round_weights(T_DN + 2 + j, i, 2)
            s = norms["o"]
            for k in range(KD):
                act.wait_ge(x2_ready, k + 1)
                square(s, xT[:, k, :], k, T)
                act.wait_ge(s["sq"], k + 1)
                nc.scalar.activation(xT[:, k, :], xT[:, k, :], ACT.Copy, scale=small[:, C_GFIN + k:C_GFIN + k + 1]
                                     ).then_inc(xg_ready, 1)
                if k == KD - 1:
                    root(s, 0, T)

        @block.vector
        def _(dve):
            V = nc.vector
            steps = Steps(dve, dve_step)
            go, link = steps.go, steps.link

            def tt(out, a, b, op):
                return V.tensor_tensor(out, a, b, op)

            def add_square(s, k, width, value):
                dve.wait_ge(s["sq"], value)
                if k == 0:
                    V.tensor_copy(sqsum[:, 0:width], sq[:, 0, 0:width]).then_inc(s["sum"], 1)
                else:
                    dve.wait_ge(s["sum"], k)
                    tt(sqsum[:, 0:width], sqsum[:, 0:width], sq[:, k % 2, 0:width], ALU.add).then_inc(s["sum"], 1)

            def normalise(s, src, gain, hi, lo, width):
                dve.wait_ge(s["std"], 1)
                link(V.reciprocal(sqsum[:, 0:width], std[:, 0:width]))

                def low(k):
                    dve.wait_ge(s["hi"], k + 1)
                    tt(lo[:, k, :], hn[:, k % 2, 0:width], fv(hi[:, k, :]), ALU.subtract).then_inc(s["lo"], 1)

                for k in range(KD):
                    if k >= 2:
                        dve.wait_ge(s["lo"], k - 1)
                    V.scalar_tensor_tensor(hn[:, k % 2, 0:width], src[:, k, :], small[:, gain + k:gain + k + 1],
                                           sqsum[:, 0:width], ALU.mult, ALU.mult).then_inc(s["hn"], 1)
                    if k >= 1:
                        low(k - 1)
                low(KD - 1)
                dve.wait_ge(s["lo"], KD)

            s = norms["x"]
            dve.wait_ge(vec_loaded, 16)

            def low_x(k):
                dve.wait_ge(s["hi"], k + 1)
                tt(h_lo[:, k, :], hn[:, k % 2, :], fv(h_hi[:, k, :]), ALU.subtract).then_inc(s["lo"], 1)

            for k in range(KD):
                if k % 2 == 0:
                    dve.wait_ge(x_loaded[k // 2], 16)
                if k >= 2:
                    dve.wait_ge(s["lo"], k - 1)
                V.tensor_scalar(hn[:, k % 2, :], xT[:, k, :], small[:, C_GMIX + k:C_GMIX + k + 1], None, ALU.mult
                                ).then_inc(s["hn"], 1)
                if k >= 1:
                    low_x(k - 1)
            low_x(KD - 1)
            dve.wait_ge(s["lo"], KD)
            for k in range(KD):
                add_square(norms["x"], k, T, k + 1)
            dve.wait_ge(norms["x"]["std"], 1)
            link(V.reciprocal(rstd[:, :], std[:, :]))
            dve.wait_ge(tok_std, 1)
            V.reciprocal(trstd[:, :], tstd[:, :]).then_inc(rstd_ready, 1)

            def take_za(c):
                dve.wait_ge(w_used, T_ZA + c + 1)
                tt(uT[:, c, :], bank[c][:, :], rstd[:, :], ALU.mult).then_inc(za_taken, 1)

            take_za(0)
            for k in range(KD):
                add_square(norms["m"], k, M, k + 1)
            take_za(1)
            take_za(2)
            normalise(norms["m"], memf, C_GMEM, m_hi, m_lo, M)
            take_za(3)

            (DT, MAG, SN, CS, XR, RC, RR, TH, ARE, AIM, T0, T1, T2, FRE, FIM, M4, ER, EI, T3, T4) = (
                s5p[:, i, 0:BLOCKS] for i in range(20))
            are, aim = small[:, C_ARE:C_ARE + 16], small[:, C_AIM:C_AIM + 16]
            dve.wait_ge(small_loaded, 16)
            go(V.memset(s5p[:, 8:10, BLOCKS:PADDED], 0.0))
            dve.wait_ge(dt_ready, 1)
            go(tt(XR, are, DT, ALU.mult))
            link(tt(TH, aim, DT, ALU.mult))
            link(V.tensor_scalar(T0, TH, 1.0 / TWO_PI, ROUNDER, ALU.mult, ALU.add))
            link(V.tensor_scalar(T1, T0, ROUNDER, None, ALU.subtract))
            link(V.scalar_tensor_tensor(T0, T1, -PI_HI, TH, ALU.mult, ALU.add))
            link(V.scalar_tensor_tensor(T2, T1, -PI_MID, T0, ALU.mult, ALU.add))
            link(V.scalar_tensor_tensor(T0, T1, -PI_LO, T2, ALU.mult, ALU.add))
            link(V.tensor_scalar(RR, T0, SIN_MAX, -SIN_MAX, ALU.min, ALU.max))
            link(V.tensor_scalar(T1, RR, -1.0, None, ALU.mult))
            link(tt(T2, T1, RR, ALU.max))
            V.tensor_scalar(RC, T2, -1.0, HALF_PI, ALU.mult, ALU.add).then_inc(ang_ready, 1)
            dve.wait_ge(trig_ready, 1)
            go(tt(ARE, MAG, CS, ALU.mult))
            go(tt(AIM, MAG, SN, ALU.mult))
            go(tt(T0, are, are, ALU.mult))
            go(tt(T1, aim, aim, ALU.mult))
            steps.wait()
            go(V.tensor_scalar(T2, ARE, -1.0, None, ALU.add))
            link(tt(T3, T0, T1, ALU.add))
            link(V.reciprocal(T4, T3))
            go(tt(T0, T2, are, ALU.mult))
            go(tt(T1, AIM, aim, ALU.mult))
            steps.wait()
            link(tt(T3, T0, T1, ALU.add))
            link(tt(FRE, T3, T4, ALU.mult))
            go(tt(T0, AIM, are, ALU.mult))
            go(tt(T1, T2, aim, ALU.mult))
            steps.wait()
            link(tt(T3, T0, T1, ALU.subtract))
            link(tt(FIM, T3, T4, ALU.mult))
            def wide(v, n):
                return v.unsqueeze(2).to_broadcast([P, BLOCKS, n])

            bre = small[:, C_BRE:C_BRE + 256].rearrange("p (b h) -> p b h", h=16)
            bim = small[:, C_BIM:C_BIM + 256].rearrange("p (b h) -> p b h", h=16)
            go(tt(bb_tmp[:, 0, :, :], bre, wide(FRE, 16), ALU.mult))
            go(tt(bb_tmp[:, 1, :, :], bim, wide(FIM, 16), ALU.mult))
            go(tt(bb_tmp[:, 2, :, :], bim, wide(FRE, 16), ALU.mult))
            go(tt(bb_tmp[:, 3, :, :], bre, wide(FIM, 16), ALU.mult))
            steps.wait()
            go(tt(bre, bb_tmp[:, 0, :, :], bb_tmp[:, 1, :, :], ALU.subtract))
            go(tt(bim, bb_tmp[:, 2, :, :], bb_tmp[:, 3, :, :], ALU.add))
            cim = small[:, C_CIM:C_CIM + 256]
            link(V.tensor_scalar(cim, cim, -1.0, None, ALU.mult))
            link(tt(T0, MAG, MAG, ALU.mult))
            link(tt(M4, T0, T0, ALU.mult))

            def turn_squared(re, im, rs, is_):
                go(tt(T0, rs, rs, ALU.mult))
                go(tt(T1, is_, is_, ALU.mult))
                go(V.scalar_tensor_tensor(T2, rs, 2.0, is_, ALU.mult, ALU.mult))
                steps.wait()
                go(tt(re, T0, T1, ALU.subtract))
                link(V.tensor_copy(im, T2))

            turn_squared(ER, EI, CS, SN)
            turn_squared(ER, EI, ER, EI)
            go(V.memset(cosT[:, :, 0:1], 1.0))
            link(V.memset(sinT[:, :, 0:1], 0.0))
            n = 1
            while n < NC:
                q = [tab_tmp[:, j, :, 0:n] for j in range(4)]
                go(tt(q[0], cosT[:, :, 0:n], wide(ER, n), ALU.mult))
                go(tt(q[1], sinT[:, :, 0:n], wide(EI, n), ALU.mult))
                go(tt(q[2], sinT[:, :, 0:n], wide(ER, n), ALU.mult))
                go(tt(q[3], cosT[:, :, 0:n], wide(EI, n), ALU.mult))
                steps.wait()
                go(tt(cosT[:, :, n:2 * n], q[0], q[1], ALU.subtract))
                link(tt(sinT[:, :, n:2 * n], q[2], q[3], ALU.add))
                n *= 2
                if n < NC:
                    turn_squared(ER, EI, ER, EI)

            for c in range(4):
                dve.wait_ge(zv_taken, c + 1)
                link(V.bn_stats(stats[:, c, :], vtok[:, c, :]))
                V.bn_aggr(mv[:, c, :], stats[:, c, :]).then_inc(var_ready, 1)
            dve.wait_ge(vstd_ready, 1)
            link(V.reciprocal(vrs[:, :], vstd[:, :]))
            dve.wait_ge(sgu_loaded, 16)
            for c in range(4):
                link(V.tensor_scalar(vtok[:, c, :], vtok[:, c, :], mv[:, c, 0:1], vrs[:, c:c + 1],
                                     ALU.subtract, ALU.mult))
                link(tt(vtok[:, c, :], vtok[:, c, :], sgu[:, 0, :], ALU.mult))
                tt(vtok[:, c, :], vtok[:, c, :], sgu[:, 1, :], ALU.add).then_inc(vln_ready, 1)
            for c in range(HEADS):
                dve.wait_ge(w_used, T_QK + 2 * c + 1)
                tt(qT[:, c, :], bank[c][:, :], rstd[:, :], ALU.mult).then_inc(zq_taken, 1)
                dve.wait_ge(w_used, T_QK + 2 * c + 2)
                V.tensor_copy(kT[:, c, :], bank[4 + c][:, 0:M]).then_inc(k_taken, 1)

            def head_max(h):
                for half in range(2):
                    i = 4 * h + 2 * half
                    dve.wait_ge(sc_done, 2 * h + half + 1)
                    b = SCORE_BANK[h] + half
                    link(V.tensor_reduce(smx[:, i:i + 2], bank[b][:, :].rearrange("p (a m) -> p a m", m=M),
                                         AX, ALU.max))
                    V.tensor_scalar(snm[:, i:i + 2], smx[:, i:i + 2], -SCALE, None, ALU.mult
                                    ).then_inc(mx_ready, 1)

            def head_scale(h):
                dve.wait_ge(exp_done, 4 * h + 4)
                link(V.reciprocal(srec[:, 4 * h:4 * h + 4], ssum[:, 4 * h:4 * h + 4]))
                for t4 in range(4):
                    i = 4 * h + t4
                    V.tensor_scalar(prob[:, i % 8, :], prob[:, i % 8, :], srec[:, i:i + 1], None, ALU.mult
                                    ).then_inc(p_ready, 1)

            def take_pt(h):
                dve.wait_ge(pt_done, h + 1)
                if h >= 2:
                    dve.wait_ge(pv_done, h - 1)
                V.tensor_copy(pT[:, h % 2, 1, :], bank[PT_BANK[h] + 1][:, :]).then_inc(pt_dve, 1)

            def low_o(h):
                dve.wait_ge(o_hi_s, h + 1)
                tt(o_loT[:, h, :], bank[4 + h % 2][:, :], fv(o_hiT[:, h, :]), ALU.subtract).then_inc(o_lo_s, 1)

            def scale_u(c):
                dve.wait_ge(w_used, T_VU + 2 * c + 2)
                tt(ug[:, c, :], bank[6 + c % 2][:, :], rstd[:, :], ALU.mult).then_inc(zu_scaled, 1)

            def gated(g):
                dve.wait_ge(sgu_done, g + 1)
                b = SGU_BANK[g]
                bias = sgu[:, 2, g * P:(g + 1) * P].unsqueeze(1).to_broadcast([P, 4, P])
                tt(prod[:, :].rearrange("p (b t) -> p b t", b=4), bank[b][:, :].rearrange("p (b t) -> p b t", b=4),
                   bias, ALU.add).then_inc(sgu_taken, 1)
                dve.wait_ge(sgu_taken, g + 1)
                dve.wait_ge(zu_ready, g + 1)
                tt(ug[:, g, :], prod[:, :], ug[:, g, :], ALU.mult).then_inc(yb_f, 1)
                dve.wait_ge(yb_f, g + 1)

            def low_yb(g):
                dve.wait_ge(yb_hi_s, g + 1)
                tt(yb_lo[:, g, :], ug[:, g, :], fv(yb_hi[:, g, :]), ALU.subtract).then_inc(yb_lo_s, 1)

            head_max(0)
            head_max(1)
            head_scale(0)
            head_scale(1)
            scale_u(0)
            take_pt(0)
            head_max(2)
            scale_u(1)
            head_scale(2)
            scale_u(2)
            take_pt(1)
            head_max(3)
            dve.wait_ge(w_used, T_VU + 7)
            for c in range(2):
                V.tensor_copy(vM[:, c, :], bank[4 + c][:, :]).then_inc(v_taken, 1)
            scale_u(3)
            head_scale(3)
            take_pt(2)
            low_o(0)
            take_pt(3)
            low_o(1)
            for g in range(4):
                gated(g)
            for g in range(4):
                low_yb(g)
            low_o(2)
            low_o(3)
            dve.wait_ge(yb_lo_s, 4)
            dve.wait_ge(pv_done, 4)
            for i in range(2):
                go(V.memset(ba[i][:, :, L - 1, :], 0.0))
                go(V.memset(ca[i][:, :, 0, :], 0.0))
                go(V.memset(st[i][:, :, 0:1], 0.0))
            go(V.memset(toep[:, :, :], 0.0))
            steps.wait()

            def b_powers(b0):
                for i, cb in enumerate((C_BRE, C_BIM)):
                    for g in range(2):
                        pr = slice(64 * g, 64 * g + 64)
                        src = small[pr, cb:cb + 16 * PADDED].rearrange("p (b h) -> p b h", h=16)[:, ds(b0, 4), :]
                        go(V.tensor_copy(ba[i][pr, :, L - 1, 16 * g:16 * g + 16], src))
                steps.wait()
                dre, dim, q = decay_of(b0)
                for j in range(L - 2, -1, -1):
                    go(tt(q[0], ba[0][:, :, j + 1, :], dre, ALU.mult))
                    go(tt(q[1], ba[1][:, :, j + 1, :], dim, ALU.mult))
                    go(tt(q[2], ba[1][:, :, j + 1, :], dre, ALU.mult))
                    go(tt(q[3], ba[0][:, :, j + 1, :], dim, ALU.mult))
                    steps.wait()
                    go(tt(ba[0][:, :, j, :], q[0], q[1], ALU.subtract))
                    link(tt(ba[1][:, :, j, :], q[2], q[3], ALU.add))

            def decay_of(b0):
                return (*(s5p[:, i, :][:, ds(b0, 4)].unsqueeze(2).to_broadcast([P, ROUND, CH]) for i in (8, 9)),
                        [rot[j][:, :, 0:CH] for j in range(4)])

            b_powers(0)
            before(dve, j1_g, j1_merge, s5_const)

            def blk(v, m):
                return v[:, ds(4 * m, 4)]

            with nc.vector.Fori(0, ROUNDS) as m:
                steps.enter(m, 75)
                dve.wait_ge(y_done, m + 1)
                for i, cc in enumerate((C_CRE, C_CIM)):
                    for g in range(2):
                        pr = slice(64 * g, 64 * g + 64)
                        src = small[pr, cc:cc + 256].rearrange("p (b h) -> p b h", h=16)[:, ds(4 * m, 4), :]
                        go(V.tensor_copy(ca[i][pr, :, 0, 16 * g:16 * g + 16], src))
                steps.wait()
                dre, dim, q = decay_of(4 * m)
                for j in range(1, L + 1):
                    go(tt(q[0], ca[0][:, :, j - 1, :], dre, ALU.mult))
                    go(tt(q[1], ca[1][:, :, j - 1, :], dim, ALU.mult))
                    go(tt(q[2], ca[1][:, :, j - 1, :], dre, ALU.mult))
                    go(tt(q[3], ca[0][:, :, j - 1, :], dim, ALU.mult))
                    steps.wait()
                    go(tt(ca[0][:, :, j, :], q[0], q[1], ALU.add))
                    ins = tt(ca[1][:, :, j, :], q[2], q[3], ALU.subtract)
                    if j < L:
                        link(ins)
                    else:
                        ins.then_inc(bc_ready, 1)

                def scale_gate(n, idx):
                    dve.wait_ge(w_used, 6 * m + (T_J1 + (0, 1, 3, 4)[idx] + 1))
                    dve.wait_ge(j1_merge, 4 * m + (1 if idx < 2 else idx))
                    tt(th[:, n, :], bank[n][:, :], rstd[:, :], ALU.mult).then_inc(j1_g, 1)

                scale_gate(0, 0)
                scale_gate(1, 1)
                dve.wait_ge(gt_done, m + 1)
                go(V.tensor_copy(flat(gt[0][:, :, :]), bank[4][:, :]))
                go(V.tensor_copy(flat(gt[1][:, :, :]), bank[5][:, :]))
                resp = bank[6][0:CH, :].rearrange("p (b c) -> p b c", b=ROUND)
                go(V.tensor_copy(toep[0:CH, :, CH:P], resp[:, :, CH:P]))
                skip = small[0:CH, C_D:C_D + 16][:, ds(4 * m, 4)].unsqueeze(2).to_broadcast([CH, ROUND, CH])
                diag = rot[0][0:CH, :, 0:CH]
                link(tt(diag, ident[0:CH, 0:CH].unsqueeze(1).to_broadcast([CH, ROUND, CH]), skip, ALU.mult))
                link(tt(toep[0:CH, :, 0:CH], resp[:, :, 0:CH], diag, ALU.add))
                for j in range(1, L):
                    ins = V.tensor_copy(toep[CH * j:CH * j + CH, :, CH * j:P], toep[0:CH, :, 0:P - CH * j])
                ins.then_inc(gt_ready, 1)

                def merge(first, n):
                    val = 4 * m + ((0 if first else 2) + n + 1)
                    dve.wait_ge(w_used, 6 * m + (T_J1 + (3 if first else 6)))
                    dve.wait_ge(j1_th, val)
                    dst = mgf[:, ds(2 * m + n, 1), :].rearrange("p a t -> p (a t)")
                    if first:
                        V.scalar_tensor_tensor(dst, th[:, n, :], 1.0, bank[2 + n][:, :], ALU.add, ALU.mult
                                               ).then_inc(j1_merge, 1)
                    else:
                        V.scalar_tensor_tensor(prod[:, :], th[:, n, :], 1.0, bank[2 + n][:, :], ALU.add,
                                               ALU.mult).then_inc(j1_merge, 1)
                        dve.wait_ge(j1_merge, val + 1)
                        link(tt(dst, dst, prod[:, :], ALU.add))

                merge(True, 0)
                merge(True, 1)
                dve.wait_ge(vin_done, m + 1)
                vre = bank[4][:, :].rearrange("p (b c) -> p b c", b=ROUND)
                vim = bank[5][:, :].rearrange("p (b c) -> p b c", b=ROUND)
                cos, sin = cosT[:, ds(4 * m, 4), :], sinT[:, ds(4 * m, 4), :]
                go(tt(rot[0][:, :, :], vre, cos, ALU.mult))
                go(tt(rot[1][:, :, :], vim, sin, ALU.mult))
                go(tt(rot[2][:, :, :], vim, cos, ALU.mult))
                go(tt(rot[3][:, :, :], vre, sin, ALU.mult))
                steps.wait()
                go(tt(rot[0][:, :, :], rot[0][:, :, :], rot[1][:, :, :], ALU.add))
                link(tt(rot[2][:, :, :], rot[2][:, :, :], rot[3][:, :, :], ALU.subtract))
                for b in range(ROUND):
                    decay = s5p[:, 15, :][:, ds(4 * m + b, 1)].to_broadcast([P, NC])
                    go(V.tensor_tensor_scan(rot[1][:, b, :], decay, rot[0][:, b, :], 0.0, ALU.mult, ALU.add))
                    go(V.tensor_tensor_scan(rot[3][:, b, :], decay, rot[2][:, b, :], 0.0, ALU.mult, ALU.add))
                steps.wait()
                rre, rim = rot[1][:, :, 0:NC - 1], rot[3][:, :, 0:NC - 1]
                cos, sin = cosT[:, ds(4 * m, 4), 0:NC - 1], sinT[:, ds(4 * m, 4), 0:NC - 1]
                q0, q2 = rot[0][:, :, 0:NC - 1], rot[2][:, :, 0:NC - 1]
                go(tt(q0, rre, cos, ALU.mult))
                go(tt(q2, rim, sin, ALU.mult))
                steps.wait()
                link(tt(st[0][:, :, 1:NC], q0, q2, ALU.subtract))
                go(tt(q0, rre, sin, ALU.mult))
                go(tt(q2, rim, cos, ALU.mult))
                steps.wait()
                tt(st[1][:, :, 1:NC], q0, q2, ALU.add).then_inc(st_ready, 1)
                scale_gate(0, 2)
                scale_gate(1, 3)
                dve.wait_ge(st_ready, m + 1)
                b_powers(4 * m + 4)
                merge(False, 0)
                merge(False, 1)
                dve.wait_ge(gt_ready, m + 1)
                dve.wait_ge(bc_ready, m + 1)
            steps.leave(ROUNDS)
            def scale_gate0(g):
                dve.wait_ge(w_used, J2_TILE[g] + 1)
                if g >= 4:
                    dve.wait_ge(j2_prod, g - 3)
                tt(zg[:, g % 4, :], bank[G_BANK[g % 4]][:, :], rstd[:, :], ALU.mult).then_inc(j2_g, 1)

            def merge0(g):
                dve.wait_ge(w_used, J2_OUT[g // 2] + 1)
                dve.wait_ge(j2_th, g + 1)
                if g:
                    dve.wait_ge(j2_m, g)
                V.scalar_tensor_tensor(prod[:, :], zg[:, g % 4, :], 1.0, bank[Y_BANK[g % 4]][:, :],
                                       ALU.add, ALU.mult).then_inc(j2_prod, 1)
                dve.wait_ge(j2_prod, g + 1)
                if g >= 2:
                    dve.wait_ge(j2_lo, g - 1)
                V.scalar_tensor_tensor(mf[:, g % 2, :], prod[:, :], 0.5, mgf[:, g, :], ALU.mult, ALU.add
                                       ).then_inc(j2_m, 1)

            def low_merged(g):
                dve.wait_ge(j2_hi, g + 1)
                tt(mg_lo[:, g, :], mf[:, g % 2, :], fv(mg_hi[:, g, :]), ALU.subtract).then_inc(j2_lo, 1)

            scale_gate0(0)
            for c in range(KB):
                dve.wait_ge(ya_hi_s, c + 1)
                tt(ya_lo[:, c, :], yaf[:, c, :], fv(ya_hi[:, c, :]), ALU.subtract).then_inc(ya_lo_s, 1)
            scale_gate0(1)
            for t in range(2):
                for c in (2 * t, 2 * t + 1):
                    dve.wait_ge(glu_th, c + 1)
                    if c >= 2:
                        dve.wait_ge(y2_lo_s, c - 1)
                    V.scalar_tensor_tensor(y2f[:, c % 2, :], th[:, c % 2, :], 1.0, yaf[:, c, :], ALU.add, ALU.mult
                                           ).then_inc(y2_f, 1)
                for c in (2 * t, 2 * t + 1):
                    dve.wait_ge(y2_hi_s, c + 1)
                    tt(y2_lo[:, c, :], y2f[:, c % 2, :], fv(y2_hi[:, c, :]), ALU.subtract).then_inc(y2_lo_s, 1)
            dve.wait_ge(y2_lo_s, KB)
            for h4 in (0, 4):
                for g in range(2 if h4 == 0 else 0, 4):
                    scale_gate0(h4 + g)
                for g in (h4, h4 + 2):
                    merge0(g)
                    merge0(g + 1)
                    low_merged(g)
                    low_merged(g + 1)
            s = norms["f"]
            dve.wait_ge(j2_lo, KD)
            V.memset(sqsum[:, :], 0.0).then_inc(s["sum"], 1)
            before(dve, x1_ready)
            with nc.vector.Fori(0, 2) as i:
                for c in range(4):
                    dve.wait_ge(w_used, 4 * i + (T_WO + c + 1))
                    xi = xT[:, ds(4 * i + c, 1), :].rearrange("p a t -> p (a t)")
                    V.scalar_tensor_tensor(xi, bank[c][:, :], 0.5, xi, ALU.mult, ALU.add).then_inc(x1_ready, 1)
                    dve.wait_ge(x1_ready, 4 * i + (c + 2))
                    V.tensor_scalar(hn[:, 0, :], xi, small[:, ds(4 * i + (C_GFFN + c), 1)], None, ALU.mult
                                    ).then_inc(s["hn"], 1)
                    dve.wait_ge(s["hi"], 4 * i + (c + 1))
                    tt(h_lo[:, ds(4 * i + c, 1), :], hn[:, 0:1, :], fv(h_hi[:, ds(4 * i + c, 1), :]), ALU.subtract
                       ).then_inc(s["lo"], 1)
                    dve.wait_ge(s["sq"], 4 * i + (c + 1))
                    dve.wait_ge(s["sum"], 4 * i + (c + 1))
                    tt(sqsum[:, :], sqsum[:, :], sq[:, c % 2, :], ALU.add).then_inc(s["sum"], 1)
                    dve.wait_ge(s["lo"], 4 * i + (c + 1))
            dve.wait_ge(s["std"], 1)
            V.reciprocal(rstd[:, :], std[:, :]).then_inc(rstd_ready, 1)
            before(dve, ff_g, ff_u, ff_lo)
            with nc.vector.Fori(0, KF // 2) as i:
                for n in range(2):
                    dve.wait_ge(w_used, 4 * i + (T_FF + n + 1))
                    dve.wait_ge(ff_lo, 2 * i + 1)
                    tt(silu[:, n, :], bank[n][:, :], rstd[:, :], ALU.mult).then_inc(ff_g, 1)
                for n in range(2):
                    dve.wait_ge(w_used, 4 * i + (T_FF + n + 3))
                    tt(actf[:, n, :], bank[2 + n][:, :], rstd[:, :], ALU.mult).then_inc(ff_u, 1)
                    dve.wait_ge(ff_u, 2 * i + (n + 2))
                    dve.wait_ge(ff_silu, 2 * i + (n + 1))
                    tt(actf[:, n, :], actf[:, n, :], silu[:, n, :], ALU.mult).then_inc(ff_act, 1)
                for n in range(2):
                    dve.wait_ge(ff_hi, 2 * i + (n + 1))
                    tt(act_lo[:, ds(2 * i + n, 1), :], actf[:, n:n + 1, :], fv(act_hi[:, ds(2 * i + n, 1), :]),
                       ALU.subtract).then_inc(ff_lo, 1)
            s = norms["o"]
            for k in range(KD):
                dve.wait_ge(dn_done, k + 1)
                tt(xT[:, k, :], bank[k][:, :], xT[:, k, :], ALU.add).then_inc(x2_ready, 1)
                if k:
                    add_square(s, k - 1, T, k)
            add_square(s, KD - 1, T, KD)
            dve.wait_ge(s["std"], 1)
            V.reciprocal(rstd[:, :], std[:, :]).then_inc(rstd_ready, 1)
            dve.wait_ge(rstd_ready, 3)
            for k in range(KD - POOL_OUT):
                dve.wait_ge(xg_ready, k + 1)
                tt(xT[:, k, :], xT[:, k, :], rstd[:, :], ALU.mult).then_inc(out_dve, 1)

        @block.tensor
        def _(pe):
            mm = nc.tensor.matmul

            def product(out, a, b, first, last):
                mm(out, a[0], b[0], start=first, stop=False)
                mm(out, a[0], b[1], start=False, stop=False)
                return mm(out, a[1], b[0], start=False, stop=last)

            def weight(slot, k, c0, n, width):
                lo = k * width + c0
                return w_hi[:, slot % NS, lo:lo + n], w_lo[:, slot % NS, lo:lo + n]

            def pair(hi, lo, k):
                return hi[:, k, :], lo[:, k, :]

            def column_tile(out, slot, x, kn, c0=0, width=P):
                for k in range(kn):
                    ins = product(out, weight(slot, k, c0, P, width), x(k), k == 0, k == kn - 1)
                return ins

            def tile_ready(t):
                pe.wait_ge(w_ready, t + 1)

            def h(k):
                return pair(h_hi, h_lo, k)

            def square_sum(s, b, width, count):
                pe.wait_ge(s["sum"], count)
                mm(bank[b][:, 0:width], ones[:, :], sqsum[:, 0:width], start=True, stop=True).then_inc(s["ssq"], 1)

            for c in range(KB):
                tile_ready(T_ZA + c)
                for k in range(KD):
                    if c == 0:
                        pe.wait_ge(norms["x"]["lo"], k + 1)
                    ins = product(bank[c][:, :], weight(c, k, 0, P, P), h(k), k == 0, k == KD - 1)
                ins.then_inc(w_used, 1)
                if c == 0:
                    pe.wait_ge(consts, 1)
                    square_sum(norms["x"], 7, T, KD)
                    for t in range(4):
                        ins = mm(bank[6][:, t:t + 1], sqsum[:, t * P:(t + 1) * P], ones[:, 0:1], start=True, stop=True)
                    ins.then_inc(tok_ssq, 1)
                if c == 2:
                    pe.wait_ge(tok_std, 1)
                    square_sum(norms["m"], 6, M, KD)
            for t in range(4):
                tile_ready(T_ZV + t)
                for c in range(4):
                    if t == 0 and c == 2:
                        pe.wait_ge(norms["m"]["std"], 1)
                    for j in range(2):
                        k = 2 * t + j
                        ins = product(bank[4 + c][:, :], [x[:, c * P:(c + 1) * P] for x in h(k)],
                                      weight(t, j, 0, WB, WB), k == 0, k == KD - 1)
                ins.then_inc(w_used, 1)
            for c in range(KB):
                tile_ready(T_QK + 2 * c)
                pe.wait_ge(za_taken, c + 1)
                column_tile(bank[c][:, :], 0, h, KD).then_inc(w_used, 1)
                tile_ready(T_QK + 2 * c + 1)
                pe.wait_ge(norms["m"]["lo"], KD)
                pe.wait_ge(zv_taken, c + 1)
                column_tile(bank[4 + c][:, 0:M], 1, lambda k: pair(m_hi, m_lo, k), KD).then_inc(w_used, 1)

            def scores(head):
                for half in range(2):
                    b = SCORE_BANK[head] + half
                    for j in range(2):
                        t0 = (2 * half + j) * P
                        ins = mm(bank[b][:, j * M:(j + 1) * M], qT[:, head, t0:t0 + P], kT[:, head, :],
                                 start=True, stop=True)
                    ins.then_inc(sc_done, 1)

            def transposes(head):
                pe.wait_ge(p_ready, 4 * head + 4)
                for half in range(2):
                    b = PT_BANK[head] + half
                    for t in range(4):
                        ins = nc.tensor.transpose(bank[b][:, t * P:(t + 1) * P],
                                                  prob[:, (4 * head + t) % 8, half * P:(half + 1) * P], ident)
                ins.then_inc(pt_done, 1)

            def values(head):
                pe.wait_ge(pt_act, head + 1)
                pe.wait_ge(pt_dve, head + 1)
                for half in range(2):
                    ins = mm(bank[4 + head % 2][:, :], vM[:, half, head * P:(head + 1) * P], pT[:, head % 2, half, :],
                             start=half == 0, stop=half == 1)
                ins.then_inc(pv_done, 1)

            def value_weights(t):
                tile_ready(T_VU + 2 * t)
                for c in range(2):
                    for j in range(2):
                        k = 2 * t + j
                        ins = product(bank[4 + c][:, :], [x[:, c * P:(c + 1) * P] for x in pair(m_hi, m_lo, k)],
                                      weight(0, j, 0, WB, WB), k == 0, k == KD - 1)
                ins.then_inc(w_used, 1)

            def zu(c):
                tile_ready(T_VU + 2 * c + 1)
                if c >= 2:
                    pe.wait_ge(zu_scaled, c - 1)
                column_tile(bank[6 + c % 2][:, :], 1, h, KD).then_inc(w_used, 1)

            pe.wait_ge(k_taken, HEADS)
            pe.wait_ge(zq_taken, KB)
            scores(0)
            scores(1)
            value_weights(0)
            zu(0)
            value_weights(1)
            transposes_free = exp_done
            pe.wait_ge(transposes_free, 8)
            transposes(0)
            scores(2)
            zu(1)
            value_weights(2)
            zu(2)
            pe.wait_ge(pt_act, 1)
            pe.wait_ge(pt_dve, 1)
            transposes(1)
            pe.wait_ge(exp_done, 12)
            scores(3)
            value_weights(3)
            zu(3)
            pe.wait_ge(v_taken, 2)
            values(0)
            pe.wait_ge(exp_done, 16)
            transposes(2)
            values(1)
            transposes(3)
            pe.wait_ge(vln_ready, 4)
            pe.wait_ge(wst_masked, 1)
            for g in range(4):
                if g < 2:
                    pe.wait_ge(zu_scaled, 3 + g)
                else:
                    pe.wait_ge(pt_act, 3)
                    pe.wait_ge(pt_dve, 3)
                for b in range(4):
                    ins = mm(bank[SGU_BANK[g]][:, b * P:(b + 1) * P], vtok[:, b, g * P:(g + 1) * P],
                             sgu[:, 3, g * P:(g + 1) * P], start=True, stop=True)
                ins.then_inc(sgu_done, 1)
            pe.wait_ge(o_lo_s, 1)
            values(2)
            pe.wait_ge(o_lo_s, 2)
            values(3)

            pe.wait_ge(sgu_taken, 4)
            pe.wait_ge(pt_act, 4)
            before(pe, y_done)
            with nc.tensor.Fori(0, ROUNDS) as m:
                def gates(j0, b0, free):
                    for n in range(2):
                        pe.wait_ge(w_ready, 6 * m + (T_J1 + j0 + n + 1))
                        pe.wait_ge(j1_g, 4 * m + free[n])
                        column_tile(bank[b0 + n][:, :], j0 + n, h, KD).then_inc(w_used, 1)

                def outs(j0, hi, lo, ready, free):
                    pe.wait_ge(w_ready, 6 * m + (T_J1 + j0 + 1))
                    for n in range(2):
                        pe.wait_ge(j1_merge, 4 * m + free[n])
                        pe.wait_ge(ready, HEADS)
                        ins = column_tile(bank[2 + n][:, :], j0, lambda k: pair(hi, lo, k), KB, n * P, 2 * P)
                    ins.then_inc(w_used, 1)

                gates(0, 0, (1, 1))
                pe.wait_ge(bc_ready, m + 1)
                for i in range(2):
                    for q in range(ROUND):
                        nc.tensor.transpose(bank[4 + i][:, q * P:(q + 1) * P],
                                            ba[i][:, q, :, :].rearrange("p a b -> p (a b)"), ident)
                for q in range(ROUND):
                    for i in range(2):
                        ins = mm(bank[6][0:CH, q * P:(q + 1) * P], ba[i][:, q, L - 1, :],
                                 ca[i][:, q, 0:L, :].rearrange("p a b -> p (a b)"), start=i == 0, stop=i == 1)
                ins.then_inc(gt_done, 1)
                outs(2, yb_hi, yb_lo, yb_lo_s, (1, 1))
                pe.wait_ge(gt_ready, m + 1)
                pe.wait_ge(uc_ready, m + 1)
                for i in range(2):
                    for q in range(ROUND):
                        ins = mm(bank[4 + i][:, q * P:(q + 1) * P], gt[i][:, q, :], uc[:, q, :], start=True, stop=True)
                ins.then_inc(vin_done, 1)
                gates(3, 0, (2, 3))
                outs(5, o_hiT, o_loT, o_lo_s, (2, 3))
                pe.wait_ge(st_ready, m + 1)
                pe.wait_ge(y_taken, m + 1)
                for q in range(ROUND):
                    o = bank[7][:, q * P:(q + 1) * P]
                    mm(o, toep[:, q, :], uc[:, q, :], start=True, stop=False)
                    mm(o, ca[0][:, q, 1:L + 1, :].rearrange("p a b -> p (a b)"), st[0][:, q, :], start=False, stop=False)
                    ins = mm(o, ca[1][:, q, 1:L + 1, :].rearrange("p a b -> p (a b)"), st[1][:, q, :],
                             start=False, stop=True)
                ins.then_inc(y_done, 1)
            def gate0(g):
                tile_ready(J2_TILE[g])
                if g >= 4:
                    pe.wait_ge(j2_g, g - 3)
                column_tile(bank[G_BANK[g % 4]][:, :], J2_TILE[g] % NS, h, KD).then_inc(w_used, 1)

            pe.wait_ge(j1_g, 17)
            gate0(0)
            gate0(1)
            pe.wait_ge(ya_lo_s, KB)
            pe.wait_ge(j1_merge, 17)
            for t in range(2):
                tile_ready(T_GLU + t)
                for n in range(2):
                    ins = column_tile(bank[Y_BANK[2 * t + n]][:, :], t, lambda k: pair(ya_hi, ya_lo, k), KB,
                                      n * P, 2 * P)
                ins.then_inc(w_used, 1)
            for h4 in (0, 4):
                for g in range(2 if h4 == 0 else 0, 4):
                    gate0(h4 + g)
                for q in range(2):
                    t = J2_OUT[h4 // 2 + q]
                    tile_ready(t)
                    pe.wait_ge(y2_lo_s, KB)
                    for n in range(2):
                        if h4:
                            pe.wait_ge(j2_prod, 2 * q + n + 1)
                        ins = column_tile(bank[Y_BANK[2 * q + n]][:, :], t % NS, lambda k: pair(y2_hi, y2_lo, k), KB,
                                          n * P, 2 * P)
                    ins.then_inc(w_used, 1)
            with nc.tensor.Fori(0, 2) as i:
                pe.wait_ge(x1_ready, 4 * i + 1)
                pe.wait_ge(j2_lo, KD)
                for c in range(4):
                    pe.wait_ge(w_ready, 4 * i + (T_WO + c + 1))
                    column_tile(bank[c][:, :], c, lambda k: pair(mg_hi, mg_lo, k), KD).then_inc(w_used, 1)

            def feed(i, g, free):
                for n in range(2):
                    pe.wait_ge(free, 2 * i + 1)
                    pe.wait_ge(w_ready, 4 * i + (T_FF + 2 * g + n + 1))
                    column_tile(bank[2 * g + n][:, :], n, h, KD).then_inc(w_used, 1)

            for n in range(2):
                tile_ready(T_FF + n)
                for k in range(KD):
                    pe.wait_ge(norms["f"]["lo"], k + 1)
                    ins = product(bank[n][:, :], weight(n, k, 0, P, P), h(k), k == 0, k == KD - 1)
                ins.then_inc(w_used, 1)
            square_sum(norms["f"], 4, T, KD + 1)
            feed(0, 1, ff_u)
            with nc.tensor.Fori(1, KF // 2) as i:
                feed(i, 0, ff_g)
                feed(i, 1, ff_u)
            pe.wait_ge(ff_g, KF + 1)
            pe.wait_ge(ff_u, KF + 1)
            pe.wait_ge(ff_lo, KF - 1)

            def down(slot, n, x, first, last):
                return product(bank[n][:, :], weight(slot, 0, n * P, P, 0), x, first, last)

            for k in range(2):
                tile_ready(T_DN + k)
                for n in range(KD):
                    ins = down(k, n, pair(act_hi, act_lo, k), k == 0, False)
                ins.then_inc(w_used, 1)
            with nc.tensor.Fori(1, KF // 2 - 1) as i:
                for j in range(2):
                    pe.wait_ge(w_ready, 2 * i + (T_DN + j + 1))
                    x = [a[:, ds(2 * i + j, 1), :].rearrange("p a t -> p (a t)") for a in (act_hi, act_lo)]
                    for n in range(KD):
                        ins = down(j, n, x, False, False)
                    ins.then_inc(w_used, 1)
            pe.wait_ge(ff_lo, KF + 1)
            tile_ready(T_DN + KF - 1)
            for n in range(KD):
                for k in (KF - 2, KF - 1):
                    ins = down(k % NS, n, pair(act_hi, act_lo, k), False, k == KF - 1)
                ins.then_inc(dn_done, 1)
            square_sum(norms["o"], 0, T, KD)


def _stream(w_in, w_kv, w_glu, w_a, w_b, w_c, w_out, w_gate, w_up, w_down):
    tiles = []

    def columns(w, c, n=1):
        part = w[:, c * P:(c + n) * P].reshape(-1, P, n * P)
        tiles.append(part.transpose(1, 0, 2).reshape(P, TILE))

    def rows(w, k, n=1):
        tiles.append(w[k * P:(k + n) * P].reshape(n, P, -1).transpose(1, 0, 2).reshape(P, TILE))

    za, zu, zv, zq, gates = np.split(w_in, [WB, 2 * WB, 3 * WB, 4 * WB], axis=1)
    for c in range(KB):
        columns(za, c)
    for k in range(0, KD, 2):
        rows(zv, k, 2)
    for c in range(KB):
        columns(zq, c)
        columns(w_kv[:, :WB], c)
    for c in range(KB):
        rows(w_kv[:, WB:], 2 * c, 2)
        columns(zu, c)
    for m in range(4):
        for g, w in ((1, w_b), (2, w_c)):
            for n in range(2):
                columns(gates, g * KD + 2 * m + n)
            columns(w, 2 * m, 2)
    for h4 in (0, 4):
        for c in range(4):
            columns(gates, h4 + c)
            if h4 == 0 and c == 1:
                columns(w_glu, 0, 2)
                columns(w_glu, 2, 2)
        for c in (0, 2):
            columns(w_a, h4 + c, 2)
    for c in range(KD):
        columns(w_out, c)
    for f in range(0, KF, 2):
        for w in (w_gate, w_up):
            for n in range(2):
                columns(w, f + n)
    for k in range(KF):
        rows(w_down, k)
    assert len(tiles) == TILES
    return np.stack(tiles)


def kernel(**inputs):
    import concourse.bacc as bacc
    from concourse.bass_utils import run_bass_kernel_spmd

    a = {k: np.asarray(v) for k, v in inputs.items()}

    def feature_major(x, n):
        return np.ascontiguousarray(x.reshape(n, KD, P).transpose(2, 1, 0))

    def states(v):
        return v.reshape(BLOCKS, P).T

    def vector(v):
        return v.reshape(-1, P).T

    def b_rows(v):
        return v.reshape(BLOCKS, P, 16).transpose(1, 0, 2).reshape(P, 256)

    def c_rows(v):
        return b_rows(v.transpose(0, 2, 1))

    def padded(v):
        return np.pad(v, ((0, 0), (0, 16 * ROUND)))

    skip = np.tile(a["d_skip"][0].reshape(BLOCKS, CH).T, (L, 1))
    small = np.concatenate([
        vector(a["g_mix"][0]), vector(a["g_mem"][0]), vector(a["g_ffn"][0]), vector(a["g_final"]),
        vector(a["b_gate"][0]), vector(a["b_glu"][0]), np.eye(P, dtype=np.float32),
        states(a["a_re"][0]), states(a["a_im"][0]), states(np.broadcast_to(a["log_dt"][0][:, None], (32, 64))),
        padded(b_rows(a["bm_re"][0])), padded(b_rows(a["bm_im"][0])), c_rows(a["cm_re"][0]), c_rows(a["cm_im"][0]),
        skip], axis=1)
    wide = [np.broadcast_to(v.reshape(1, WB), (P, WB)) for v in (a["g_sgu"][0], a["beta_sgu"][0], a["b_s"][0])]
    mix = a["w_s"][0].transpose(2, 0, 1).reshape(P, WB)
    arrays = {
        "xt_dram": feature_major(a["x"], T),
        "mem_dram": feature_major(a["mem"], M),
        "small_dram": np.ascontiguousarray(small),
        "sgu_dram": np.ascontiguousarray(np.stack([*wide, mix], axis=1)),
        "w_dram": _stream(*(a[k][0] for k in ("w_in", "w_kv", "w_glu", "w_a_out", "w_b_out", "w_c_out", "w_out",
                                              "w_gate", "w_up", "w_down"))),
    }
    nc = bacc.Bacc("TRN2", target_bir_lowering=False, num_devices=1)
    args = [nc.dram_tensor(n, x.shape, mybir.dt.from_np(x.dtype), kind="ExternalInput").ap()
            for n, x in arrays.items()]
    out = nc.dram_tensor("out_dram", (KD, P, T), mybir.dt.float32, kind="ExternalOutput").ap()
    build(nc, *args, out)
    r = run_bass_kernel_spmd(nc, [arrays], core_ids=[0])
    return r.results[0]["out_dram"].reshape(D, T).T.reshape(1, T, D)
```

```python
from contextlib import ExitStack

import concourse.bass as bass
import numpy as np
from concourse import mybir

P = 128
D = 1024
T = 512
M = 256
KD = D // P
WB = 512
KB = WB // P
FF = 2816
KF = FF // P
HEADS = 4
EPS = 1e-6
SCALE = 128.0 ** -0.5
TILE = 1024

BLOCKS = 16
ROUND = 4
ROUNDS = BLOCKS // ROUND
L = 4
NC = T // L
CH = 32

T_ZA, T_ZV = 0, 4
T_QK = 8
T_VU = 16
T_J1 = 24
T_J2 = T_J1 + 6 * 4
T_GLU = T_J2 + 2
T_WO = T_J2 + 14
T_FF = T_WO + KD
T_DN = T_FF + 4 * (KF // 2)
TILES = T_DN + KF
WARM_UP = 24
RAW = 2
NS = 2

C_GMIX, C_GMEM, C_GFFN, C_GFIN = 0, 8, 16, 24
C_BGATE = 32
C_BGLU = C_BGATE + 24
C_ID = C_BGLU + 4
C_ARE = C_ID + P
C_AIM, C_LDT = C_ARE + 16, C_ARE + 32
PADDED = BLOCKS + ROUND
C_BRE = C_ARE + 48
C_BIM = C_BRE + 16 * PADDED
C_CRE = C_BIM + 16 * PADDED
C_CIM = C_CRE + 256
C_D = C_CIM + 256
N_SMALL = C_D + 16

TWO_PI = 2 * np.pi
ROUNDER = 12582912.0
PI_HI = 6.28125
PI_MID = float(np.float32(round((TWO_PI - PI_HI) * 2 ** 20) / 2 ** 20))
PI_LO = float(np.float32(TWO_PI - PI_HI - PI_MID))
HALF_PI = float(np.float32(np.pi / 2))
SIN_MAX = 3.1415925


def build(nc, xt_d, mem_d, small_d, sgu_d, w_d, out_d):
    F = mybir.dt.float32
    R = mybir.dt.float32r
    ACT = mybir.ActivationFunctionType
    ALU = mybir.AluOpType
    AX = mybir.AxisListType.X
    ds = bass.ds

    with ExitStack() as ctx:
        def sem(name):
            return ctx.enter_context(nc.semaphore(name))

        base = (nc.sbuf_base + 63) // 64 * 64

        def at(name, off, shape, dt=F):
            return nc.alloc_sbuf_tensor_at(name, shape, dt, offset=off)

        o_raw = base
        o_hi = o_raw + RAW * 4096
        o_lo = o_hi + NS * 4096
        o_x = o_lo + NS * 4096
        o_h = o_x + 16384
        o_a = o_h + 32768
        o_b = o_a + 16384
        o_c = o_b + 32768
        o_u = o_c + 32768
        o_e = o_u + 8192
        o_f = o_e + 16384
        o_g = o_f + 8192
        o_s = o_g + 6144
        o_d = o_s + (N_SMALL * 4 + 63) // 64 * 64

        raw = at("raw", o_raw, [P, RAW, TILE])
        w_hi = at("w_hi", o_hi, [P, NS, TILE], R)
        w_lo = at("w_lo", o_lo, [P, NS, TILE], R)
        xT = at("xT", o_x, [P, KD, T])
        h_hi = at("h_hi", o_h, [P, KD, T], R)
        h_lo = at("h_lo", o_h + 16384, [P, KD, T], R)
        osq = at("osq", o_h, [P, KD, T])
        osum = at("osum", o_h + 16384, [P, 2, T])
        spread = at("spread", o_h + 20480, [P, 4, P])
        last_raw = at("last_raw", o_h, [P, TILE])
        last_hi = at("last_hi", o_h + 22528, [P, TILE], R)
        last_lo = at("last_lo", o_h + 26624, [P, TILE], R)
        memf = at("memf", o_a, [P, KD, M])
        qT = at("qT", o_a, [P, HEADS, T])
        kT = at("kT", o_a + 8192, [P, HEADS, M])
        vM = at("vM", o_a + 12288, [P, 2, WB])
        mgf = at("mgf", o_a, [P, KD, T])
        vtok = at("vtok", o_b, [P, 4, WB])
        ug = at("ug", o_b + 8192, [P, KB, T])
        sgu = at("sgu", o_b + 16384, [P, 4, WB])
        prob = at("prob", o_b + 24576, [P, 8, M])
        bb_tmp = at("bb_tmp", o_b + 24576, [P, 4, BLOCKS, 16])
        ba = [at(f"ba{i}", o_b + 2048 * i, [P, ROUND, L, CH]) for i in range(2)]
        gt = [at(f"gt{i}", o_b + 4096 + 2048 * i, [P, ROUND, P]) for i in range(2)]
        ca = [at(f"ca{i}", o_b + 8192 + 4096 * i, [P, ROUND, L + 1, CH]) for i in range(2)]
        toep = at("toep", o_b + 16384, [P, ROUND, P])
        uc = at("uc", o_b + 18432, [P, ROUND, NC])
        rot = [at(f"rot{i}", o_b + 20480 + 2048 * i, [P, ROUND, NC]) for i in range(4)]
        st = [at(f"st{i}", o_b + 28672 + 2048 * i, [P, ROUND, NC]) for i in range(2)]
        ya_hi = at("ya_hi", o_b, [P, KB, T], R)
        ya_lo = at("ya_lo", o_b + 8192, [P, KB, T], R)
        y2f = at("y2f", o_b + 16384, [P, 2, T])
        mg_hi = at("mg_hi", o_b, [P, KD, T], R)
        mg_lo = at("mg_lo", o_b + 16384, [P, KD, T], R)
        m_hi = at("m_hi", o_c, [P, KD, M], R)
        m_lo = at("m_lo", o_c + 8192, [P, KD, M], R)
        yb_hi = at("yb_hi", o_c, [P, KB, T], R)
        yb_lo = at("yb_lo", o_c + 8192, [P, KB, T], R)
        y2_hi = at("y2_hi", o_c, [P, KB, T], R)
        y2_lo = at("y2_lo", o_c + 8192, [P, KB, T], R)
        tab_tmp = at("tab_tmp", o_c + 16384, [P, 4, BLOCKS, NC // 2])
        o_hiT = at("o_hiT", o_c + 16384, [P, HEADS, T], R)
        o_loT = at("o_loT", o_c + 24576, [P, HEADS, T], R)
        uT = at("uT", o_u, [P, KB, T])
        act_hi = at("act_hi", o_a, [P, KF, T], R)
        act_lo = at("act_lo", o_a + KF * T * 4, [P, KF, T], R)
        assert o_a + 2 * KF * T * 4 == o_e
        cosT = at("cosT", o_e, [P, BLOCKS, NC])
        sinT = at("sinT", o_e + 8192, [P, BLOCKS, NC])
        silu = at("silu", o_e, [P, 2, T])
        actf = at("actf", o_e + 4096, [P, 2, T])
        zg = at("zg", o_e, [P, 4, T])
        std = at("std", o_e + 10240, [P, T])
        mstd = at("mstd", o_f, [P, M])
        mrstd = at("mrstd", o_f + 1024, [P, M])
        pT = at("pT", o_f, [P, 2, 2, T])
        yaf = at("yaf", o_f, [P, KB, T])
        mf = at("mf", o_f, [P, 2, T])
        sq = at("sq", o_g, [P, 2, T])
        sqsum = at("sqsum", o_g + 4096, [P, T])
        th = at("th", o_g, [P, 2, T])
        prod = at("prod", o_g + 4096, [P, T])
        small = at("small", o_s, [P, N_SMALL])
        s5p = at("s5p", o_d, [P, 20, PADDED])
        o_d2 = o_d + 1600
        ones = at("ones", o_d2, [P, P])
        rstd = at("rstd", o_d2 + 512, [P, T])
        o_d3 = o_d2 + 2560
        (eps, hbias, stats, mv, vrs, vstd, smx, snm, ssum, srec, tstd, trstd, mtstd, mtrstd) = (
            at(n, o_d3 + 128 * i, shape) for i, (n, shape) in enumerate((
                ("eps", [P, 1]), ("hbias", [P, 28]), ("stats", [P, 4, 6]), ("mv", [P, 4, 2]), ("vrs", [P, 4]),
                ("vstd", [P, 4]), ("smx", [P, 16]), ("snm", [P, 16]), ("ssum", [P, 16]), ("srec", [P, 16]),
                ("tstd", [P, 4]), ("trstd", [P, 4]), ("mtstd", [P, 2]), ("mtrstd", [P, 2]))))
        assert o_d3 + 128 * 14 <= nc.sbuf_usable_end, o_d3 + 128 * 14 - nc.sbuf_usable_end

        bank = [ctx.enter_context(nc.psum_tensor(f"bank{i}", [P, T], F)) for i in range(8)]
        ident = small[:, C_ID:C_ID + P]

        def fv(t):
            return t.bitcast(F)

        def flat(ap):
            return ap.rearrange("p a b -> p (a b)")

        def sems(names):
            return [sem(n) for n in names.split()]

        raw_loaded = [sem(f"raw_loaded{i}") for i in range(RAW)]
        w_rounded, w_ready, w_half = sems("w_rounded w_ready w_half")
        w_used = sem("w_used")
        x_loaded = [sem(f"x_loaded{i}") for i in range(4)]
        vec_loaded, small_loaded, mem_loaded, sgu_loaded, last_loaded = sems(
            "vec_loaded small_loaded mem_loaded sgu_loaded last_loaded")
        consts, wst_masked = sems("consts wst_masked")
        dve_step = sem("dve_step")
        norms = {n: dict(zip(("sq", "sum", "ssq", "std", "hi", "lo"),
                             sems(" ".join(f"{n}_{k}" for k in ("sq", "sum", "ssq", "std", "hi", "lo")))))
                 for n in ("x", "m", "f")}
        tok_ssq, tok_std, rstd_ready, mrstd_ready = sems("tok_ssq tok_std rstd_ready mrstd_ready")
        za_taken, zv_taken, zq_taken, k_taken, v_taken, zu_scaled, zu_ready = sems(
            "za_taken zv_taken zq_taken k_taken v_taken zu_scaled zu_ready")
        var_ready, vstd_ready, vln_ready = sems("var_ready vstd_ready vln_ready")
        sgu_done, sgu_taken, yb_f, yb_hi_s, yb_lo_s = sems("sgu_done sgu_taken yb_f yb_hi_s yb_lo_s")
        sc_done, mx_ready, exp_done, p_ready = sems("sc_done mx_ready exp_done p_ready")
        pt_done, pt_act, pt_dve, pv_done, o_hi_s, o_lo_s = sems("pt_done pt_act pt_dve pv_done o_hi_s o_lo_s")
        dt_ready, ang_ready, trig_ready = sems("dt_ready ang_ready trig_ready")
        j1_g, j1_th, j1_merge = sems("j1_g j1_th j1_merge")
        uc_ready, bc_ready, gt_done, gt_ready, vin_done, st_ready, y_done, y_taken = sems(
            "uc_ready bc_ready gt_done gt_ready vin_done st_ready y_done y_taken")
        ya_hi_s, ya_lo_s, glu_th, y2_f, y2_hi_s, y2_lo_s = sems("ya_hi_s ya_lo_s glu_th y2_f y2_hi_s y2_lo_s")
        j2_g, j2_th, j2_prod, j2_m, j2_hi, j2_lo = sems("j2_g j2_th j2_prod j2_m j2_hi j2_lo")
        x1_ready = sem("x1_ready")
        ff_g, ff_u, ff_silu, ff_act, ff_hi, ff_lo = sems("ff_g ff_u ff_silu ff_act ff_hi ff_lo")
        dn_part, part_taken = sems("dn_part part_taken")
        dn_done, x2_ready, x2_sq, sum_dve, sum_pool, xg_ready = sems(
            "dn_done x2_ready x2_sq sum_dve sum_pool xg_ready")
        o_ssq, o_std, diag_ready, o_wide, o_rstd = sems("o_ssq o_std diag_ready o_wide o_rstd")
        out_dve, out_pool, out_stored = sems("out_dve out_pool out_stored")
        OUT_DVE, OUT_POOL = range(0, 6), range(6, KD)
        HALF = T // 2
        HALVES = (slice(0, HALF), slice(HALF, T))

        def before(eng, *sems):
            for x in sems:
                eng.drain().then_inc(x, 1)

        SCORE_BANK, PT_BANK = (0, 2, 0, 0), (2, 2, 0, 2)
        SGU_BANK = (6, 7, 0, 1)
        J2_TILE = [T_J2 + t for t in (0, 1, 4, 5, 8, 9, 10, 11)]
        J2_OUT = [T_J2 + t for t in (6, 7, 12, 13)]
        WIDE_BANKS = ((1, 2), (3, 4))
        Y_BANK, G_BANK = (2, 3, 6, 7), (0, 1, 4, 5)

        class Steps:

            def __init__(self, eng, s):
                self.eng, self.s, self.base, self.n = eng, s, 0, 0

            def go(self, ins):
                ins.then_inc(self.s, 1)
                self.n += 1

            def wait(self):
                self.eng.wait_ge(self.s, self.base + self.n)

            def link(self, ins):
                self.go(ins)
                self.wait()

            def enter(self, i, per):
                self.outer, self.per = self.base + self.n, per
                self.base, self.n = self.base + self.n + i * per, 0

            def leave(self, count):
                assert self.n == self.per, self.n
                self.base, self.n = self.outer + count * self.per, 0

        block = ctx.enter_context(nc.Block())

        @block.sync
        def _(sp):
            def load_weights(s, t, tile):
                sp.dma_start(raw[:, s, :], tile).then_inc(raw_loaded[s], 16)

            def load_x(i):
                sp.dma_start(xT[:, 2 * i:2 * i + 2, :], xt_d[:, 2 * i:2 * i + 2, :]).then_inc(x_loaded[i], 16)

            sp.dma_start(small[:, 0:C_ARE], small_d[:, 0:C_ARE]).then_inc(vec_loaded, 16)
            load_x(0)
            load_weights(0, 0, w_d[0, :, :])
            load_x(1)
            load_x(2)
            load_x(3)
            load_weights(1, 1, w_d[1, :, :])

            def next_weights(t):
                sp.wait_ge(w_ready, t + 1 - RAW)
                load_weights(t % RAW, t, w_d[t, :, :])

            next_weights(2)
            sp.dma_start(memf[:, :, :], mem_d).then_inc(mem_loaded, 16)
            next_weights(3)
            sp.dma_start(small[:, C_ARE:N_SMALL], small_d[:, C_ARE:N_SMALL]).then_inc(small_loaded, 16)
            next_weights(4)
            sp.dma_start(sgu[:, :, :], sgu_d).then_inc(sgu_loaded, 16)
            next_weights(5)
            with nc.sync.Fori(3, TILES // RAW - 1) as i:
                for s in range(RAW):
                    sp.wait_ge(w_ready, i * RAW + (s + 1 - RAW))
                    load_weights(s, i * RAW + s, w_d[ds(i * RAW + s, 1), :, :].rearrange("a p n -> p (a n)"))
            next_weights(TILES - 2)
            sp.wait_ge(w_used, T_DN)
            sp.dma_start(last_raw[:, :], w_d[TILES - 1, :, :]).then_inc(last_loaded, 16)
            for h, tokens in enumerate(HALVES):
                for k in (0, 2, 6, 4):
                    if k in OUT_DVE:
                        sp.wait_ge(out_dve, len(OUT_DVE) * h + k + 2)
                    else:
                        sp.wait_ge(out_pool, len(OUT_POOL) * h + k - OUT_POOL[0] + 2)
                    sp.dma_start(out_d[k:k + 2, :, tokens].rearrange("k p t -> p k t"), xT[:, k:k + 2, tokens]
                                 ).then_inc(out_stored, 16)
            sp.wait_ge(out_stored, 16 * KD)

        @block.gpsimd
        def _(pool):
            nc.gpsimd.memset(ones[:, :], 1.0)
            nc.gpsimd.memset(eps[:, :], EPS).then_inc(consts, 1)

            def low_weights(s, t, rounded=None):
                pool.wait_ge(w_rounded, t + 1 if rounded is None else rounded)
                nc.gpsimd.tensor_tensor(w_lo[:, s, :], raw[:, s, :], fv(w_hi[:, s, :]),
                                        ALU.subtract).then_inc(w_ready, 1)

            def low_weights_in_halves(s, t):
                pool.wait_ge(w_rounded, t + 1)
                for j, done in enumerate((w_half, w_ready)):
                    c = slice(j * TILE // 2, (j + 1) * TILE // 2)
                    nc.gpsimd.tensor_tensor(w_lo[:, s, c], raw[:, s, c], fv(w_hi[:, s, c]),
                                            ALU.subtract).then_inc(done, 1)

            for t in range(NS):
                low_weights_in_halves(t, t)
            with nc.gpsimd.Fori(1, T_QK // NS) as i:
                for s in range(NS):
                    low_weights(s, i * NS + s)
            pool.wait_ge(sgu_loaded, 16)
            wst = sgu[:, 3, :].rearrange("p (g t) -> p g t", g=4)
            nc.gpsimd.affine_select(out=wst, in_=wst, pattern=[[0, 4], [1, P]], compare_op=ALU.is_ge,
                                    fill=0.0, base=0, channel_multiplier=-1).then_inc(wst_masked, 1)
            with nc.gpsimd.Fori(T_QK // NS, T_J1 // NS) as i:
                for s in range(NS):
                    low_weights_in_halves(s, i * NS + s)
            with nc.gpsimd.Fori(T_J1 // NS, TILES // NS - 1) as i:
                for s in range(NS):
                    low_weights(s, i * NS + s)
            pool.wait_ge(w_rounded, TILES - 1)
            nc.gpsimd.tensor_tensor(last_lo[:, :], last_raw[:, :], fv(last_hi[:, :]), ALU.subtract
                                    ).then_inc(w_ready, 1)
            low_weights(0, TILES - 2, TILES)
            def sum_odd(h, tokens):
                pool.wait_ge(x2_sq, KD * h + 4)
                nc.gpsimd.tensor_tensor(osum[:, 1, tokens], osq[:, 1, tokens], osq[:, 3, tokens], ALU.add
                                        ).then_inc(sum_pool, 1)
                pool.wait_ge(x2_sq, KD * h + 6)
                pool.wait_ge(sum_pool, 2 * h + 1)
                nc.gpsimd.tensor_tensor(osum[:, 1, tokens], osum[:, 1, tokens], osq[:, 5, tokens], ALU.add
                                        ).then_inc(sum_pool, 1)

            def scale_out(h, tokens):
                pool.wait_ge(o_rstd, h + 1)
                for k in OUT_POOL:
                    pool.wait_ge(xg_ready, len(OUT_POOL) * h + k - OUT_POOL[0] + 1)
                    nc.gpsimd.tensor_tensor(xT[:, k, tokens], xT[:, k, tokens], rstd[:, tokens], ALU.mult
                                            ).then_inc(out_pool, 1)

            for step in (sum_odd, scale_out):
                for h, tokens in enumerate(HALVES):
                    step(h, tokens)

        @block.scalar
        def _(act):
            def round_weights(t, m=0, per=0):
                slot = t % NS
                act.wait_ge(raw_loaded[slot], 16 * (per // 2) * m + 16 * (t // 2 + 1))
                if t >= NS:
                    act.wait_ge(w_used, per * m + (t + 1 - NS))
                nc.scalar.activation(w_hi[:, slot, :], raw[:, slot, :], ACT.Copy).then_inc(w_rounded, 1)

            def square(s, src, k, width):
                if k >= 2:
                    act.wait_ge(s["sum"], k - 1)
                nc.scalar.activation(sq[:, k % 2, 0:width], src, ACT.Square).then_inc(s["sq"], 1)

            def root(out, src):
                return nc.scalar.activation(out, src, ACT.Sqrt, bias=eps[:, 0:1], scale=1.0 / D)

            def round_tile(s, dst, src, gain, k):
                nc.scalar.activation(dst[:, k, :], src[:, k, :], ACT.Copy,
                                     scale=small[:, gain + k:gain + k + 1]).then_inc(s["hi"], 1)

            act.wait_ge(consts, 1)
            nc.scalar.activation(tstd[:, 0:1], ones[:, 0:1], ACT.Copy)
            act.wait_ge(vec_loaded, 16)
            for k in range(KD):
                if k % 2 == 0:
                    act.wait_ge(x_loaded[k // 2], 16)
                round_tile(norms["x"], h_hi, xT, C_GMIX, k)
                if k in (1, 7):
                    round_weights(k // 4)
            for k in range(KD):
                square(norms["x"], xT[:, k, :], k, T)
                if k == 3:
                    round_weights(T_ZA + 2)
            act.wait_ge(mem_loaded, 16)
            for k in range(KD):
                round_tile(norms["m"], m_hi, memf, C_GMEM, k)
            round_weights(T_ZA + 3)
            act.wait_ge(norms["x"]["sum"], KD)
            for k in range(KD):
                square(norms["m"], memf[:, k, :], k, M)
            act.wait_ge(consts, 1)
            act.wait_ge(norms["x"]["ssq"], 1)
            root(std[:, :], bank[7][:, :]).then_inc(norms["x"]["std"], 1)
            act.wait_ge(tok_ssq, 1)
            root(tstd[:, :], bank[6][:, 0:4]).then_inc(tok_std, 1)
            round_weights(T_ZV)
            act.wait_ge(norms["m"]["ssq"], 1)
            root(mstd[:, :], bank[7][:, 0:M]).then_inc(norms["m"]["std"], 1)
            act.wait_ge(tok_ssq, 2)
            root(mtstd[:, :], bank[6][:, 0:2]).then_inc(tok_std, 1)
            round_weights(T_ZV + 1)
            act.wait_ge(small_loaded, 16)
            nc.scalar.activation(s5p[:, 0, 0:16], small[:, C_LDT:C_LDT + 16], ACT.Exp).then_inc(dt_ready, 1)
            round_weights(T_ZV + 2)
            act.wait_ge(ang_ready, 1)
            nc.scalar.activation(s5p[:, 1, 0:16], s5p[:, 4, 0:16], ACT.Exp)
            nc.scalar.activation(s5p[:, 2, 0:16], s5p[:, 6, 0:16], ACT.Sin)
            nc.scalar.activation(s5p[:, 3, 0:16], s5p[:, 5, 0:16], ACT.Sin).then_inc(trig_ready, 1)
            round_weights(T_ZV + 3)
            round_weights(T_QK)
            round_weights(T_QK + 1)
            act.wait_ge(w_used, T_ZV + 4)
            act.wait_ge(rstd_ready, 1)
            for c in range(4):
                nc.scalar.activation(vtok[:, c, :], bank[4 + c][:, :], ACT.Gelu_apprx_tanh,
                                     scale=trstd[:, c:c + 1]).then_inc(zv_taken, 1)
            for t in range(2, 6):
                round_weights(T_QK + t)
            act.wait_ge(var_ready, 4)
            nc.scalar.activation(vstd[:, :], mv[:, :, 1], ACT.Sqrt, bias=eps[:, 0:1]).then_inc(vstd_ready, 1)
            for t in range(6, 10):
                round_weights(T_QK + t)

            def softmax_exp(h):
                for tt in range(4):
                    act.wait_ge(mx_ready, 2 * h + tt // 2 + 1)
                    if h >= 2:
                        act.wait_ge(pt_done, h - 1)
                    i = 4 * h + tt
                    b = SCORE_BANK[h] + tt // 2
                    nc.scalar.activation(prob[:, i % 8, :], bank[b][:, (tt % 2) * M:(tt % 2 + 1) * M], ACT.Exp,
                                         bias=snm[:, i:i + 1], scale=SCALE, accum_out=ssum[:, i:i + 1]
                                         ).then_inc(exp_done, 1)

            def gelu_u(c):
                act.wait_ge(zu_scaled, c + 1)
                nc.scalar.activation(ug[:, c, :], ug[:, c, :], ACT.Gelu_apprx_tanh).then_inc(zu_ready, 1)

            def take_pt(h):
                act.wait_ge(pt_done, h + 1)
                if h >= 2:
                    act.wait_ge(pv_done, h - 1)
                nc.scalar.activation(pT[:, h % 2, 0, :], bank[PT_BANK[h]][:, :], ACT.Copy).then_inc(pt_act, 1)

            def round_o(h):
                act.wait_ge(pv_done, h + 1)
                nc.scalar.activation(o_hiT[:, h, :], bank[4 + h % 2][:, :], ACT.Copy).then_inc(o_hi_s, 1)

            def round_yb(g):
                act.wait_ge(yb_f, g + 1)
                nc.scalar.activation(yb_hi[:, g, :], ug[:, g, :], ACT.Copy).then_inc(yb_hi_s, 1)

            softmax_exp(0)
            softmax_exp(1)
            round_weights(T_VU + 2)
            round_weights(T_VU + 3)
            gelu_u(0)
            round_weights(T_VU + 4)
            take_pt(0)
            softmax_exp(2)
            round_weights(T_VU + 5)
            gelu_u(1)
            round_weights(T_VU + 6)
            round_weights(T_VU + 7)
            gelu_u(2)
            round_weights(T_J1)
            take_pt(1)
            softmax_exp(3)
            round_weights(T_J1 + 1)
            gelu_u(3)
            take_pt(2)
            round_o(0)
            take_pt(3)
            round_o(1)
            for g in range(4):
                round_yb(g)
            round_o(2)
            round_o(3)
            nc.scalar.mul(hbias[:, :], small[:, C_BGATE:C_BGATE + 28], 0.5)
            before(act, y_taken)
            act.wait_ge(y_taken, 1)

            def half_tanh(buf, src, bias):
                return nc.scalar.activation(buf, src, ACT.Tanh, bias=bias, scale=0.5)

            def gate(n, m, done, col):
                act.wait_ge(j1_g, 4 * m + (done + 1))
                half_tanh(th[:, n, :], th[:, n, :], hbias[:, ds(2 * m + (col + n), 1)]).then_inc(j1_th, 1)

            with nc.scalar.Fori(0, ROUNDS) as m:
                for n in range(2):
                    round_weights(T_J1 + 2 + n, m, 6)
                for n in range(2):
                    gate(n, m, n + 1, 8)
                act.wait_ge(y_done, m + 1)
                for q in range(ROUND):
                    for j in range(L):
                        src = uT[32 * q:32 * q + 32, ds(m, 1), :].rearrange("p a (c j) -> p (a c) j", j=L)
                        ins = nc.scalar.activation(uc[32 * j:32 * j + 32, q, :], src[:, :, j], ACT.Copy)
                ins.then_inc(uc_ready, 1)
                for j in range(4, 7):
                    round_weights(T_J1 + j, m, 6)
                for n in range(2):
                    gate(n, m, n + 3, 16)
                round_weights(T_J1 + 7, m, 6)
                act.wait_ge(y_done, m + 2)
                for q in range(ROUND):
                    for i in range(L):
                        dst = yaf[32 * q:32 * q + 32, ds(m, 1), :].rearrange("p a (c j) -> p (a c) j", j=L)
                        ins = nc.scalar.activation(dst[:, :, i], bank[7][32 * i:32 * i + 32, q * NC:(q + 1) * NC],
                                                   ACT.Gelu_apprx_tanh)
                ins.then_inc(y_taken, 1)
            act.wait_ge(y_taken, ROUNDS + 1)
            act.wait_ge(j1_merge, 17)
            for c in range(KB):
                nc.scalar.activation(ya_hi[:, c, :], yaf[:, c, :], ACT.Copy).then_inc(ya_hi_s, 1)

            def gate0(g):
                act.wait_ge(j2_g, g + 1)
                half_tanh(zg[:, g % 4, :], zg[:, g % 4, :], hbias[:, g:g + 1]).then_inc(j2_th, 1)

            def round_merged(g):
                act.wait_ge(j2_m, g + 1)
                nc.scalar.activation(mg_hi[:, g, :], mf[:, g % 2, :], ACT.Copy).then_inc(j2_hi, 1)

            for n in range(2):
                round_weights(T_J2 + 2 + n)
                gate0(n)
            for t in range(2):
                round_weights(T_J2 + 4 + t)
                act.wait_ge(w_used, T_GLU + t + 1)
                for c in (2 * t, 2 * t + 1):
                    if c >= 2:
                        act.wait_ge(y2_f, c - 1)
                    half_tanh(th[:, c % 2, :], bank[Y_BANK[c]][:, :], hbias[:, 24 + c:25 + c]).then_inc(glu_th, 1)
                for c in (2 * t, 2 * t + 1):
                    act.wait_ge(y2_f, c + 1)
                    nc.scalar.activation(y2_hi[:, c, :], y2f[:, c % 2, :], ACT.Copy).then_inc(y2_hi_s, 1)
            for n in range(2):
                round_weights(T_J2 + 6 + n)
                gate0(2 + n)
            for g in (0, 2):
                round_weights(T_J2 + 8 + g // 2)
                round_merged(g)
                round_merged(g + 1)
            for n in range(4):
                round_weights(T_J2 + 10 + n)
                gate0(4 + n)
            for g in (4, 6):
                round_weights(T_WO + g // 2 - 2)
                round_merged(g)
                round_merged(g + 1)
            s = norms["f"]
            for k in range(KD):
                round_weights(T_WO + k + 2)
                act.wait_ge(x1_ready, k + 5)
                round_tile(s, h_hi, xT, C_GFFN, k)
                act.wait_ge(s["sum"], max(k, 1))
                nc.scalar.activation(sq[:, k % 2, :], xT[:, k, :], ACT.Square).then_inc(s["sq"], 1)
            round_weights(T_FF + 2)
            act.wait_ge(s["ssq"], 1)
            root(std[:, :], bank[4][:, :]).then_inc(s["std"], 1)
            with nc.scalar.Fori(0, KF // 2) as i:
                def round_hidden(n):
                    act.wait_ge(ff_act, 2 * i + (n + 1))
                    nc.scalar.activation(act_hi[:, ds(2 * i + n, 1), :], actf[:, n:n + 1, :], ACT.Copy
                                         ).then_inc(ff_hi, 1)

                round_weights(T_FF + 3, i, 4)
                round_weights(T_FF + 4, i, 4)
                for n in range(2):
                    act.wait_ge(ff_g, 2 * i + (n + 2))
                    nc.scalar.activation(silu[:, n, :], silu[:, n, :], ACT.Silu).then_inc(ff_silu, 1)
                round_hidden(0)
                round_weights(T_FF + 5, i, 4)
                round_hidden(1)
                round_weights(T_FF + 6, i, 4)
            with nc.scalar.Fori(0, KF // 2 - 3) as i:
                for j in range(2):
                    round_weights(T_DN + 3 + j, i, 2)
            round_weights(T_DN + KF - 3)
            act.wait_ge(last_loaded, 16)
            nc.scalar.activation(last_hi[:, :], last_raw[:, :], ACT.Copy).then_inc(w_rounded, 1)
            round_weights(T_DN + KF - 2)
            nc.scalar.activation(tstd[:, :], trstd[:, :], ACT.Sqrt)
            def square_x2(h, k):
                act.wait_ge(x2_ready, KD * h + k + 1)
                nc.scalar.activation(osq[:, k, HALVES[h]], xT[:, k, HALVES[h]], ACT.Square).then_inc(x2_sq, 1)

            def times_gain(h):
                for k in OUT_POOL:
                    act.wait_ge(x2_sq, KD * h + k + 1)
                    nc.scalar.activation(xT[:, k, HALVES[h]], xT[:, k, HALVES[h]], ACT.Copy,
                                         scale=small[:, C_GFIN + k:C_GFIN + k + 1]).then_inc(xg_ready, 1)

            def last_root(h):
                act.wait_ge(o_ssq, h + 1)
                root(tstd[:, 2 * h:2 * h + 2], bank[0][:, 0:2]).then_inc(o_std, 1)

            def take_wide(h):
                act.wait_ge(o_wide, 2 * h + 2)
                nc.scalar.activation(rstd[:, HALVES[h]], bank[WIDE_BANKS[h][1]][:, 0:HALF], ACT.Copy
                                     ).then_inc(o_rstd, 1)

            for k in range(KD):
                square_x2(0, k)
            times_gain(0)
            for k in range(KD):
                square_x2(1, k)
                if k == 3:
                    last_root(0)
            times_gain(1)
            take_wide(0)
            last_root(1)
            take_wide(1)

        @block.vector
        def _(dve):
            V = nc.vector
            steps = Steps(dve, dve_step)
            go, link = steps.go, steps.link

            def tt(out, a, b, op):
                return V.tensor_tensor(out, a, b, op)

            def add_square(s, k, width, value):
                dve.wait_ge(s["sq"], value)
                if k == 0:
                    V.tensor_copy(sqsum[:, 0:width], sq[:, 0, 0:width]).then_inc(s["sum"], 1)
                else:
                    dve.wait_ge(s["sum"], k)
                    tt(sqsum[:, 0:width], sqsum[:, 0:width], sq[:, k % 2, 0:width], ALU.add).then_inc(s["sum"], 1)

            def low_tile(s, hi, lo, src, gain, k):
                dve.wait_ge(s["hi"], k + 1)
                V.scalar_tensor_tensor(lo[:, k, :], src[:, k, :], small[:, gain + k:gain + k + 1], fv(hi[:, k, :]),
                                       ALU.mult, ALU.subtract).then_inc(s["lo"], 1)

            dve.wait_ge(vec_loaded, 16)
            for k in range(KD):
                if k % 2 == 0:
                    dve.wait_ge(x_loaded[k // 2], 16)
                low_tile(norms["x"], h_hi, h_lo, xT, C_GMIX, k)
            for k in range(KD):
                add_square(norms["x"], k, T, k + 1)
            dve.wait_ge(mem_loaded, 16)
            for k in range(KD):
                low_tile(norms["m"], m_hi, m_lo, memf, C_GMEM, k)
            dve.wait_ge(norms["x"]["ssq"], 1)
            dve.wait_ge(tok_ssq, 1)
            for k in range(KD):
                add_square(norms["m"], k, M, k + 1)
            dve.wait_ge(norms["x"]["std"], 1)
            link(V.reciprocal(rstd[:, :], std[:, :]))
            dve.wait_ge(tok_std, 1)
            V.reciprocal(trstd[:, :], tstd[:, :]).then_inc(rstd_ready, 1)
            for c in range(3):
                dve.wait_ge(w_used, T_ZA + c + 1)
                tt(uT[:, c, :], bank[c][:, :], rstd[:, :], ALU.mult).then_inc(za_taken, 1)
            dve.wait_ge(norms["m"]["std"], 1)
            link(V.reciprocal(mrstd[:, :], mstd[:, :]))
            dve.wait_ge(tok_std, 2)
            V.reciprocal(mtrstd[:, :], mtstd[:, :]).then_inc(mrstd_ready, 1)
            dve.wait_ge(w_used, T_ZA + 4)
            tt(uT[:, 3, :], bank[3][:, :], rstd[:, :], ALU.mult).then_inc(za_taken, 1)

            (DT, MAG, SN, CS, XR, RC, RR, TH, ARE, AIM, T0, T1, T2, FRE, FIM, M4, ER, EI, T3, T4) = (
                s5p[:, i, 0:BLOCKS] for i in range(20))
            are, aim = small[:, C_ARE:C_ARE + 16], small[:, C_AIM:C_AIM + 16]
            dve.wait_ge(small_loaded, 16)
            go(V.memset(s5p[:, 8:10, BLOCKS:PADDED], 0.0))
            dve.wait_ge(dt_ready, 1)
            go(tt(XR, are, DT, ALU.mult))
            link(tt(TH, aim, DT, ALU.mult))
            link(V.tensor_scalar(T0, TH, 1.0 / TWO_PI, ROUNDER, ALU.mult, ALU.add))
            link(V.tensor_scalar(T1, T0, ROUNDER, None, ALU.subtract))
            link(V.scalar_tensor_tensor(T0, T1, -PI_HI, TH, ALU.mult, ALU.add))
            link(V.scalar_tensor_tensor(T2, T1, -PI_MID, T0, ALU.mult, ALU.add))
            link(V.scalar_tensor_tensor(T0, T1, -PI_LO, T2, ALU.mult, ALU.add))
            link(V.tensor_scalar(RR, T0, SIN_MAX, -SIN_MAX, ALU.min, ALU.max))
            link(V.tensor_scalar(T1, RR, -1.0, None, ALU.mult))
            link(tt(T2, T1, RR, ALU.max))
            V.tensor_scalar(RC, T2, -1.0, HALF_PI, ALU.mult, ALU.add).then_inc(ang_ready, 1)
            dve.wait_ge(trig_ready, 1)
            go(tt(ARE, MAG, CS, ALU.mult))
            go(tt(AIM, MAG, SN, ALU.mult))
            go(tt(T0, are, are, ALU.mult))
            go(tt(T1, aim, aim, ALU.mult))
            steps.wait()
            go(V.tensor_scalar(T2, ARE, -1.0, None, ALU.add))
            link(tt(T3, T0, T1, ALU.add))
            link(V.reciprocal(T4, T3))
            go(tt(T0, T2, are, ALU.mult))
            go(tt(T1, AIM, aim, ALU.mult))
            steps.wait()
            link(tt(T3, T0, T1, ALU.add))
            link(tt(FRE, T3, T4, ALU.mult))
            go(tt(T0, AIM, are, ALU.mult))
            go(tt(T1, T2, aim, ALU.mult))
            steps.wait()
            link(tt(T3, T0, T1, ALU.subtract))
            link(tt(FIM, T3, T4, ALU.mult))
            def wide(v, n):
                return v.unsqueeze(2).to_broadcast([P, BLOCKS, n])

            bre = small[:, C_BRE:C_BRE + 256].rearrange("p (b h) -> p b h", h=16)
            bim = small[:, C_BIM:C_BIM + 256].rearrange("p (b h) -> p b h", h=16)
            go(tt(bb_tmp[:, 0, :, :], bre, wide(FRE, 16), ALU.mult))
            go(tt(bb_tmp[:, 1, :, :], bim, wide(FIM, 16), ALU.mult))
            go(tt(bb_tmp[:, 2, :, :], bim, wide(FRE, 16), ALU.mult))
            go(tt(bb_tmp[:, 3, :, :], bre, wide(FIM, 16), ALU.mult))
            steps.wait()
            go(tt(bre, bb_tmp[:, 0, :, :], bb_tmp[:, 1, :, :], ALU.subtract))
            go(tt(bim, bb_tmp[:, 2, :, :], bb_tmp[:, 3, :, :], ALU.add))
            cim = small[:, C_CIM:C_CIM + 256]
            link(V.tensor_scalar(cim, cim, -1.0, None, ALU.mult))
            link(tt(T0, MAG, MAG, ALU.mult))
            link(tt(M4, T0, T0, ALU.mult))

            def turn_squared(re, im, rs, is_):
                go(tt(T0, rs, rs, ALU.mult))
                go(tt(T1, is_, is_, ALU.mult))
                go(V.scalar_tensor_tensor(T2, rs, 2.0, is_, ALU.mult, ALU.mult))
                steps.wait()
                go(tt(re, T0, T1, ALU.subtract))
                link(V.tensor_copy(im, T2))

            turn_squared(ER, EI, CS, SN)
            turn_squared(ER, EI, ER, EI)
            go(V.memset(cosT[:, :, 0:1], 1.0))
            link(V.memset(sinT[:, :, 0:1], 0.0))
            n = 1
            while n < NC:
                q = [tab_tmp[:, j, :, 0:n] for j in range(4)]
                go(tt(q[0], cosT[:, :, 0:n], wide(ER, n), ALU.mult))
                go(tt(q[1], sinT[:, :, 0:n], wide(EI, n), ALU.mult))
                go(tt(q[2], sinT[:, :, 0:n], wide(ER, n), ALU.mult))
                go(tt(q[3], cosT[:, :, 0:n], wide(EI, n), ALU.mult))
                steps.wait()
                go(tt(cosT[:, :, n:2 * n], q[0], q[1], ALU.subtract))
                link(tt(sinT[:, :, n:2 * n], q[2], q[3], ALU.add))
                n *= 2
                if n < NC:
                    turn_squared(ER, EI, ER, EI)

            for c in range(4):
                dve.wait_ge(zv_taken, c + 1)
                link(V.bn_stats(stats[:, c, :], vtok[:, c, :]))
                V.bn_aggr(mv[:, c, :], stats[:, c, :]).then_inc(var_ready, 1)
            dve.wait_ge(vstd_ready, 1)
            link(V.reciprocal(vrs[:, :], vstd[:, :]))
            dve.wait_ge(sgu_loaded, 16)
            for c in range(4):
                link(V.tensor_scalar(vtok[:, c, :], vtok[:, c, :], mv[:, c, 0:1], vrs[:, c:c + 1],
                                     ALU.subtract, ALU.mult))
                link(tt(vtok[:, c, :], vtok[:, c, :], sgu[:, 0, :], ALU.mult))
                tt(vtok[:, c, :], vtok[:, c, :], sgu[:, 1, :], ALU.add).then_inc(vln_ready, 1)
            for c in range(HEADS):
                dve.wait_ge(w_used, T_QK + 2 * c + 1)
                tt(qT[:, c, :], bank[c][:, :], rstd[:, :], ALU.mult).then_inc(zq_taken, 1)
                dve.wait_ge(w_used, T_QK + 2 * c + 2)
                dve.wait_ge(mrstd_ready, 1)
                tt(kT[:, c, :], bank[4 + c][:, 0:M], mrstd[:, :], ALU.mult).then_inc(k_taken, 1)

            def head_max(h):
                for half in range(2):
                    i = 4 * h + 2 * half
                    dve.wait_ge(sc_done, 2 * h + half + 1)
                    b = SCORE_BANK[h] + half
                    link(V.tensor_reduce(smx[:, i:i + 2], bank[b][:, :].rearrange("p (a m) -> p a m", m=M),
                                         AX, ALU.max))
                    V.tensor_scalar(snm[:, i:i + 2], smx[:, i:i + 2], -SCALE, None, ALU.mult
                                    ).then_inc(mx_ready, 1)

            def head_scale(h):
                dve.wait_ge(exp_done, 4 * h + 4)
                link(V.reciprocal(srec[:, 4 * h:4 * h + 4], ssum[:, 4 * h:4 * h + 4]))
                for t4 in range(4):
                    i = 4 * h + t4
                    V.tensor_scalar(prob[:, i % 8, :], prob[:, i % 8, :], srec[:, i:i + 1], None, ALU.mult
                                    ).then_inc(p_ready, 1)

            def take_pt(h):
                dve.wait_ge(pt_done, h + 1)
                if h >= 2:
                    dve.wait_ge(pv_done, h - 1)
                V.tensor_copy(pT[:, h % 2, 1, :], bank[PT_BANK[h] + 1][:, :]).then_inc(pt_dve, 1)

            def low_o(h):
                dve.wait_ge(o_hi_s, h + 1)
                tt(o_loT[:, h, :], bank[4 + h % 2][:, :], fv(o_hiT[:, h, :]), ALU.subtract).then_inc(o_lo_s, 1)

            def scale_u(c):
                dve.wait_ge(w_used, T_VU + 2 * c + 2)
                tt(ug[:, c, :], bank[6 + c % 2][:, :], rstd[:, :], ALU.mult).then_inc(zu_scaled, 1)

            def add_mix_bias(g):
                dve.wait_ge(sgu_done, g + 1)
                b = SGU_BANK[g]
                if g >= 2:
                    dve.wait_ge(yb_f, g - 1)
                bias = sgu[:, 2, g * P:(g + 1) * P].unsqueeze(1).to_broadcast([P, 4, P])
                tt(th[:, g % 2, :].rearrange("p (b t) -> p b t", b=4),
                   bank[b][:, :].rearrange("p (b t) -> p b t", b=4), bias, ALU.add).then_inc(sgu_taken, 1)

            def gated(g):
                dve.wait_ge(sgu_taken, g + 1)
                dve.wait_ge(zu_ready, g + 1)
                tt(ug[:, g, :], th[:, g % 2, :], ug[:, g, :], ALU.mult).then_inc(yb_f, 1)

            def low_yb(g):
                dve.wait_ge(yb_hi_s, g + 1)
                tt(yb_lo[:, g, :], ug[:, g, :], fv(yb_hi[:, g, :]), ALU.subtract).then_inc(yb_lo_s, 1)

            head_max(0)
            head_max(1)
            head_scale(0)
            head_scale(1)
            scale_u(0)
            take_pt(0)
            head_max(2)
            scale_u(1)
            head_scale(2)
            scale_u(2)
            take_pt(1)
            head_max(3)
            dve.wait_ge(w_used, T_VU + 7)
            for c in range(2):
                V.tensor_scalar(vM[:, c, :], bank[4 + c][:, :], mtrstd[:, c:c + 1], None, ALU.mult
                                ).then_inc(v_taken, 1)
            scale_u(3)
            head_scale(3)
            take_pt(2)
            low_o(0)
            take_pt(3)
            low_o(1)
            add_mix_bias(0)
            for g in range(3):
                add_mix_bias(g + 1)
                gated(g)
            before(dve, j1_g, j1_merge)
            gated(3)
            for g in range(4):
                low_yb(g)
            low_o(2)
            low_o(3)
            dve.wait_ge(yb_lo_s, 4)
            dve.wait_ge(pv_done, 4)
            for i in range(2):
                go(V.memset(ba[i][:, :, L - 1, :], 0.0))
                go(V.memset(ca[i][:, :, 0, :], 0.0))
                go(V.memset(st[i][:, :, 0:1], 0.0))
            go(V.memset(toep[:, :, :], 0.0))
            steps.wait()

            def b_powers(b0):
                for i, cb in enumerate((C_BRE, C_BIM)):
                    for g in range(2):
                        pr = slice(64 * g, 64 * g + 64)
                        src = small[pr, cb:cb + 16 * PADDED].rearrange("p (b h) -> p b h", h=16)[:, ds(b0, 4), :]
                        go(V.tensor_copy(ba[i][pr, :, L - 1, 16 * g:16 * g + 16], src))
                steps.wait()
                dre, dim, q = decay_of(b0)
                for j in range(L - 2, -1, -1):
                    go(tt(q[0], ba[0][:, :, j + 1, :], dre, ALU.mult))
                    go(tt(q[1], ba[1][:, :, j + 1, :], dim, ALU.mult))
                    go(tt(q[2], ba[1][:, :, j + 1, :], dre, ALU.mult))
                    go(tt(q[3], ba[0][:, :, j + 1, :], dim, ALU.mult))
                    steps.wait()
                    go(tt(ba[0][:, :, j, :], q[0], q[1], ALU.subtract))
                    link(tt(ba[1][:, :, j, :], q[2], q[3], ALU.add))

            def decay_of(b0):
                return (*(s5p[:, i, :][:, ds(b0, 4)].unsqueeze(2).to_broadcast([P, ROUND, CH]) for i in (8, 9)),
                        [rot[j][:, :, 0:CH] for j in range(4)])

            b_powers(0)

            with nc.vector.Fori(0, ROUNDS) as m:
                steps.enter(m, 75)
                dve.wait_ge(y_done, m + 1)
                for i, cc in enumerate((C_CRE, C_CIM)):
                    for g in range(2):
                        pr = slice(64 * g, 64 * g + 64)
                        src = small[pr, cc:cc + 256].rearrange("p (b h) -> p b h", h=16)[:, ds(4 * m, 4), :]
                        go(V.tensor_copy(ca[i][pr, :, 0, 16 * g:16 * g + 16], src))
                steps.wait()
                dre, dim, q = decay_of(4 * m)
                for j in range(1, L + 1):
                    go(tt(q[0], ca[0][:, :, j - 1, :], dre, ALU.mult))
                    go(tt(q[1], ca[1][:, :, j - 1, :], dim, ALU.mult))
                    go(tt(q[2], ca[1][:, :, j - 1, :], dre, ALU.mult))
                    go(tt(q[3], ca[0][:, :, j - 1, :], dim, ALU.mult))
                    steps.wait()
                    go(tt(ca[0][:, :, j, :], q[0], q[1], ALU.add))
                    ins = tt(ca[1][:, :, j, :], q[2], q[3], ALU.subtract)
                    if j < L:
                        link(ins)
                    else:
                        ins.then_inc(bc_ready, 1)

                def scale_gate(n, idx):
                    dve.wait_ge(w_used, 6 * m + (T_J1 + (0, 1, 3, 4)[idx] + 1))
                    dve.wait_ge(j1_merge, 4 * m + (1 if idx < 2 else idx))
                    tt(th[:, n, :], bank[n][:, :], rstd[:, :], ALU.mult).then_inc(j1_g, 1)

                scale_gate(0, 0)
                scale_gate(1, 1)
                def merge(first, n):
                    val = 4 * m + ((0 if first else 2) + n + 1)
                    dve.wait_ge(w_used, 6 * m + (T_J1 + (3 if first else 6)))
                    dve.wait_ge(j1_th, val)
                    dst = mgf[:, ds(2 * m + n, 1), :].rearrange("p a t -> p (a t)")
                    if first:
                        V.scalar_tensor_tensor(dst, th[:, n, :], 1.0, bank[2 + n][:, :], ALU.add, ALU.mult
                                               ).then_inc(j1_merge, 1)
                    else:
                        V.scalar_tensor_tensor(prod[:, :], th[:, n, :], 1.0, bank[2 + n][:, :], ALU.add,
                                               ALU.mult).then_inc(j1_merge, 1)
                        dve.wait_ge(j1_merge, val + 1)
                        link(tt(dst, dst, prod[:, :], ALU.add))

                merge(True, 0)
                merge(True, 1)
                dve.wait_ge(gt_done, m + 1)
                go(V.tensor_copy(flat(gt[0][:, :, :]), bank[4][:, :]))
                go(V.tensor_copy(flat(gt[1][:, :, :]), bank[5][:, :]))
                resp = bank[6][0:CH, :].rearrange("p (b c) -> p b c", b=ROUND)
                go(V.tensor_copy(toep[0:CH, :, CH:P], resp[:, :, CH:P]))
                skip = small[0:CH, C_D:C_D + 16][:, ds(4 * m, 4)].unsqueeze(2).to_broadcast([CH, ROUND, CH])
                diag = rot[0][0:CH, :, 0:CH]
                link(tt(diag, ident[0:CH, 0:CH].unsqueeze(1).to_broadcast([CH, ROUND, CH]), skip, ALU.mult))
                link(tt(toep[0:CH, :, 0:CH], resp[:, :, 0:CH], diag, ALU.add))
                for j in range(1, L):
                    ins = V.tensor_copy(toep[CH * j:CH * j + CH, :, CH * j:P], toep[0:CH, :, 0:P - CH * j])
                ins.then_inc(gt_ready, 1)
                scale_gate(0, 2)
                dve.wait_ge(vin_done, m + 1)
                vre = bank[4][:, :].rearrange("p (b c) -> p b c", b=ROUND)
                vim = bank[5][:, :].rearrange("p (b c) -> p b c", b=ROUND)
                cos, sin = cosT[:, ds(4 * m, 4), :], sinT[:, ds(4 * m, 4), :]
                go(tt(rot[0][:, :, :], vre, cos, ALU.mult))
                go(tt(rot[1][:, :, :], vim, sin, ALU.mult))
                go(tt(rot[2][:, :, :], vim, cos, ALU.mult))
                go(tt(rot[3][:, :, :], vre, sin, ALU.mult))
                steps.wait()
                go(tt(rot[0][:, :, :], rot[0][:, :, :], rot[1][:, :, :], ALU.add))
                link(tt(rot[2][:, :, :], rot[2][:, :, :], rot[3][:, :, :], ALU.subtract))
                for b in range(ROUND):
                    decay = s5p[:, 15, :][:, ds(4 * m + b, 1)].to_broadcast([P, NC])
                    go(V.tensor_tensor_scan(rot[1][:, b, :], decay, rot[0][:, b, :], 0.0, ALU.mult, ALU.add))
                    go(V.tensor_tensor_scan(rot[3][:, b, :], decay, rot[2][:, b, :], 0.0, ALU.mult, ALU.add))
                steps.wait()
                rre, rim = rot[1][:, :, 0:NC - 1], rot[3][:, :, 0:NC - 1]
                cos, sin = cosT[:, ds(4 * m, 4), 0:NC - 1], sinT[:, ds(4 * m, 4), 0:NC - 1]
                q0, q2 = rot[0][:, :, 0:NC - 1], rot[2][:, :, 0:NC - 1]
                go(tt(q0, rre, cos, ALU.mult))
                go(tt(q2, rim, sin, ALU.mult))
                steps.wait()
                link(tt(st[0][:, :, 1:NC], q0, q2, ALU.subtract))
                go(tt(q0, rre, sin, ALU.mult))
                go(tt(q2, rim, cos, ALU.mult))
                steps.wait()
                tt(st[1][:, :, 1:NC], q0, q2, ALU.add).then_inc(st_ready, 1)
                scale_gate(1, 3)
                dve.wait_ge(st_ready, m + 1)
                b_powers(4 * m + 4)
                merge(False, 0)
                merge(False, 1)
                dve.wait_ge(gt_ready, m + 1)
                dve.wait_ge(bc_ready, m + 1)
            steps.leave(ROUNDS)
            def scale_gate0(g):
                dve.wait_ge(w_used, J2_TILE[g] + 1)
                if g >= 4:
                    dve.wait_ge(j2_prod, g - 3)
                tt(zg[:, g % 4, :], bank[G_BANK[g % 4]][:, :], rstd[:, :], ALU.mult).then_inc(j2_g, 1)

            def merge0(g):
                dve.wait_ge(w_used, J2_OUT[g // 2] + 1)
                dve.wait_ge(j2_th, g + 1)
                if g:
                    dve.wait_ge(j2_m, g)
                V.scalar_tensor_tensor(prod[:, :], zg[:, g % 4, :], 1.0, bank[Y_BANK[g % 4]][:, :],
                                       ALU.add, ALU.mult).then_inc(j2_prod, 1)
                dve.wait_ge(j2_prod, g + 1)
                if g >= 2:
                    dve.wait_ge(j2_lo, g - 1)
                V.scalar_tensor_tensor(mf[:, g % 2, :], prod[:, :], 0.5, mgf[:, g, :], ALU.mult, ALU.add
                                       ).then_inc(j2_m, 1)

            def low_merged(g):
                dve.wait_ge(j2_hi, g + 1)
                tt(mg_lo[:, g, :], mf[:, g % 2, :], fv(mg_hi[:, g, :]), ALU.subtract).then_inc(j2_lo, 1)

            scale_gate0(0)
            for c in range(KB):
                dve.wait_ge(ya_hi_s, c + 1)
                tt(ya_lo[:, c, :], yaf[:, c, :], fv(ya_hi[:, c, :]), ALU.subtract).then_inc(ya_lo_s, 1)
            scale_gate0(1)
            for t in range(2):
                for c in (2 * t, 2 * t + 1):
                    dve.wait_ge(glu_th, c + 1)
                    if c >= 2:
                        dve.wait_ge(y2_lo_s, c - 1)
                    V.scalar_tensor_tensor(y2f[:, c % 2, :], th[:, c % 2, :], 1.0, yaf[:, c, :], ALU.add, ALU.mult
                                           ).then_inc(y2_f, 1)
                for c in (2 * t, 2 * t + 1):
                    dve.wait_ge(y2_hi_s, c + 1)
                    tt(y2_lo[:, c, :], y2f[:, c % 2, :], fv(y2_hi[:, c, :]), ALU.subtract).then_inc(y2_lo_s, 1)
            dve.wait_ge(y2_lo_s, KB)
            for h4 in (0, 4):
                for g in range(2 if h4 == 0 else 0, 4):
                    scale_gate0(h4 + g)
                for g in (h4, h4 + 2):
                    merge0(g)
                    merge0(g + 1)
                    if g == 4:
                        dve.drain().then_inc(x1_ready, 4)
                    low_merged(g)
                    low_merged(g + 1)
            s = norms["f"]
            dve.wait_ge(j2_lo, KD)
            V.memset(sqsum[:, :], 0.0).then_inc(s["sum"], 1)
            with nc.vector.Fori(0, 2) as i:
                for c in range(4):
                    dve.wait_ge(w_used, 4 * i + (T_WO + c + 1))
                    xi = xT[:, ds(4 * i + c, 1), :].rearrange("p a t -> p (a t)")
                    V.scalar_tensor_tensor(xi, bank[c][:, :], 0.5, xi, ALU.mult, ALU.add).then_inc(x1_ready, 1)
                    dve.wait_ge(x1_ready, 4 * i + (c + 5))
                    dve.wait_ge(s["hi"], 4 * i + (c + 1))
                    V.scalar_tensor_tensor(h_lo[:, ds(4 * i + c, 1), :].rearrange("p a t -> p (a t)"), xi,
                                           small[:, ds(4 * i + (C_GFFN + c), 1)],
                                           fv(h_hi[:, ds(4 * i + c, 1), :]).rearrange("p a t -> p (a t)"),
                                           ALU.mult, ALU.subtract).then_inc(s["lo"], 1)
                    dve.wait_ge(s["sq"], 4 * i + (c + 1))
                    dve.wait_ge(s["sum"], 4 * i + (c + 1))
                    tt(sqsum[:, :], sqsum[:, :], sq[:, c % 2, :], ALU.add).then_inc(s["sum"], 1)
                    dve.wait_ge(s["lo"], 4 * i + (c + 1))
            before(dve, ff_g, ff_u, ff_lo)
            dve.wait_ge(s["std"], 1)
            V.reciprocal(rstd[:, :], std[:, :]).then_inc(rstd_ready, 1)
            dve.wait_ge(rstd_ready, 2)
            with nc.vector.Fori(0, KF // 2) as i:
                for n in range(2):
                    dve.wait_ge(w_used, 4 * i + (T_FF + n + 1))
                    dve.wait_ge(ff_lo, 2 * i + 1)
                    tt(silu[:, n, :], bank[n][:, :], rstd[:, :], ALU.mult).then_inc(ff_g, 1)
                for n in range(2):
                    dve.wait_ge(w_used, 4 * i + (T_FF + n + 3))
                    tt(actf[:, n, :], bank[2 + n][:, :], rstd[:, :], ALU.mult).then_inc(ff_u, 1)
                    dve.wait_ge(ff_u, 2 * i + (n + 2))
                    dve.wait_ge(ff_silu, 2 * i + (n + 1))
                    tt(actf[:, n, :], actf[:, n, :], silu[:, n, :], ALU.mult).then_inc(ff_act, 1)
                for n in range(2):
                    dve.wait_ge(ff_hi, 2 * i + (n + 1))
                    tt(act_lo[:, ds(2 * i + n, 1), :], actf[:, n:n + 1, :], fv(act_hi[:, ds(2 * i + n, 1), :]),
                       ALU.subtract).then_inc(ff_lo, 1)
            def add_x1(h, k):
                tokens = HALVES[h]
                dve.wait_ge(dn_done, KD * h + k + 1)
                tt(xT[:, k, tokens], bank[k][:, tokens], xT[:, k, tokens], ALU.add).then_inc(x2_ready, 1)
                if k in (3, 5, 7):
                    dve.wait_ge(x2_sq, KD * h + k)
                    if k > 3:
                        dve.wait_ge(sum_dve, 3 * h + k // 2 - 1)
                    tt(osum[:, 0, tokens], osq[:, 0, tokens] if k == 3 else osum[:, 0, tokens],
                       osq[:, k - 1, tokens], ALU.add).then_inc(sum_dve, 1)

            def spread_root(h):
                dve.wait_ge(o_std, h + 1)
                c = slice(2 * h, 2 * h + 2)
                link(V.reciprocal(trstd[:, c], tstd[:, c]))
                tt(spread[:, c, :], ident.unsqueeze(1).to_broadcast([P, 2, P]),
                   trstd[:, c].unsqueeze(2).to_broadcast([P, 2, P]), ALU.mult).then_inc(diag_ready, 1)

            def scale_out(h, tiles):
                dve.wait_ge(o_wide, 2 * h + 1)
                for k in tiles:
                    V.scalar_tensor_tensor(xT[:, k, HALVES[h]], xT[:, k, HALVES[h]],
                                           small[:, C_GFIN + k:C_GFIN + k + 1], bank[WIDE_BANKS[h][0]][:, 0:HALF],
                                           ALU.mult, ALU.mult).then_inc(out_dve, 1)

            for k in range(KD):
                if k < KD - 1:
                    dve.wait_ge(dn_part, k + 1)
                else:
                    dve.wait_ge(w_used, T_DN + KF - 2)
                tt(xT[:, k, :], bank[k][:, :], xT[:, k, :], ALU.add).then_inc(part_taken, 1)
            dve.wait_ge(part_taken, KD)
            for k in range(KD):
                add_x1(0, k)
            for k in range(KD):
                if k == 4:
                    spread_root(0)
                add_x1(1, k)
            dve.wait_ge(x2_ready, 2 * KD)
            scale_out(0, OUT_DVE[:4])
            spread_root(1)
            scale_out(0, OUT_DVE[4:])
            scale_out(1, OUT_DVE)

        @block.tensor
        def _(pe):
            mm = nc.tensor.matmul

            def product(out, a, b, first, last):
                mm(out, a[0], b[0], start=first, stop=False)
                mm(out, a[0], b[1], start=False, stop=False)
                return mm(out, a[1], b[0], start=False, stop=last)

            def weight(slot, k, c0, n, width):
                lo = k * width + c0
                return w_hi[:, slot % NS, lo:lo + n], w_lo[:, slot % NS, lo:lo + n]

            def pair(hi, lo, k):
                return hi[:, k, :], lo[:, k, :]

            def column_tile(out, slot, x, kn, c0=0, width=P):
                for k in range(kn):
                    ins = product(out, weight(slot, k, c0, P, width), x(k), k == 0, k == kn - 1)
                return ins

            def tile_ready(t):
                pe.wait_ge(w_ready, t + 1)

            def h(k):
                return pair(h_hi, h_lo, k)

            def column_tile_in_halves(t, out, x):
                pe.wait_ge(w_half, t + 1 if t < NS else t - T_QK + NS + 1)
                for k in range(KD):
                    if k == KD // 2:
                        tile_ready(t)
                    ins = product(out, weight(t, k, 0, P, P), x(k), k == 0, k == KD - 1)
                return ins

            def square_sum(s, b, width, count):
                pe.wait_ge(s["sum"], count)
                mm(bank[b][:, 0:width], ones[:, :], sqsum[:, 0:width], start=True, stop=True).then_inc(s["ssq"], 1)

            def token_sum(n):
                for t in range(n):
                    ins = mm(bank[6][:, t:t + 1], sqsum[:, t * P:(t + 1) * P], ones[:, 0:1], start=True, stop=True)
                ins.then_inc(tok_ssq, 1)

            def h_when_ready(k):
                pe.wait_ge(norms["x"]["lo"], k + 1)
                return h(k)

            pe.wait_ge(consts, 1)
            for i in range(WARM_UP):
                mm(bank[7][:, 0:P], ones[:, :], ones[:, :], start=True, stop=True)
            column_tile_in_halves(T_ZA, bank[0][:, :], h_when_ready).then_inc(w_used, 1)
            column_tile_in_halves(T_ZA + 1, bank[1][:, :], h).then_inc(w_used, 1)
            square_sum(norms["x"], 7, T, KD)
            token_sum(T // P)
            for c in range(2, KB):
                tile_ready(T_ZA + c)
                column_tile(bank[c][:, :], c, h, KD).then_inc(w_used, 1)
            pe.wait_ge(norms["x"]["std"], 1)
            pe.wait_ge(tok_std, 1)
            square_sum(norms["m"], 7, M, KD)
            token_sum(M // P)
            for t in range(4):
                tile_ready(T_ZV + t)
                for c in range(4):
                    if t == 0 and c == 2:
                        pe.wait_ge(norms["m"]["std"], 1)
                        pe.wait_ge(tok_std, 2)
                    for j in range(2):
                        k = 2 * t + j
                        ins = product(bank[4 + c][:, :], [x[:, c * P:(c + 1) * P] for x in h(k)],
                                      weight(t, j, 0, WB, WB), k == 0, k == KD - 1)
                ins.then_inc(w_used, 1)
            pe.wait_ge(norms["m"]["lo"], KD)
            for c in range(KB):
                pe.wait_ge(za_taken, c + 1)
                column_tile_in_halves(T_QK + 2 * c, bank[c][:, :], h).then_inc(w_used, 1)
                pe.wait_ge(zv_taken, c + 1)
                column_tile_in_halves(T_QK + 2 * c + 1, bank[4 + c][:, 0:M], lambda k: pair(m_hi, m_lo, k)
                                      ).then_inc(w_used, 1)

            def scores(head):
                for half in range(2):
                    b = SCORE_BANK[head] + half
                    for j in range(2):
                        t0 = (2 * half + j) * P
                        ins = mm(bank[b][:, j * M:(j + 1) * M], qT[:, head, t0:t0 + P], kT[:, head, :],
                                 start=True, stop=True)
                    ins.then_inc(sc_done, 1)

            def transposes(head):
                pe.wait_ge(p_ready, 4 * head + 4)
                for half in range(2):
                    b = PT_BANK[head] + half
                    for t in range(4):
                        ins = nc.tensor.transpose(bank[b][:, t * P:(t + 1) * P],
                                                  prob[:, (4 * head + t) % 8, half * P:(half + 1) * P], ident)
                ins.then_inc(pt_done, 1)

            def values(head):
                pe.wait_ge(pt_act, head + 1)
                pe.wait_ge(pt_dve, head + 1)
                for half in range(2):
                    ins = mm(bank[4 + head % 2][:, :], vM[:, half, head * P:(head + 1) * P], pT[:, head % 2, half, :],
                             start=half == 0, stop=half == 1)
                ins.then_inc(pv_done, 1)

            def value_weights(t):
                tile = T_VU + 2 * t
                pe.wait_ge(w_half, tile - T_QK + NS + 1)
                for j in range(2):
                    if j == 1:
                        tile_ready(tile)
                    k = 2 * t + j
                    for c in range(2):
                        ins = product(bank[4 + c][:, :], [x[:, c * P:(c + 1) * P] for x in pair(m_hi, m_lo, k)],
                                      weight(0, j, 0, WB, WB), k == 0, k == KD - 1)
                ins.then_inc(w_used, 1)

            def zu(c):
                if c >= 2:
                    pe.wait_ge(zu_scaled, c - 1)
                column_tile_in_halves(T_VU + 2 * c + 1, bank[6 + c % 2][:, :], h).then_inc(w_used, 1)

            pe.wait_ge(k_taken, HEADS)
            pe.wait_ge(zq_taken, KB)
            scores(0)
            scores(1)
            value_weights(0)
            zu(0)
            value_weights(1)
            pe.wait_ge(exp_done, 8)
            transposes(0)
            scores(2)
            zu(1)
            value_weights(2)
            zu(2)
            pe.wait_ge(pt_act, 1)
            pe.wait_ge(pt_dve, 1)
            transposes(1)
            pe.wait_ge(exp_done, 12)
            scores(3)
            value_weights(3)
            zu(3)
            pe.wait_ge(v_taken, 2)
            values(0)
            pe.wait_ge(exp_done, 16)
            transposes(2)
            values(1)
            transposes(3)
            pe.wait_ge(vln_ready, 4)
            pe.wait_ge(wst_masked, 1)
            for g in range(4):
                if g < 2:
                    pe.wait_ge(zu_scaled, 3 + g)
                else:
                    pe.wait_ge(pt_act, 3)
                    pe.wait_ge(pt_dve, 3)
                for b in range(4):
                    ins = mm(bank[SGU_BANK[g]][:, b * P:(b + 1) * P], vtok[:, b, g * P:(g + 1) * P],
                             sgu[:, 3, g * P:(g + 1) * P], start=True, stop=True)
                ins.then_inc(sgu_done, 1)
            pe.wait_ge(o_lo_s, 1)
            values(2)
            pe.wait_ge(o_lo_s, 2)
            values(3)

            pe.wait_ge(sgu_taken, 4)
            pe.wait_ge(pt_act, 4)
            before(pe, y_done)
            with nc.tensor.Fori(0, ROUNDS) as m:
                def gate(j, b, free):
                    pe.wait_ge(w_ready, 6 * m + (T_J1 + j + 1))
                    pe.wait_ge(j1_g, 4 * m + free)
                    column_tile(bank[b][:, :], j, h, KD).then_inc(w_used, 1)

                def outs(j0, hi, lo, ready, free):
                    pe.wait_ge(w_ready, 6 * m + (T_J1 + j0 + 1))
                    for n in range(2):
                        pe.wait_ge(j1_merge, 4 * m + free[n])
                        pe.wait_ge(ready, HEADS)
                        ins = column_tile(bank[2 + n][:, :], j0, lambda k: pair(hi, lo, k), KB, n * P, 2 * P)
                    ins.then_inc(w_used, 1)

                gate(0, 0, 1)
                gate(1, 1, 1)
                outs(2, yb_hi, yb_lo, yb_lo_s, (1, 1))
                pe.wait_ge(bc_ready, m + 1)
                for i in range(2):
                    for q in range(ROUND):
                        nc.tensor.transpose(bank[4 + i][:, q * P:(q + 1) * P],
                                            ba[i][:, q, :, :].rearrange("p a b -> p (a b)"), ident)
                for q in range(ROUND):
                    for i in range(2):
                        ins = mm(bank[6][0:CH, q * P:(q + 1) * P], ba[i][:, q, L - 1, :],
                                 ca[i][:, q, 0:L, :].rearrange("p a b -> p (a b)"), start=i == 0, stop=i == 1)
                ins.then_inc(gt_done, 1)
                gate(3, 0, 2)
                pe.wait_ge(gt_ready, m + 1)
                pe.wait_ge(uc_ready, m + 1)
                for i in range(2):
                    for q in range(ROUND):
                        ins = mm(bank[4 + i][:, q * P:(q + 1) * P], gt[i][:, q, :], uc[:, q, :], start=True, stop=True)
                ins.then_inc(vin_done, 1)
                gate(4, 1, 3)
                outs(5, o_hiT, o_loT, o_lo_s, (2, 3))
                pe.wait_ge(st_ready, m + 1)
                pe.wait_ge(y_taken, m + 1)
                for q in range(ROUND):
                    o = bank[7][:, q * P:(q + 1) * P]
                    mm(o, toep[:, q, :], uc[:, q, :], start=True, stop=False)
                    mm(o, ca[0][:, q, 1:L + 1, :].rearrange("p a b -> p (a b)"), st[0][:, q, :], start=False, stop=False)
                    ins = mm(o, ca[1][:, q, 1:L + 1, :].rearrange("p a b -> p (a b)"), st[1][:, q, :],
                             start=False, stop=True)
                ins.then_inc(y_done, 1)
            def gate0(g):
                tile_ready(J2_TILE[g])
                if g >= 4:
                    pe.wait_ge(j2_g, g - 3)
                column_tile(bank[G_BANK[g % 4]][:, :], J2_TILE[g] % NS, h, KD).then_inc(w_used, 1)

            pe.wait_ge(j1_g, 17)
            gate0(0)
            gate0(1)
            pe.wait_ge(ya_lo_s, KB)
            pe.wait_ge(j1_merge, 17)
            for t in range(2):
                tile_ready(T_GLU + t)
                for n in range(2):
                    ins = column_tile(bank[Y_BANK[2 * t + n]][:, :], t, lambda k: pair(ya_hi, ya_lo, k), KB,
                                      n * P, 2 * P)
                ins.then_inc(w_used, 1)
            for h4 in (0, 4):
                for g in range(2 if h4 == 0 else 0, 4):
                    gate0(h4 + g)
                for q in range(2):
                    t = J2_OUT[h4 // 2 + q]
                    tile_ready(t)
                    pe.wait_ge(y2_lo_s, KB)
                    for n in range(2):
                        if h4:
                            pe.wait_ge(j2_prod, 2 * q + n + 1)
                        ins = column_tile(bank[Y_BANK[2 * q + n]][:, :], t % NS, lambda k: pair(y2_hi, y2_lo, k), KB,
                                          n * P, 2 * P)
                    ins.then_inc(w_used, 1)
            with nc.tensor.Fori(0, 2) as i:
                def merged(k):
                    pe.wait_ge(j2_lo, k + 1)
                    return pair(mg_hi, mg_lo, k)

                for c in range(4):
                    pe.wait_ge(x1_ready, 4 * i + (c + 1))
                    pe.wait_ge(w_ready, 4 * i + (T_WO + c + 1))
                    column_tile(bank[c][:, :], c, merged if c == 0 else lambda k: pair(mg_hi, mg_lo, k), KD
                                ).then_inc(w_used, 1)

            def feed(i, g, free):
                for n in range(2):
                    pe.wait_ge(free, 2 * i + 1)
                    pe.wait_ge(w_ready, 4 * i + (T_FF + 2 * g + n + 1))
                    column_tile(bank[2 * g + n][:, :], n, h, KD).then_inc(w_used, 1)

            for n in range(2):
                tile_ready(T_FF + n)
                for k in range(KD):
                    pe.wait_ge(norms["f"]["lo"], k + 1)
                    ins = product(bank[n][:, :], weight(n, k, 0, P, P), h(k), k == 0, k == KD - 1)
                ins.then_inc(w_used, 1)
            square_sum(norms["f"], 4, T, KD + 1)
            feed(0, 1, ff_u)
            with nc.tensor.Fori(1, KF // 2) as i:
                feed(i, 0, ff_g)
                feed(i, 1, ff_u)

            def down(slot, n, x, first, last):
                return product(bank[n][:, :], weight(slot, 0, n * P, P, 0), x, first, last)

            for k in range(2):
                tile_ready(T_DN + k)
                for n in (4, 5, 6, 7, 0, 1, 2, 3):
                    if k == 0 and n == 0:
                        pe.wait_ge(ff_g, KF + 1)
                        pe.wait_ge(ff_u, KF + 1)
                    pe.wait_ge(ff_lo, k + 2)
                    ins = down(k, n, pair(act_hi, act_lo, k), k == 0, False)
                ins.then_inc(w_used, 1)
            pe.wait_ge(ff_lo, KF - 1)
            with nc.tensor.Fori(1, KF // 2 - 2) as i:
                for j in range(2):
                    pe.wait_ge(w_ready, 2 * i + (T_DN + j + 1))
                    x = [a[:, ds(2 * i + j, 1), :].rearrange("p a t -> p (a t)") for a in (act_hi, act_lo)]
                    for n in range(KD):
                        ins = down(j, n, x, False, False)
                    ins.then_inc(w_used, 1)
            for k in (KF - 4, KF - 3):
                tile_ready(T_DN + k)
                for n in range(KD):
                    ins = down(k, n, pair(act_hi, act_lo, k), False, k == KF - 3)
                    if k == KF - 3 and n < KD - 1:
                        ins.then_inc(dn_part, 1)
                ins.then_inc(w_used, 1)

            def last_products(h, n):
                cols = slice(n * P, (n + 1) * P)
                weights = ((w_hi[:, 0, cols], w_lo[:, 0, cols]), (last_hi[:, cols], last_lo[:, cols]))
                for k, w in zip((KF - 2, KF - 1), weights):
                    x = act_hi[:, k, HALVES[h]], act_lo[:, k, HALVES[h]]
                    ins = product(bank[n][:, HALVES[h]], w, x, k == KF - 2, k == KF - 1)
                ins.then_inc(dn_done, 1)

            def last_sum(h):
                pe.wait_ge(sum_dve, 3 * h + 3)
                pe.wait_ge(sum_pool, 2 * h + 2)
                pe.wait_ge(x2_sq, KD * h + KD)
                sums = (osum[:, 0, HALVES[h]], osum[:, 1, HALVES[h]], osq[:, KD - 1, HALVES[h]])
                for t in range(HALF // P):
                    for i, x in enumerate(sums):
                        ins = mm(bank[0][:, t:t + 1], x[:, t * P:(t + 1) * P], ones[:, 0:1],
                                 start=i == 0, stop=i == len(sums) - 1)
                ins.then_inc(o_ssq, 1)

            def widen(h):
                pe.wait_ge(diag_ready, h + 1)
                for b in WIDE_BANKS[h]:
                    mm(bank[b][:, 0:HALF], ones[:, :], flat(spread[:, 2 * h:2 * h + 2, :]), start=True, stop=True
                       ).then_inc(o_wide, 1)

            pe.wait_ge(ff_lo, KF + 1)
            tile_ready(TILES - 1)
            for n in range(KD):
                pe.wait_ge(part_taken, n + 1)
                last_products(0, n)
            for n in range(KD):
                pe.wait_ge(x2_ready, n + 1)
                last_products(1, n)
                if n == 3:
                    pe.wait_ge(x2_ready, KD + 1)
                    last_sum(0)
                if n == 6:
                    pe.wait_ge(x2_ready, KD + 3)
                    widen(0)
            pe.wait_ge(o_std, 1)
            last_sum(1)
            pe.wait_ge(x2_ready, KD + 5)
            widen(1)


def _stream(w_in, w_kv, w_glu, w_a, w_b, w_c, w_out, w_gate, w_up, w_down):
    tiles = []

    def columns(w, c, n=1):
        part = w[:, c * P:(c + n) * P].reshape(-1, P, n * P)
        tiles.append(part.transpose(1, 0, 2).reshape(P, TILE))

    def rows(w, k, n=1):
        tiles.append(w[k * P:(k + n) * P].reshape(n, P, -1).transpose(1, 0, 2).reshape(P, TILE))

    za, zu, zv, zq, gates = np.split(w_in, [WB, 2 * WB, 3 * WB, 4 * WB], axis=1)
    for c in range(KB):
        columns(za, c)
    for k in range(0, KD, 2):
        rows(zv, k, 2)
    for c in range(KB):
        columns(zq, c)
        columns(w_kv[:, :WB], c)
    for c in range(KB):
        rows(w_kv[:, WB:], 2 * c, 2)
        columns(zu, c)
    for m in range(4):
        for g, w in ((1, w_b), (2, w_c)):
            for n in range(2):
                columns(gates, g * KD + 2 * m + n)
            columns(w, 2 * m, 2)
    for h4 in (0, 4):
        for c in range(4):
            columns(gates, h4 + c)
            if h4 == 0 and c == 1:
                columns(w_glu, 0, 2)
                columns(w_glu, 2, 2)
        for c in (0, 2):
            columns(w_a, h4 + c, 2)
    for c in range(KD):
        columns(w_out, c)
    for f in range(0, KF, 2):
        for w in (w_gate, w_up):
            for n in range(2):
                columns(w, f + n)
    for k in range(KF):
        rows(w_down, k)
    assert len(tiles) == TILES
    return np.stack(tiles)


def kernel(**inputs):
    import concourse.bacc as bacc
    from concourse.bass_utils import run_bass_kernel_spmd

    a = {k: np.asarray(v) for k, v in inputs.items()}

    def feature_major(x, n):
        return np.ascontiguousarray(x.reshape(n, KD, P).transpose(2, 1, 0))

    def states(v):
        return v.reshape(BLOCKS, P).T

    def vector(v):
        return v.reshape(-1, P).T

    def b_rows(v):
        return v.reshape(BLOCKS, P, 16).transpose(1, 0, 2).reshape(P, 256)

    def c_rows(v):
        return b_rows(v.transpose(0, 2, 1))

    def padded(v):
        return np.pad(v, ((0, 0), (0, 16 * ROUND)))

    skip = np.tile(a["d_skip"][0].reshape(BLOCKS, CH).T, (L, 1))
    small = np.concatenate([
        vector(a["g_mix"][0]), vector(a["g_mem"][0]), vector(a["g_ffn"][0]), vector(a["g_final"]),
        vector(a["b_gate"][0]), vector(a["b_glu"][0]), np.eye(P, dtype=np.float32),
        states(a["a_re"][0]), states(a["a_im"][0]), states(np.broadcast_to(a["log_dt"][0][:, None], (32, 64))),
        padded(b_rows(a["bm_re"][0])), padded(b_rows(a["bm_im"][0])), c_rows(a["cm_re"][0]), c_rows(a["cm_im"][0]),
        skip], axis=1)
    wide = [np.broadcast_to(v.reshape(1, WB), (P, WB)) for v in (a["g_sgu"][0], a["beta_sgu"][0], a["b_s"][0])]
    mix = a["w_s"][0].transpose(2, 0, 1).reshape(P, WB)
    arrays = {
        "xt_dram": feature_major(a["x"], T),
        "mem_dram": feature_major(a["mem"], M),
        "small_dram": np.ascontiguousarray(small),
        "sgu_dram": np.ascontiguousarray(np.stack([*wide, mix], axis=1)),
        "w_dram": _stream(*(a[k][0] for k in ("w_in", "w_kv", "w_glu", "w_a_out", "w_b_out", "w_c_out", "w_out",
                                              "w_gate", "w_up", "w_down"))),
    }
    nc = bacc.Bacc("TRN2", target_bir_lowering=False, num_devices=1)
    args = [nc.dram_tensor(n, x.shape, mybir.dt.from_np(x.dtype), kind="ExternalInput").ap()
            for n, x in arrays.items()]
    out = nc.dram_tensor("out_dram", (KD, P, T), mybir.dt.float32, kind="ExternalOutput").ap()
    build(nc, *args, out)
    r = run_bass_kernel_spmd(nc, [arrays], core_ids=[0])
    return r.results[0]["out_dram"].reshape(D, T).T.reshape(1, T, D)
```
